# Optimizing a Trainium2 kernel written in Bass

```python
import jax, jax.numpy as jnp
from jax import lax
import numpy as np

D_MODEL = 1024
BATCH = 1
SEQ = 256
DEPTH = 1

PLE_DIM = 256
MOBA_HEADS = 8
MOBA_HEAD_DIM = 64
MOBA_BLOCK = 256
MOBA_TOPK = 3
MOBA_Q_CHUNK = 32
ROPE_THETA = 500000.0
PARTIAL_ROT = MOBA_HEAD_DIM // 4
MOBA_W = MOBA_HEADS * MOBA_HEAD_DIM
MLA_HEADS = 8
MLA_Q_LORA = 512
MLA_KV_LORA = 256
MLA_NOPE = 64
MLA_ROPE = 32
MLA_V = 64
MLA_QK = MLA_NOPE + MLA_ROPE
MLA_ROPE_THETA = 10000.0
ATTN_Q_BLOCK = 128
PEER_HEADS = 8
PEER_N_KEYS = 128
PEER_N_EXPERTS = PEER_N_KEYS * PEER_N_KEYS
PEER_KEY_DIM = 256
PEER_TOPK = 16
PEER_TOKEN_CHUNK = 128
N_BRANCH = 2
IN_SPLITS = [MOBA_W, 2 * MOBA_W, 3 * MOBA_W, 3 * MOBA_W + MLA_Q_LORA,
             3 * MOBA_W + MLA_Q_LORA + MLA_KV_LORA,
             3 * MOBA_W + MLA_Q_LORA + MLA_KV_LORA + MLA_ROPE,
             3 * MOBA_W + MLA_Q_LORA + MLA_KV_LORA + MLA_ROPE + D_MODEL]
IN_COLS = 3 * MOBA_W + MLA_Q_LORA + MLA_KV_LORA + MLA_ROPE + N_BRANCH * D_MODEL
DEEPNORM_ALPHA = (2.0 * DEPTH) ** 0.25
DEEPNORM_BETA = (8.0 * DEPTH) ** -0.25
NEG_INF = -1e30
LN_EPS = 1e-5
RMS_EPS = 1e-6

kernel_name = "hybrid_moba_mla_peer_deepnorm_block"

def layer_norm(x, g, b):
    xf = x.astype(jnp.float32)
    mu = jnp.mean(xf, axis=-1, keepdims=True)
    var = jnp.mean(jnp.square(xf - mu), axis=-1, keepdims=True)
    y = (xf - mu) * lax.rsqrt(var + LN_EPS) * g.astype(jnp.float32) + b.astype(jnp.float32)
    return y.astype(x.dtype)

def rms_norm(x, g):
    xf = x.astype(jnp.float32)
    y = xf * lax.rsqrt(jnp.mean(xf * xf, axis=-1, keepdims=True) + RMS_EPS) * g.astype(jnp.float32)
    return y.astype(x.dtype)

def rope_tables(pos, rot_dim, theta):
    inv = jnp.power(jnp.float32(theta), -jnp.arange(0, rot_dim, 2, dtype=jnp.float32) / rot_dim)
    ang = pos.astype(jnp.float32)[:, None] * inv[None, :]
    ang = jnp.concatenate([ang, ang], axis=-1)
    return jnp.cos(ang), jnp.sin(ang)

def apply_rope(x, cos, sin):
    r = cos.shape[-1]
    xr, xp = x[..., :r], x[..., r:]
    x1, x2 = xr[..., : r // 2], xr[..., r // 2:]
    rot = jnp.concatenate([-x2, x1], axis=-1)
    c = cos[:, None, :].astype(x.dtype)
    s = sin[:, None, :].astype(x.dtype)
    return jnp.concatenate([xr * c + rot * s, xp], axis=-1)

def moba_attention(q, k, v):
    B, H, S, dh = q.shape
    nb = -(-S // MOBA_BLOCK)
    pad = nb * MOBA_BLOCK - S
    kp = jnp.pad(k, ((0, 0), (0, 0), (0, pad), (0, 0))).reshape(B, H, nb, MOBA_BLOCK, dh)
    vp = jnp.pad(v, ((0, 0), (0, 0), (0, pad), (0, 0))).reshape(B, H, nb, MOBA_BLOCK, dh)
    k_mean = jnp.mean(kp.astype(jnp.float32), axis=3)
    n_sel = min(MOBA_TOPK, nb)
    scale = dh ** -0.5
    bi = jnp.arange(B)[:, None, None, None]
    hi = jnp.arange(H)[None, :, None, None]
    blk_ids = jnp.arange(nb)

    def chunk(c):
        start = c * MOBA_Q_CHUNK
        qc = lax.dynamic_slice_in_dim(q, start, MOBA_Q_CHUNK, axis=2)
        qpos = start + jnp.arange(MOBA_Q_CHUNK)
        qblk = start // MOBA_BLOCK
        gate = jnp.einsum('bhqd,bhnd->bhqn', qc.astype(jnp.float32), k_mean)
        gate = jnp.where(blk_ids < qblk, gate, NEG_INF)
        _, sel = lax.top_k(gate, n_sel)
        sel_valid = jnp.repeat(sel < qblk, MOBA_BLOCK, axis=-1)
        k_sel = kp[bi, hi, sel].reshape(B, H, MOBA_Q_CHUNK, n_sel * MOBA_BLOCK, dh)
        v_sel = vp[bi, hi, sel].reshape(B, H, MOBA_Q_CHUNK, n_sel * MOBA_BLOCK, dh)
        s_sel = jnp.einsum('bhqd,bhqkd->bhqk', qc, k_sel).astype(jnp.float32) * scale
        s_sel = jnp.where(sel_valid, s_sel, NEG_INF)
        k_own = lax.dynamic_index_in_dim(kp, qblk, axis=2, keepdims=False)
        v_own = lax.dynamic_index_in_dim(vp, qblk, axis=2, keepdims=False)
        kpos = qblk * MOBA_BLOCK + jnp.arange(MOBA_BLOCK)
        s_own = jnp.einsum('bhqd,bhkd->bhqk', qc, k_own).astype(jnp.float32) * scale
        s_own = jnp.where(kpos[None, :] <= qpos[:, None], s_own, NEG_INF)
        probs = jax.nn.softmax(jnp.concatenate([s_sel, s_own], axis=-1), axis=-1).astype(v.dtype)
        p_sel = probs[..., : n_sel * MOBA_BLOCK]
        p_own = probs[..., n_sel * MOBA_BLOCK:]
        return (jnp.einsum('bhqk,bhqkd->bhqd', p_sel, v_sel)
                + jnp.einsum('bhqk,bhkd->bhqd', p_own, v_own))

    out = lax.map(chunk, jnp.arange(S // MOBA_Q_CHUNK))
    return out.transpose(1, 0, 3, 2, 4).reshape(B, S, H * dh)

def causal_attention(q, k, v):
    B, H, S, dk = q.shape
    dv = v.shape[-1]
    nq = S // ATTN_Q_BLOCK
    qb = q.reshape(B, H, nq, ATTN_Q_BLOCK, dk).transpose(2, 0, 1, 3, 4)
    kpos = jnp.arange(S)
    scale = dk ** -0.5

    def block(args):
        qi, i = args
        qpos = i * ATTN_Q_BLOCK + jnp.arange(ATTN_Q_BLOCK)
        s = jnp.einsum('bhqd,bhkd->bhqk', qi, k).astype(jnp.float32) * scale
        s = jnp.where(kpos[None, :] <= qpos[:, None], s, NEG_INF)
        pr = jax.nn.softmax(s, axis=-1).astype(v.dtype)
        return jnp.einsum('bhqk,bhkd->bhqd', pr, v)

    out = lax.map(block, (qb, jnp.arange(nq)))
    return out.transpose(1, 0, 3, 2, 4).reshape(B, S, H * dv)

def peer_ffn(h, w_q, sub_keys, u_tab, v_tab):
    B, S, D = h.shape
    T = B * S
    ht = h.reshape(T, D)
    q = (ht @ w_q).reshape(T, PEER_HEADS, 2, PEER_KEY_DIM // 2)
    s_half = jnp.einsum('thpd,hpnd->thpn', q, sub_keys).astype(jnp.float32)
    top_s, top_i = lax.top_k(s_half, PEER_TOPK)
    cand_s = (top_s[:, :, 0, :, None] + top_s[:, :, 1, None, :]).reshape(T, PEER_HEADS, PEER_TOPK * PEER_TOPK)
    cand_i = (top_i[:, :, 0, :, None] * PEER_N_KEYS + top_i[:, :, 1, None, :]).reshape(T, PEER_HEADS, PEER_TOPK * PEER_TOPK)
    best_s, best_pos = lax.top_k(cand_s, PEER_TOPK)
    experts = jnp.take_along_axis(cand_i, best_pos, axis=-1)
    gates = jax.nn.softmax(best_s, axis=-1).astype(h.dtype)
    nc = T // PEER_TOKEN_CHUNK
    xs = (ht.reshape(nc, PEER_TOKEN_CHUNK, D),
          experts.reshape(nc, PEER_TOKEN_CHUNK, PEER_HEADS * PEER_TOPK),
          gates.reshape(nc, PEER_TOKEN_CHUNK, PEER_HEADS * PEER_TOPK))

    def chunk(args):
        xc, ec, gc = args
        a = jnp.einsum('td,ted->te', xc, u_tab[ec])
        w = gc * jax.nn.gelu(a, approximate=False)
        return jnp.einsum('te,ted->td', w, v_tab[ec])

    out = lax.map(chunk, xs)
    return out.reshape(B, S, D)

def setup_inputs(seed: int = 0) -> dict:
    key = jax.random.key(seed)
    ks = jax.random.split(key, 24)
    f32 = jnp.float32
    L, D = DEPTH, D_MODEL

    def nrm(k, shape, scale):
        return jax.random.normal(k, shape, f32) * scale

    return {
        "x": nrm(ks[0], (BATCH, SEQ, D), 1.0),
        "p": nrm(ks[1], (DEPTH, BATCH, SEQ, PLE_DIM), 1.0),
        "w_in": nrm(ks[2], (L, D, IN_COLS), D ** -0.5),
        "b_gates": nrm(ks[3], (L, N_BRANCH, D), 0.02),
        "mla_q_norm": 1.0 + nrm(ks[4], (L, MLA_Q_LORA), 0.02),
        "w_q_up": nrm(ks[5], (L, MLA_Q_LORA, MLA_HEADS * MLA_QK), MLA_Q_LORA ** -0.5),
        "mla_kv_norm": 1.0 + nrm(ks[6], (L, MLA_KV_LORA), 0.02),
        "w_kv_up": nrm(ks[7], (L, MLA_KV_LORA, MLA_HEADS * (MLA_NOPE + MLA_V)), MLA_KV_LORA ** -0.5),
        "w_branch_moba": nrm(ks[8], (L, MOBA_W, D), MOBA_W ** -0.5),
        "w_branch_mla": nrm(ks[9], (L, MLA_HEADS * MLA_V, D), (MLA_HEADS * MLA_V) ** -0.5),
        "w_out": nrm(ks[10], (L, D, D), D ** -0.5 * DEEPNORM_BETA),
        "ln1_g": 1.0 + nrm(ks[11], (L, D), 0.02),
        "ln1_b": nrm(ks[12], (L, D), 0.02),
        "peer_w_q": nrm(ks[13], (L, D, PEER_HEADS * PEER_KEY_DIM), D ** -0.5),
        "peer_sub_keys": nrm(ks[14], (L, PEER_HEADS, 2, PEER_N_KEYS, PEER_KEY_DIM // 2), (PEER_KEY_DIM // 2) ** -0.5),
        "peer_u": nrm(ks[15], (L, PEER_N_EXPERTS, D), D ** -0.5),
        "peer_v": nrm(ks[16], (L, PEER_N_EXPERTS, D), DEEPNORM_BETA),
        "w_ple_proj": nrm(ks[17], (L, PLE_DIM, D), PLE_DIM ** -0.5 * DEEPNORM_BETA),
        "w_ple_gate": nrm(ks[18], (L, D, D), D ** -0.5),
        "b_ple_gate": nrm(ks[19], (L, D), 0.02),
        "ln2_g": 1.0 + nrm(ks[20], (L, D), 0.02),
        "ln2_b": nrm(ks[21], (L, D), 0.02),
    }

def reference(x, p, w_in, b_gates, mla_q_norm, w_q_up, mla_kv_norm, w_kv_up, w_branch_moba,
              w_branch_mla, w_out, ln1_g, ln1_b, peer_w_q, peer_sub_keys, peer_u, peer_v,
              w_ple_proj, w_ple_gate, b_ple_gate, ln2_g, ln2_b):
    B, S, _ = x.shape
    pos = jnp.arange(S)
    cos_p, sin_p = rope_tables(pos, PARTIAL_ROT, ROPE_THETA)
    cos_m, sin_m = rope_tables(pos, MLA_ROPE, MLA_ROPE_THETA)
    for i in range(DEPTH):
        proj = x @ w_in[i]
        q_a, k_a, v_a, c_q, c_kv, k_r, g_a, g_b = jnp.split(proj, IN_SPLITS, axis=-1)

        q_a = apply_rope(q_a.reshape(B, S, MOBA_HEADS, MOBA_HEAD_DIM), cos_p, sin_p)
        k_a = apply_rope(k_a.reshape(B, S, MOBA_HEADS, MOBA_HEAD_DIM), cos_p, sin_p)
        v_a = v_a.reshape(B, S, MOBA_HEADS, MOBA_HEAD_DIM)
        y_a = moba_attention(q_a.transpose(0, 2, 1, 3), k_a.transpose(0, 2, 1, 3), v_a.transpose(0, 2, 1, 3))

        c_q = rms_norm(c_q, mla_q_norm[i])
        q_m = (c_q @ w_q_up[i]).reshape(B, S, MLA_HEADS, MLA_QK)
        q_m = jnp.concatenate([q_m[..., :MLA_NOPE], apply_rope(q_m[..., MLA_NOPE:], cos_m, sin_m)], axis=-1)
        c_kv = rms_norm(c_kv, mla_kv_norm[i])
        kv = (c_kv @ w_kv_up[i]).reshape(B, S, MLA_HEADS, MLA_NOPE + MLA_V)
        k_nope, v_m = kv[..., :MLA_NOPE], kv[..., MLA_NOPE:]
        k_rope = apply_rope(k_r.reshape(B, S, 1, MLA_ROPE), cos_m, sin_m)
        k_m = jnp.concatenate([k_nope, jnp.broadcast_to(k_rope, (B, S, MLA_HEADS, MLA_ROPE))], axis=-1)
        y_b = causal_attention(q_m.transpose(0, 2, 1, 3), k_m.transpose(0, 2, 1, 3), v_m.transpose(0, 2, 1, 3))

        merged = (jax.nn.sigmoid(g_a + b_gates[i, 0]) * (y_a @ w_branch_moba[i])
                  + jax.nn.sigmoid(g_b + b_gates[i, 1]) * (y_b @ w_branch_mla[i]))
        mix = merged @ w_out[i]
        h = layer_norm(DEEPNORM_ALPHA * x + mix, ln1_g[i], ln1_b[i])

        r = DEEPNORM_ALPHA * h + peer_ffn(h, peer_w_q[i], peer_sub_keys[i], peer_u[i], peer_v[i])
        ple = jax.nn.sigmoid(r @ w_ple_gate[i] + b_ple_gate[i]) * (p[i] @ w_ple_proj[i])
        x = layer_norm(r + ple, ln2_g[i], ln2_b[i])
    return x


_drawn_inputs = setup_inputs


def setup_inputs(seed=0):
    import zlib

    import numpy as np

    out = dict(_drawn_inputs(seed))
    spreads = {}
    factors = {'b_gates': 8.0,
     'mla_q_norm': 7.383,
     'mla_kv_norm': 5.68,
     'b_ple_gate': 30.446,
     'ln2_g': 8.792,
     'ln2_b': 8.126}
    for name, (base, spread) in spreads.items():
        noise = np.random.default_rng([zlib.crc32(name.encode()), seed]).standard_normal(out[name].shape)
        drawn = base * np.exp(spread * noise) if base else spread * noise
        out[name] = __import__('jax').numpy.asarray(drawn.astype(out[name].dtype))
    for name, factor in factors.items():
        out[name] = (out[name] * factor).astype(out[name].dtype)
    return out
```

```python
from contextlib import ExitStack

import numpy as np

import concourse.bass as bass
from concourse import mybir

P = 128
D = 1024
T = 256
NT = T // P
KD = D // P
H = 8
DH = 64
ROT = DH // 4
QLORA, KVLORA, ROPE = 512, 256, 32
DQK = DH + ROPE
W = H * DH
Q0, K0, V0, CQ0, CKV0, KR0 = 0, W, 2 * W, 3 * W, 3 * W + QLORA, 3 * W + QLORA + KVLORA
TOK = KR0 + ROPE
IN_COLS = TOK + 2 * D
CHUNK = 512
PH = 8
NK = 128
DKH = 128
HP = 2 * PH
TK = 16
SLOTS = PH * TK
PLE = 256
ALPHA = 2.0 ** 0.25
LN_EPS, RMS_EPS = 1e-5, 1e-6
NEG = -1e30
LOWEST = -3.0e38

F32 = mybir.dt.float32
F32R = mybir.dt.float32r
U32 = mybir.dt.uint32
ALU = mybir.AluOpType
ACT = mybir.ActivationFunctionType
AX_X = mybir.AxisListType.X

C_ID, C_MASK, C_IOTA, C_ROPE = 0, P, P + T, 2 * P + T
ROPE_W = 2 * ROT + 2 * ROPE
C_COLS = C_ROPE + NT * ROPE_W
B_GATE, B_QN, B_KVN = 0, 2 * KD, 2 * KD + QLORA // P
B_COLS = B_KVN + KVLORA // P

KB = 1024


class Banks:

    def __init__(self, ctx, nc, psum, order):
        self.psum = psum
        self.full = [ctx.enter_context(nc.semaphore(f"bank_full{b}")) for b in range(8)]
        self.drained = [ctx.enter_context(nc.semaphore(f"bank_drained{b}")) for b in range(8)]
        self.at = {name: g for g, name in enumerate(order)}

    def fill(self, pe, name):
        g = self.at[name]
        if g >= 8:
            pe.wait_ge(self.drained[g % 8], g // 8)
        return self.psum[g % 8]

    def filled(self, name, last):
        last.then_inc(self.full[self.at[name] % 8], 1)

    def read(self, eng, name):
        g = self.at[name]
        eng.wait_ge(self.full[g % 8], g // 8 + 1)
        return self.psum[g % 8]

    def drain(self, name, last):
        last.then_inc(self.drained[self.at[name] % 8], 1)

    def await_drained(self, eng, name):
        g = self.at[name]
        eng.wait_ge(self.drained[g % 8], g // 8 + 1)


class Steps:

    def __init__(self, ctx, nc, name):
        self.sem = ctx.enter_context(nc.semaphore(name))
        self.n = 0

    def done(self, ins):
        ins.then_inc(self.sem, 1)
        self.n += 1

    def wait(self, eng):
        eng.wait_ge(self.sem, self.n)


def group_order():
    o = [("tok", c, n) for c in range(5) for n in range(NT)]
    o += [("qT", n) for n in range(NT)] + [("kT", n) for n in range(NT)]
    o += [("gate", j) for j in range(0, 8)]
    o += [("cqT", n) for n in range(NT)] + [("ckvT", n) for n in range(NT)] + [("krT",)]
    o += [("gate", j) for j in range(8, 12)]
    o += [("qup", n, c) for n in range(NT) for c in range(2)]
    o += [("knT", g) for g in range(H // 2)]
    o += [("vm", n) for n in range(NT)]
    o += [("gate", j) for j in range(12, 16)]
    o += [("qmT", n, c) for n in range(NT) for c in range(2)]
    o += [("S", 0), ("S", 1)]
    for h in range(2 * H):
        o += [("PT", h)]
        if h + 2 < 2 * H:
            o += [("S", h + 2)]
        o += [("Y", h)]
    o += [("br", c) for c in range(KD)]
    o += [("mix", n, c) for n in range(NT) for c in range(2)]
    o += [("hT", n, c) for n in range(NT) for c in range(2)]
    for c in range(4):
        o += [("pq", 2 * c), ("pq", 2 * c + 1)] + [("sim", n, c) for n in range(NT)]
    o += [("slotT", w) for w in range(3)]
    return o


def memory(nc):
    m = {}
    base = -(-nc.sbuf_base // 32) * 32

    def put(name, shape, off, dt=F32):
        size = int(np.prod(shape[1:])) * 4
        m[name] = nc.alloc_sbuf_tensor_at(name, shape, dt, offset=base + off)
        return off + -(-size // 32) * 32

    o = put("xT", [P, KD, T], 0)
    o = put("ring", [P, 3, KD, CHUNK], o)
    o = put("tok", [P, NT, TOK], o)
    o = put("sigT", [P, 2, KD, T], o)
    o = put("qT", [P, W // P, T], o)
    o = put("kT", [P, W // P, T], o)
    o = put("cqT", [P, QLORA // P, T], o)
    o = put("ckvT", [P, KVLORA // P, T], o)
    o = put("qm", [P, NT, H * DQK], o)
    o = put("qmT", [P, H, T], o)
    o = put("kmT", [P, H, T], o)
    o = put("vm", [P, NT, W], o)
    o = put("w_q_up", [P, QLORA // P, H * DQK], o)
    o = put("w_kv_up", [P, KVLORA // P, H * 2 * DH], o)
    o = put("w_br", [P, 2, W // P, D], o)
    o = put("probs", [P, 2, NT, T], o)
    o = put("probsT", [P, 2, 3, P], o)
    assert o <= 196 * KB, o
    put("yT", [P, 2, W // P, T], 0)
    put("mergedT", [P, KD, T], (8 + 48) * KB + 2 * TOK * 4 + 16 * KB)
    put("w_out", [P, KD, D], 8 * KB)
    put("x_tok", [P, NT, D], 40 * KB)
    put("ln1", [P, 2, D], 48 * KB)
    put("h", [P, NT, D], 196 * KB)
    o = put("consts", [P, C_COLS], 204 * KB)
    o = put("cols", [P, B_COLS], o)
    o = put("small", [P, 160], o)
    assert base + o <= nc.sbuf_usable_end, o

    put("G", [P, NK, T], 0)
    o = put("hT", [P, KD, T], 0)
    o = put("ring2", [P, 3, KD, CHUNK], o)
    o = put("subk", [P, HP, NK], o)
    o = put("pqT", [P, HP, T], o)
    o = put("sims", [P, NT, HP, NK], o)
    o = put("sims2", [P, 4, NK], o)
    assert o <= 128 * KB, o
    o = put("cand", [P, PH, TK * TK], 128 * KB)
    o = put("cand2", [P, 2, TK * TK], o)
    o = put("eq", [P, SLOTS, TK], o)
    o = put("topv", [P, HP, TK], o)
    o = put("topi", [P, HP, TK], o, U32)
    o = put("topf", [P, HP, TK], o)
    o = put("best", [P, PH, TK], o)
    o = put("bpos", [P, PH, TK], o, U32)
    o = put("bab", [P, 2, SLOTS], o, U32)
    o = put("babf", [P, 2, SLOTS], o)
    o = put("slot", [P, 3, NT, SLOTS], o)
    o = put("ex", [P, PH, TK], o)
    o = put("pstat", [P, 4, PH], o)
    assert o <= 160 * KB, o
    o = put("slotT", [P, 3, T], 160 * KB)
    o = put("oh1", [P, 8, NK], o)
    o = put("oh2", [P, 8, NK], o)
    assert o <= 176 * KB, o
    o = put("u_raw", [P, 2, KD, P], 128 * KB)
    o = put("v_raw", [P, 2, D], o)
    o = put("u_hi", [P, 2, KD, P], o, F32R)
    o = put("u_lo", [P, 2, KD, P], o, F32R)
    o = put("v_hi", [P, 2, D], o, F32R)
    o = put("v_lo", [P, 2, D], o, F32R)
    o = put("h_hi", [P, KD, T], o, F32R)
    o = put("h_lo", [P, KD, T], o, F32R)
    o = put("w_hi", [P, 2, T], o, F32R)
    o = put("w_lo", [P, 2, T], o, F32R)
    assert o <= 196 * KB, o
    o = put("w_ple_gate", [P, KD, D], 0)
    o = put("w_ple_proj", [P, PLE // P, D], o)
    o = put("pT", [P, PLE // P, T], o)
    o = put("rows", [P, 3, D], o)
    o = put("r", [P, NT, D], o)
    o = put("rT", [P, KD, T], o)
    o = put("ple", [P, NT, D], o)
    o = put("ple2", [P, NT, D], o)
    o = put("y_out", [P, NT, D], o)
    assert o <= 120 * KB, o
    return m


def rope(nc, dve, steps, src, dst, tmp, table, heads, rot, last):
    half = rot // 2
    cos = table[:, 0:rot].unsqueeze(1).to_broadcast([P, heads, rot])
    sin = table[:, rot:2 * rot].unsqueeze(1).to_broadcast([P, heads, rot])
    a, b = tmp
    steps.done(nc.vector.tensor_tensor(a, src, cos, ALU.mult))
    steps.done(nc.vector.tensor_tensor(b[:, :, 0:half], src[:, :, half:rot], sin[:, :, 0:half], ALU.mult))
    steps.done(nc.vector.tensor_tensor(b[:, :, half:rot], src[:, :, 0:half], sin[:, :, half:rot], ALU.mult))
    steps.wait(dve)
    last.done(nc.vector.tensor_tensor(dst, a, b, ALU.add))
    last.wait(dve)


def layer_norm(nc, dve, steps, st, z, out, gain, shift, var_ok, std_ok, n, last):
    zz = z.rearrange("p (c f) -> p c f", f=512)
    for c in range(D // 512):
        steps.done(nc.vector.bn_stats(st[:, 6 * c:6 * c + 6], zz[:, c, :]))
    steps.wait(dve)
    steps.done(nc.vector.bn_aggr(st[:, 12:14], st[:, 0:12]))
    steps.wait(dve)
    nc.vector.tensor_scalar(st[:, 14:15], st[:, 13:14], LN_EPS, None, ALU.add).then_inc(var_ok, 1)
    dve.wait_ge(std_ok, n + 1)
    steps.done(nc.vector.reciprocal(st[:, 16:17], st[:, 15:16]))
    steps.wait(dve)
    steps.done(nc.vector.tensor_scalar(out, z, st[:, 12:13], st[:, 16:17], ALU.subtract, ALU.mult))
    steps.wait(dve)
    steps.done(nc.vector.tensor_tensor(out, out, gain, ALU.mult))
    steps.wait(dve)
    last.done(nc.vector.tensor_tensor(out, out, shift, ALU.add))
    last.wait(dve)


QUP = ((0, 5 * DQK), (5 * DQK, H * DQK))
W_STARTS = [Q0, K0, V0, CQ0, CKV0] + [TOK + CHUNK * j for j in range(2 * D // CHUNK)]
W_WIDTHS = [CHUNK] * 4 + [TOK - CKV0] + [CHUNK] * (2 * D // CHUNK)
TOK_CHUNKS = 5


def front(nc, io, m, bank):
    ident = m["consts"][:, C_ID:C_ID + P]
    tok, ring, small = m["tok"], m["ring"], m["small"]
    n_chunks = len(W_STARTS)
    scales = [DH ** -0.5] * H + [DQK ** -0.5] * H
    ss, rs = small[:, 0:4], small[:, 4:8]
    mx, nmx = small[:, 8:40], small[:, 40:72]
    den, rden = small[:, 72:104], small[:, 104:136]
    st = small[:, 136:160]

    with ExitStack() as ctx:
        def sem(name):
            return ctx.enter_context(nc.semaphore(name))

        x_in, c_in, b_in = sem("x_in"), sem("consts_in"), sem("cols_in")
        w_in_sem = [sem(f"w_in_slot{k}") for k in range(3)]
        wq_in, wkv_in, wb_in = sem("w_q_up_in"), sem("w_kv_up_in"), sem("w_branch_in")
        wo_in, xt_in, ln_in = sem("w_out_in"), sem("x_rows_in"), sem("ln1_in")
        ss_ready, root_ready, ms_ready = sem("squares_summed"), sem("root_ready"), sem("mean_square_ready")
        exped = sem("exp_done")
        var_ok, std_ok = sem("var_ready"), sem("std_ready")
        dv = Steps(ctx, nc, "front_dve")
        qk_roped = Steps(ctx, nc, "qk_roped")
        lora_ready = Steps(ctx, nc, "lora_ready")
        qm_roped = Steps(ctx, nc, "qm_roped")
        nmax = Steps(ctx, nc, "neg_max_ready")
        probs_ok = Steps(ctx, nc, "probs_ready")
        merged_ok = Steps(ctx, nc, "merged_ready")
        h_ok = Steps(ctx, nc, "h_ready")
        block = ctx.enter_context(nc.Block())

        @block.sync
        def _(sp):
            sp.dma_start(m["xT"][:], io["xT"].rearrange("(k p) t -> p k t", p=P)).then_inc(x_in, 16)
            w_in = io["w_in"].rearrange("(k p) c -> p k c", p=P)
            for c in range(n_chunks):
                if c >= 3:
                    used = c - 3
                    bank.read(sp, ("tok", used, NT - 1) if used < TOK_CHUNKS else ("gate", 4 * (used - TOK_CHUNKS) + 3))
                a, w = W_STARTS[c], W_WIDTHS[c]
                sp.dma_start(ring[:, c % 3, :, 0:w], w_in[:, :, a:a + w]).then_inc(w_in_sem[c % 3], 16)
                if c == 0:
                    sp.dma_start(m["consts"][:], io["consts"]).then_inc(c_in, 16)
                    sp.dma_start(m["cols"][:], io["cols"]).then_inc(b_in, 16)
                if c == 5:
                    sp.dma_start(m["w_q_up"][:], io["w_q_up"].rearrange("(k p) c -> p k c", p=P)).then_inc(wq_in, 16)
                    sp.dma_start(m["w_kv_up"][:], io["w_kv_up"].rearrange("(k p) c -> p k c", p=P)).then_inc(wkv_in, 16)
            for b, w in enumerate(("w_branch_moba", "w_branch_mla")):
                sp.dma_start(m["w_br"][:, b], io[w].rearrange("(k p) c -> p k c", p=P)).then_inc(wb_in, 16)
            for j in (7, 11, 15):
                bank.read(sp, ("gate", j))
            sp.dma_start(m["w_out"][:], io["w_out"].rearrange("(k p) c -> p k c", p=P)).then_inc(wo_in, 16)
            sp.dma_start(m["x_tok"][:], io["x"].rearrange("(n p) d -> p n d", p=P)).then_inc(xt_in, 16)
            sp.dma_start(m["ln1"][:, 0, :], io["ln1_g"].partition_broadcast(P)).then_inc(ln_in, 16)
            sp.dma_start(m["ln1"][:, 1, :], io["ln1_b"].partition_broadcast(P)).then_inc(ln_in, 16)

        @block.tensor
        def _(pe):
            def gate(j):
                c = TOK_CHUNKS + j // 4
                if j % 4 == 0:
                    pe.wait_ge(w_in_sem[c % 3], 16 * (c // 3 + 1))
                ps = bank.fill(pe, ("gate", j))
                for k in range(KD):
                    last = nc.tensor.matmul(ps[:, 0:T], ring[:, c % 3, k, (j % 4) * P:(j % 4 + 1) * P],
                                            m["xT"][:, k, :], start=(k == 0), stop=(k == KD - 1))
                bank.filled(("gate", j), last)

            def turn(name, blocks, width=P):
                ps = bank.fill(pe, name)
                for i, b in enumerate(blocks):
                    last = nc.tensor.transpose(ps[0:width, i * P:(i + 1) * P], b, ident)
                bank.filled(name, last)

            pe.wait_ge(x_in, 16)
            for c in range(TOK_CHUNKS):
                pe.wait_ge(w_in_sem[c % 3], 16 * (c // 3 + 1))
                for n in range(NT):
                    ps = bank.fill(pe, ("tok", c, n))
                    for k in range(KD):
                        last = nc.tensor.matmul(ps[:, 0:W_WIDTHS[c]], m["xT"][:, k, n * P:(n + 1) * P],
                                                ring[:, c % 3, k, 0:W_WIDTHS[c]], start=(k == 0), stop=(k == KD - 1))
                    bank.filled(("tok", c, n), last)
            pe.wait_ge(c_in, 16)
            for j in range(4):
                gate(j)
            for which, base in (("qT", Q0), ("kT", K0)):
                for n in range(NT):
                    pe.wait_ge(qk_roped.sem, n + 1)
                    turn((which, n), [tok[:, n, base + i * P:base + (i + 1) * P] for i in range(W // P)])
            for j in range(4, 8):
                gate(j)
            for n in range(NT):
                pe.wait_ge(lora_ready.sem, n + 1)
                turn(("cqT", n), [tok[:, n, CQ0 + i * P:CQ0 + (i + 1) * P] for i in range(QLORA // P)])
            for n in range(NT):
                turn(("ckvT", n), [tok[:, n, CKV0 + i * P:CKV0 + (i + 1) * P] for i in range(KVLORA // P)])
            turn(("krT",), [tok[:, n, KR0:KR0 + ROPE] for n in range(NT)], ROPE)
            for j in range(8, 12):
                gate(j)
            pe.wait_ge(wq_in, 16)
            for n in range(NT):
                bank.await_drained(pe, ("cqT", n))
                for c, (a, b) in enumerate(QUP):
                    ps = bank.fill(pe, ("qup", n, c))
                    for k in range(QLORA // P):
                        last = nc.tensor.matmul(ps[:, 0:b - a], m["cqT"][:, k, n * P:(n + 1) * P],
                                                m["w_q_up"][:, k, a:b], start=(k == 0), stop=(k == QLORA // P - 1))
                    bank.filled(("qup", n, c), last)
            pe.wait_ge(wkv_in, 16)
            for n in range(NT):
                bank.await_drained(pe, ("ckvT", n))
            KK = KVLORA // P
            for g in range(H // 2):
                ps = bank.fill(pe, ("knT", g))
                for e in range(2):
                    col = (2 * g + e) * 2 * DH
                    for k in range(KK):
                        last = nc.tensor.matmul(ps[0:DH, e * T:(e + 1) * T], m["w_kv_up"][:, k, col:col + DH],
                                                m["ckvT"][:, k, :], start=(k == 0), stop=(k == KK - 1))
                bank.filled(("knT", g), last)
            v_cols = m["w_kv_up"][:].rearrange("p k (h e d) -> p k h e d", h=H, e=2)
            for n in range(NT):
                ps = bank.fill(pe, ("vm", n))
                for k in range(KK):
                    last = nc.tensor.matmul(ps[:, 0:W].rearrange("p (h d) -> p h d", h=H),
                                            m["ckvT"][:, k, n * P:(n + 1) * P], v_cols[:, k, :, 1, :],
                                            start=(k == 0), stop=(k == KK - 1))
                bank.filled(("vm", n), last)
            for j in range(12, 16):
                gate(j)
            for n in range(NT):
                pe.wait_ge(qm_roped.sem, n + 1)
                for c in range(2):
                    turn(("qmT", n, c), [m["qm"][:, n, (4 * c + i) * DQK:(4 * c + i + 1) * DQK] for i in range(4)], DQK)

            def operands(h):
                if h < H:
                    r = slice(DH * (h % 2), DH * (h % 2) + DH)
                    return m["qT"][r, h // 2, :], m["kT"][r, h // 2, :]
                return m["qmT"][0:DQK, h - H, :], m["kmT"][0:DQK, h - H, :]

            def scores(h):
                if h == 0:
                    for n in range(NT):
                        bank.await_drained(pe, ("qT", n))
                        bank.await_drained(pe, ("kT", n))
                if h == H:
                    bank.await_drained(pe, ("krT",))
                    for g in range(H // 2):
                        bank.await_drained(pe, ("knT", g))
                    for n in range(NT):
                        bank.await_drained(pe, ("vm", n))
                        for c in range(2):
                            bank.await_drained(pe, ("qmT", n, c))
                q, k = operands(h)
                ps = bank.fill(pe, ("S", h))
                nc.tensor.matmul(ps[:, 0:P], q[:, 0:P], k[:, 0:P], start=True, stop=True)
                bank.filled(("S", h), nc.tensor.matmul(ps[:, P:P + T], q[:, P:T], k[:, :], start=True, stop=True))

            def values(h):
                bank.await_drained(pe, ("PT", h))
                v = (lambda n: tok[:, n, V0 + h * DH:V0 + (h + 1) * DH]) if h < H else \
                    (lambda n: m["vm"][:, n, (h - H) * DH:(h - H + 1) * DH])
                pT = m["probsT"][:, h % 2]
                ps = bank.fill(pe, ("Y", h))
                nc.tensor.matmul(ps[0:DH, 0:P], v(0), pT[:, 0, :], start=True, stop=True)
                nc.tensor.matmul(ps[0:DH, P:T], v(0), pT[:, 1, :], start=True, stop=False)
                last = nc.tensor.matmul(ps[0:DH, P:T], v(1), pT[:, 2, :], start=False, stop=True)
                bank.filled(("Y", h), last)

            scores(0)
            scores(1)
            for h in range(2 * H):
                pe.wait_ge(probs_ok.sem, h + 1)
                pr = m["probs"][:, h % 2]
                turn(("PT", h), [pr[:, 0, 0:P], pr[:, 1, 0:P], pr[:, 1, P:T]])
                if h + 2 < 2 * H:
                    scores(h + 2)
                values(h)
            pe.wait_ge(wb_in, 32)
            for h in range(2 * H):
                bank.await_drained(pe, ("Y", h))
            for c in range(KD):
                ps = bank.fill(pe, ("br", c))
                for b in range(2):
                    for k in range(W // P):
                        last = nc.tensor.matmul(ps[:, b * T:(b + 1) * T], m["w_br"][:, b, k, c * P:(c + 1) * P],
                                                m["yT"][:, b, k, :], start=(k == 0), stop=(k == W // P - 1))
                bank.filled(("br", c), last)
            pe.wait_ge(merged_ok.sem, KD)
            pe.wait_ge(wo_in, 16)
            for n in range(NT):
                for c in range(2):
                    ps = bank.fill(pe, ("mix", n, c))
                    for k in range(KD):
                        last = nc.tensor.matmul(ps[:, :], m["mergedT"][:, k, n * P:(n + 1) * P],
                                                m["w_out"][:, k, c * 512:(c + 1) * 512],
                                                start=(k == 0), stop=(k == KD - 1))
                    bank.filled(("mix", n, c), last)

        @block.scalar
        def _(act):
            def copy_out(name, dst, src):
                bank.drain(name, nc.scalar.activation(dst, src(bank.read(act, name)), ACT.Copy))

            for c in range(TOK_CHUNKS):
                a, w = W_STARTS[c], W_WIDTHS[c]
                for n in range(NT):
                    copy_out(("tok", c, n), tok[:, n, a:a + w], lambda ps: ps[:, 0:w])
            squares = [m["probs"][:, 0].rearrange("p a b -> p (a b)"), m["probs"][:, 1].rearrange("p a b -> p (a b)")]
            for n in range(NT):
                bank.await_drained(act, ("tok", 3, n))
                bank.await_drained(act, ("tok", 4, n))
                if n:
                    act.wait_ge(ss_ready, 2 * n)
                nc.scalar.activation(squares[0][:, 0:QLORA], tok[:, n, CQ0:CQ0 + QLORA],
                                     ACT.Square, accum_out=ss[:, n:n + 1]).then_inc(ss_ready, 1)
                nc.scalar.activation(squares[1][:, 0:KVLORA], tok[:, n, CKV0:CKV0 + KVLORA],
                                     ACT.Square, accum_out=ss[:, NT + n:NT + n + 1]).then_inc(ss_ready, 1)
            act.wait_ge(ms_ready, 1)
            nc.scalar.activation(rs, ss, ACT.Sqrt).then_inc(root_ready, 1)
            act.wait_ge(b_in, 16)

            def gate(j):
                ps = bank.read(act, ("gate", j))
                bank.drain(("gate", j), nc.scalar.activation(m["sigT"][:, j // KD, j % KD, :], ps[:, 0:T], ACT.Sigmoid,
                                                             bias=m["cols"][:, B_GATE + j:B_GATE + j + 1]))

            for j in range(8):
                gate(j)
            copy_out(("krT",), m["kmT"][DH:DQK, :, :], lambda ps: ps[0:ROPE, 0:T].unsqueeze(1).to_broadcast([ROPE, H, T]))
            for j in range(8, 12):
                gate(j)
            for n in range(NT):
                for c, (a, b) in enumerate(QUP):
                    copy_out(("qup", n, c), m["qm"][:, n, a:b], lambda ps: ps[:, 0:b - a])
            for g in range(H // 2):
                copy_out(("knT", g), m["kmT"][0:DH, 2 * g:2 * g + 2, :],
                         lambda ps: ps[0:DH, :].rearrange("p (e t) -> p e t", e=2))
            for n in range(NT):
                copy_out(("vm", n), m["vm"][:, n, :], lambda ps: ps[:, 0:W])
            for j in range(12, 16):
                gate(j)
            for n in range(NT):
                for c in range(2):
                    copy_out(("qmT", n, c), m["qmT"][0:DQK, 4 * c:4 * c + 4, n * P:(n + 1) * P],
                             lambda ps: ps[0:DQK, :].rearrange("p (h t) -> p h t", h=4))

            def expo(h):
                act.wait_ge(nmax.sem, h + 1)
                for n in range(NT):
                    w = (n + 1) * P
                    pr = m["probs"][:, h % 2, n, 0:w]
                    last = nc.scalar.activation(pr, pr, ACT.Exp, bias=nmx[:, 2 * h + n:2 * h + n + 1],
                                                accum_out=den[:, 2 * h + n:2 * h + n + 1])
                last.then_inc(exped, 1)

            expo(0)
            for h in range(2 * H):
                if h + 1 < 2 * H:
                    expo(h + 1)
                if h >= 2:
                    bank.read(act, ("Y", h - 2))
                copy_out(("PT", h), m["probsT"][:, h % 2].rearrange("p a b -> p (a b)"), lambda ps: ps[:, 0:3 * P])
            for n in range(NT):
                act.wait_ge(var_ok, n + 1)
                nc.scalar.activation(st[:, 15:16], st[:, 14:15], ACT.Sqrt).then_inc(std_ok, 1)

        @block.vector
        def _(dve):
            dve.wait_ge(c_in, 16)
            idle = m["probsT"][:].rearrange("p a b c -> p (a b c)")
            tmp = (idle[:, 0:T], idle[:, T:2 * T])

            def table(n, rot):
                o = C_ROPE + n * ROPE_W + (0 if rot == ROT else 2 * ROT)
                return m["consts"][:, o:o + 2 * rot]

            def temps(heads, rot):
                return [x[:, 0:heads * rot].rearrange("p (h d) -> p h d", d=rot) for x in tmp]

            for n in range(NT):
                bank.await_drained(dve, ("tok", 0, n))
                bank.await_drained(dve, ("tok", 1, n))
                qk = tok[:, n, 0:2 * W].rearrange("p (h d) -> p h d", d=DH)[:, :, 0:ROT]
                rope(nc, dve, dv, qk, qk, temps(2 * H, ROT), table(n, ROT), 2 * H, ROT, qk_roped)
            dve.wait_ge(ss_ready, 2 * NT)
            dv.done(nc.vector.tensor_scalar(ss[:, 0:NT], ss[:, 0:NT], 1.0 / QLORA, RMS_EPS, ALU.mult, ALU.add))
            dv.wait(dve)
            nc.vector.tensor_scalar(ss[:, NT:2 * NT], ss[:, NT:2 * NT], 1.0 / KVLORA, RMS_EPS,
                                    ALU.mult, ALU.add).then_inc(ms_ready, 1)
            dve.wait_ge(root_ready, 1)
            dv.done(nc.vector.reciprocal(rs, rs))
            dv.wait(dve)
            for n in range(NT):
                for base, w, col in ((CQ0, QLORA, n), (CKV0, KVLORA, NT + n)):
                    dv.done(nc.vector.tensor_scalar(tok[:, n, base:base + w], tok[:, n, base:base + w],
                                                    rs[:, col:col + 1], None, ALU.mult))
                kr = tok[:, n, KR0:KR0 + ROPE].unsqueeze(1)
                rope(nc, dve, dv, kr, kr, temps(1, ROPE), table(n, ROPE), 1, ROPE, lora_ready)
            for which in ("qT", "kT"):
                for n in range(NT):
                    ps = bank.read(dve, (which, n))
                    bank.drain((which, n), nc.vector.tensor_copy(m[which][:, :, n * P:(n + 1) * P],
                                                                 ps[:, :].rearrange("p (k t) -> p k t", t=P)))
            dve.wait_ge(b_in, 16)
            for which, K, col in (("cqT", QLORA // P, B_QN), ("ckvT", KVLORA // P, B_KVN)):
                for n in range(NT):
                    ps = bank.read(dve, (which, n))
                    gain = m["cols"][:, col:col + K].unsqueeze(2).to_broadcast([P, K, P])
                    bank.drain((which, n), nc.vector.tensor_tensor(
                        m[which][:, :, n * P:(n + 1) * P],
                        ps[:, 0:K * P].rearrange("p (k t) -> p k t", t=P), gain, ALU.mult))
            for n in range(NT):
                bank.await_drained(dve, ("qup", n, 0))
                bank.await_drained(dve, ("qup", n, 1))
                qr = m["qm"][:, n, :].rearrange("p (h d) -> p h d", d=DQK)[:, :, DH:DQK]
                rope(nc, dve, dv, qr, qr, temps(H, ROPE), table(n, ROPE), H, ROPE, qm_roped)

            def mask_max(h):
                ps = bank.read(dve, ("S", h))
                if h >= 2:
                    bank.read(dve, ("PT", h - 2))
                for n in range(NT):
                    w = (n + 1) * P
                    mask = m["consts"][:, C_MASK + (NT - 1 - n) * P:C_MASK + T]
                    c = 2 * h + n
                    last = nc.vector.tensor_tensor_reduce(
                        out=m["probs"][:, h % 2, n, 0:w], in0=ps[:, n * P:n * P + w], in1=mask, scale=scales[h],
                        scalar=LOWEST, op0=ALU.add, op1=ALU.max, accum_out=mx[:, c:c + 1])
                bank.drain(("S", h), last)
                bank.await_drained(dve, ("S", h))
                nmax.done(nc.vector.tensor_scalar(nmx[:, 2 * h:2 * h + 2], mx[:, 2 * h:2 * h + 2], -1.0, None, ALU.mult))

            def normalise(h):
                dve.wait_ge(exped, h + 1)
                dv.done(nc.vector.reciprocal(rden[:, 2 * h:2 * h + 2], den[:, 2 * h:2 * h + 2]))
                dv.wait(dve)
                for n in range(NT):
                    pr = m["probs"][:, h % 2, n, 0:(n + 1) * P]
                    last = nc.vector.tensor_scalar(pr, pr, rden[:, 2 * h + n:2 * h + n + 1], None, ALU.mult)
                probs_ok.done(last)

            def keep_y(h):
                ps = bank.read(dve, ("Y", h))
                r = slice(DH * (h % 2), DH * (h % 2) + DH)
                bank.drain(("Y", h), nc.vector.tensor_copy(m["yT"][r, h // H, h % H // 2, :], ps[0:DH, 0:T]))

            mask_max(0)
            mask_max(1)
            for h in range(2 * H):
                normalise(h)
                if h >= 1:
                    keep_y(h - 1)
                if h + 2 < 2 * H:
                    mask_max(h + 2)
            keep_y(2 * H - 1)
            for j in range(2 * KD):
                bank.await_drained(dve, ("gate", j))
            for c in range(KD):
                ps = bank.read(dve, ("br", c))
                t = m["probs"][:, c % 2]
                bank.drain(("br", c), nc.vector.tensor_tensor(t, ps[:, :].rearrange("p (b t) -> p b t", b=2),
                                                              m["sigT"][:, :, c, :], ALU.mult))
                bank.await_drained(dve, ("br", c))
                merged_ok.done(nc.vector.tensor_tensor(m["mergedT"][:, c, :], t[:, 0, :], t[:, 1, :], ALU.add))
            dve.wait_ge(xt_in, 16)
            dve.wait_ge(ln_in, 32)
            for n in range(NT):
                z = m["x_tok"][:, n, :]
                for c in range(2):
                    ps = bank.read(dve, ("mix", n, c))
                    zc = z[:, c * 512:(c + 1) * 512]
                    bank.drain(("mix", n, c), nc.vector.scalar_tensor_tensor(
                        out=zc, in0=zc, scalar=ALPHA, in1=ps[:, :], op0=ALU.mult, op1=ALU.add))
                for c in range(2):
                    bank.await_drained(dve, ("mix", n, c))
                layer_norm(nc, dve, dv, st, z, m["h"][:, n, :], m["ln1"][:, 0, :], m["ln1"][:, 1, :],
                           var_ok, std_ok, n, h_ok)


def route(nc, io, m, bank):
    consts = m["consts"]
    ident, iota = consts[:, C_ID:C_ID + P], consts[:, C_IOTA:C_IOTA + NK]
    iota16 = consts[:, C_IOTA:C_IOTA + TK]
    GT = 4
    BODY = 8
    HALVES = BODY // GT

    with ExitStack() as ctx:
        def sem(name):
            return ctx.enter_context(nc.semaphore(name))

        wq_in = [sem(f"peer_wq_slot{k}") for k in range(3)]
        subk_in, split_ok = sem("sub_keys_in"), sem("h_split")
        exp_ok = sem("gate_exp_ready")
        oh_ready = sem("onehot_ready")
        g_full, g_free = sem("g_bank_full"), sem("g_bank_free")
        dv = Steps(ctx, nc, "route_dve")
        exp_in = Steps(ctx, nc, "gate_exp_in")
        slot_ok = Steps(ctx, nc, "slots_ready")
        block = ctx.enter_context(nc.Block())

        @block.sync
        def _(sp):
            w_q = io["peer_w_q"].rearrange("(k p) c -> p k c", p=P)
            for c in range(4):
                if c >= 3:
                    bank.read(sp, ("pq", 2 * (c - 3) + 1))
                sp.dma_start(m["ring2"][:, c % 3], w_q[:, :, c * CHUNK:(c + 1) * CHUNK]).then_inc(wq_in[c % 3], 16)
                if c == 0:
                    sp.dma_start(m["subk"][:], io["subkT"].rearrange("h d n -> d h n")).then_inc(subk_in, 16)

        @block.tensor
        def _(pe):
            for n in range(NT):
                for c in range(2):
                    ps = bank.fill(pe, ("hT", n, c))
                    for i in range(4):
                        k = 4 * c + i
                        last = nc.tensor.transpose(ps[:, i * P:(i + 1) * P], m["h"][:, n, k * P:(k + 1) * P], ident)
                    bank.filled(("hT", n, c), last)
            for n in range(NT):
                for c in range(2):
                    bank.await_drained(pe, ("hT", n, c))
            for c in range(4):
                pe.wait_ge(wq_in[c % 3], 16 * (c // 3 + 1))
                for g in (2 * c, 2 * c + 1):
                    ps = bank.fill(pe, ("pq", g))
                    for e in range(2):
                        col = (2 * (g % 2) + e) * DKH
                        for k in range(KD):
                            last = nc.tensor.matmul(ps[:, e * T:(e + 1) * T], m["ring2"][:, c % 3, k, col:col + DKH],
                                                    m["hT"][:, k, :], start=(k == 0), stop=(k == KD - 1))
                    bank.filled(("pq", g), last)
                if c == 0:
                    pe.wait_ge(subk_in, 16)
                for g in (2 * c, 2 * c + 1):
                    bank.await_drained(pe, ("pq", g))
                for n in range(NT):
                    ps = bank.fill(pe, ("sim", n, c))
                    for i in range(4):
                        hp = 4 * c + i
                        last = nc.tensor.matmul(ps[:, i * NK:(i + 1) * NK], m["pqT"][:, hp, n * P:(n + 1) * P],
                                                m["subk"][:, hp, :], start=True, stop=True)
                    bank.filled(("sim", n, c), last)
            pe.wait_ge(slot_ok.sem, NT)
            for w in range(3):
                ps = bank.fill(pe, ("slotT", w))
                for n in range(NT):
                    last = nc.tensor.transpose(ps[:, n * P:(n + 1) * P], m["slot"][:, w, n, :], ident)
                bank.filled(("slotT", w), last)
            for w in range(3):
                bank.await_drained(pe, ("slotT", w))
            with pe.Fori(0, T // BODY) as i:
                for g in range(HALVES):
                    pe.wait_ge(g_free, i * HALVES + g + 1)
                    pe.wait_ge(oh_ready, i * BODY + GT * (g + 1))
                    for j in range(GT):
                        s = GT * g + j
                        last = nc.tensor.matmul(bank.psum[g][:, j * NK:(j + 1) * NK], m["oh2"][:, s, :],
                                                m["oh1"][:, s, :], start=True, stop=True)
                    last.then_inc(g_full, 1)

        @block.scalar
        def _(act):
            for n in range(NT):
                for c in range(2):
                    ps = bank.read(act, ("hT", n, c))
                    bank.drain(("hT", n, c), nc.scalar.activation(
                        m["hT"][:, 4 * c:4 * c + 4, n * P:(n + 1) * P],
                        ps[:, :].rearrange("p (k t) -> p k t", t=P), ACT.Copy))
            for n in range(NT):
                for c in range(2):
                    bank.await_drained(act, ("hT", n, c))
            nc.scalar.activation(m["h_hi"][:], m["hT"][:], ACT.Copy).then_inc(split_ok, 1)
            for c in range(4):
                for g in (2 * c, 2 * c + 1):
                    ps = bank.read(act, ("pq", g))
                    bank.drain(("pq", g), nc.scalar.activation(
                        m["pqT"][:, 2 * g:2 * g + 2, :], ps[:, :].rearrange("p (e t) -> p e t", e=2), ACT.Copy))
                for n in range(NT):
                    ps = bank.read(act, ("sim", n, c))
                    bank.drain(("sim", n, c), nc.scalar.activation(
                        m["sims"][:, n, 4 * c:4 * c + 4, :], ps[:, :].rearrange("p (i k) -> p i k", k=NK), ACT.Copy))
            for n in range(NT):
                act.wait_ge(exp_in.sem, n + 1)
                nc.scalar.activation(m["ex"][:], m["ex"][:], ACT.Exp).then_inc(exp_ok, 1)
            for w in range(3):
                bank.await_drained(act, ("slotT", w))
            act.sem_inc(g_free, HALVES)
            with act.Fori(0, T // BODY) as i:
                for g in range(HALVES):
                    act.wait_ge(g_full, i * HALVES + g + 1)
                    nc.scalar.activation(m["G"][:, :, bass.ds(i * BODY + GT * g, GT)],
                                         bank.psum[g][:, :].rearrange("p (t i) -> p i t", t=GT),
                                         ACT.Copy).then_inc(g_free, 1)

        @block.vector
        def _(dve):
            def top16(src, scratch, vals, idx):
                dv.done(nc.vector.max(vals[:, 0:8], src))
                dv.wait(dve)
                dv.done(nc.vector.max_index(idx[:, 0:8], vals[:, 0:8], src))
                dv.done(nc.vector.match_replace(scratch, vals[:, 0:8], src, LOWEST))
                dv.wait(dve)
                dv.done(nc.vector.max(vals[:, 8:16], scratch))
                dv.wait(dve)
                dv.done(nc.vector.max_index(idx[:, 8:16], vals[:, 8:16], scratch))

            pst = m["pstat"]
            dve.wait_ge(split_ok, 1)
            dv.done(nc.vector.tensor_tensor(m["h_lo"][:], m["hT"][:], m["h_hi"][:].bitcast(F32), ALU.subtract))
            for n in range(NT):
                for hp in range(HP):
                    bank.await_drained(dve, ("sim", n, hp // 4))
                    top16(m["sims"][:, n, hp, :], m["sims2"][:, hp % 4, :], m["topv"][:, hp, :], m["topi"][:, hp, :])
                dv.wait(dve)
                dv.done(nc.vector.tensor_copy(m["topf"][:], m["topi"][:]))
                tv = m["topv"][:].rearrange("p (h e) k -> p h e k", e=2)
                dv.done(nc.vector.tensor_tensor(
                    m["cand"][:].rearrange("p h (a b) -> p h a b", a=TK),
                    tv[:, :, 0, :].unsqueeze(3).to_broadcast([P, PH, TK, TK]),
                    tv[:, :, 1, :].unsqueeze(2).to_broadcast([P, PH, TK, TK]), ALU.add))
                dv.wait(dve)
                for h in range(PH):
                    top16(m["cand"][:, h, :], m["cand2"][:, h % 2, :], m["best"][:, h, :], m["bpos"][:, h, :])
                dv.wait(dve)
                exp_in.done(nc.vector.tensor_tensor(m["ex"][:], m["best"][:],
                                                    m["best"][:, :, 0:1].to_broadcast([P, PH, TK]), ALU.subtract))
                pos = m["bpos"][:].rearrange("p h k -> p (h k)")
                dv.done(nc.vector.tensor_scalar(m["bab"][:, 0, :], pos, 4, None, ALU.logical_shift_right))
                dv.done(nc.vector.tensor_scalar(m["bab"][:, 1, :], pos, TK - 1, None, ALU.bitwise_and))
                dv.wait(dve)
                dv.done(nc.vector.tensor_copy(m["babf"][:], m["bab"][:]))
                dv.wait(dve)
                tf = m["topf"][:].rearrange("p (h e) k -> p h e k", e=2)
                for e in range(2):
                    dv.done(nc.vector.tensor_tensor(
                        m["eq"][:], m["babf"][:, e, :].unsqueeze(2).to_broadcast([P, SLOTS, TK]),
                        iota16.unsqueeze(1).to_broadcast([P, SLOTS, TK]), ALU.is_equal))
                    dv.wait(dve)
                    eq4 = m["eq"][:].rearrange("p (h k) a -> p h k a", h=PH)
                    dv.done(nc.vector.tensor_tensor(
                        eq4, eq4, tf[:, :, e, :].unsqueeze(2).to_broadcast([P, PH, TK, TK]), ALU.mult))
                    dv.wait(dve)
                    dv.done(nc.vector.tensor_reduce(m["slot"][:, e, n, :], m["eq"][:], AX_X, ALU.add))
                    dv.wait(dve)
                dve.wait_ge(exp_ok, n + 1)
                dv.done(nc.vector.tensor_reduce(pst[:, 0, :], m["ex"][:], AX_X, ALU.add))
                dv.wait(dve)
                dv.done(nc.vector.reciprocal(pst[:, 1, :], pst[:, 0, :]))
                dv.wait(dve)
                slot_ok.done(nc.vector.tensor_tensor(m["slot"][:, 2, n, :].rearrange("p (h k) -> p h k", h=PH),
                                                     m["ex"][:], pst[:, 1, :].unsqueeze(2).to_broadcast([P, PH, TK]),
                                                     ALU.mult))
                slot_ok.wait(dve)
            for w in range(3):
                ps = bank.read(dve, ("slotT", w))
                bank.drain(("slotT", w), nc.vector.tensor_copy(m["slotT"][:, w, :], ps[:, 0:T]))
            for w in range(3):
                bank.await_drained(dve, ("slotT", w))
            sT = m["slotT"]
            with dve.Fori(0, T // BODY) as i:
                for s in range(BODY):
                    if s % GT == 0:
                        dve.wait_ge(g_free, i * HALVES + s // GT + 1)
                    t = bass.ds(i * BODY + s, 1)
                    nc.vector.tensor_scalar(m["oh1"][:, s, :], iota, sT[:, 0, t], None, ALU.is_equal)
                    nc.vector.tensor_scalar(m["oh2"][:, s, :], iota, sT[:, 1, t], sT[:, 2, t],
                                            ALU.is_equal, ALU.mult).then_inc(oh_ready, 1)


def experts(nc, io, m, bank):
    acts = [bank.psum[b][:, 0:T] for b in range(4)]
    prods = [bank.psum[b][:, T:2 * T] for b in range(4)]
    out = [[bank.psum[4 + 2 * n + c] for c in range(2)] for n in range(NT)]
    UNROLL = 4
    SLOTS2 = 2
    ROUNDS = (NK - 1) // UNROLL

    with ExitStack() as ctx:
        def sem(name):
            return ctx.enter_context(nc.semaphore(name))

        u_in = [sem(f"u_slot{k}") for k in range(2)]
        v_in = [sem(f"v_slot{k}") for k in range(2)]
        u_hi_ok, v_hi_ok = sem("u_hi_ready"), sem("v_hi_ready")
        u_ok, v_ok = sem("u_split"), sem("v_split")
        acts_ok, act_used = sem("uh_ready"), sem("uh_used")
        gelu_ok, prod_ok, w_hi_ok = sem("gelu_ready"), sem("gated_ready"), sem("w_hi_ready")
        w_ok = sem("w_split")
        uh_done, wv_done = sem("uh_done"), sem("wv_done")
        tail_in = sem("tail_weights_in")
        block = ctx.enter_context(nc.Block())


        def over_blocks(eng, step):
            with eng.Fori(0, ROUNDS) as i:
                for r in range(UNROLL):
                    step(i * UNROLL + (1 + r), 1 + r)
            for b in range(1 + ROUNDS * UNROLL, NK):
                step(b, b)

        @block.sync
        def _(sp):
            def load(b, s):
                sp.wait_ge(u_ok, b + 1)
                sp.dma_start(m["u_raw"][:, s % SLOTS2], io["uT"][bass.ds(b, 1)].rearrange("o p k e -> (o p) k e")
                             ).then_inc(u_in[s % SLOTS2], 16)
                sp.wait_ge(v_ok, b + 1)
                sp.dma_start(m["v_raw"][:, s % SLOTS2], io["v"][bass.ds(b, 1)].rearrange("o p d -> (o p) d")
                             ).then_inc(v_in[s % SLOTS2], 16)

            load(0, 0)
            over_blocks(sp, load)
            sp.dma_start(m["w_ple_gate"][:], io["w_ple_gate"].rearrange("(k p) c -> p k c", p=P)).then_inc(tail_in, 16)
            sp.dma_start(m["w_ple_proj"][:], io["w_ple_proj"].rearrange("(k p) c -> p k c", p=P)).then_inc(tail_in, 16)
            sp.dma_start(m["pT"][:], io["pT"].rearrange("(k p) t -> p k t", p=P)).then_inc(tail_in, 16)
            for j, w in enumerate(("b_ple_gate", "ln2_g", "ln2_b")):
                sp.dma_start(m["rows"][:, j, :], io[w].partition_broadcast(P)).then_inc(tail_in, 16)
            sp.wait_ge(tail_in, 16 * 6)

        @block.tensor
        def _(pe):
            def activations(b, s):
                pe.wait_ge(u_ok, b + 1 + SLOTS2)
                pe.wait_ge(w_ok, b + 1)
                u_hi, u_lo = m["u_hi"][:, s % SLOTS2], m["u_lo"][:, s % SLOTS2]
                for k in range(KD):
                    nc.tensor.matmul(acts[s % 4], u_hi[:, k, :], m["h_hi"][:, k, :], start=(k == 0), stop=False)
                    nc.tensor.matmul(acts[s % 4], u_hi[:, k, :], m["h_lo"][:, k, :], start=False, stop=False)
                    last = nc.tensor.matmul(acts[s % 4], u_lo[:, k, :], m["h_hi"][:, k, :],
                                            start=False, stop=(k == KD - 1))
                last.then_inc(uh_done, 1)

            def values(b, s, first=False):
                pe.wait_ge(v_ok, b + 1 + SLOTS2)
                pe.wait_ge(w_ok, b + 1 + UNROLL)
                v = s % SLOTS2
                for n in range(NT):
                    t = slice(n * P, (n + 1) * P)
                    for w, x, f in (("w_hi", "v_hi", first), ("w_hi", "v_lo", False), ("w_lo", "v_hi", False)):
                        for c in range(2):
                            last = nc.tensor.matmul(out[n][c][:, :], m[w][:, v, t], m[x][:, v, c * 512:(c + 1) * 512],
                                                    start=f, stop=False, skip_group_check=True)
                last.then_inc(wv_done, 1)

            def step(b, s):
                activations(b, s)
                values(b - 1, s - 1, first=(isinstance(b, int) and b == 1))

            activations(0, 0)
            activations(1, 1)
            values(0, 0, first=True)

            def later(b, s):
                activations(b + 1, s + 1)
                values(b, s)

            with pe.Fori(0, ROUNDS) as i:
                for r in range(UNROLL):
                    later(i * UNROLL + (1 + r), 1 + r)
            for b in range(1 + ROUNDS * UNROLL, NK - 1):
                later(b, b)
            values(NK - 1, NK - 1)

        def split_hi(act, raw, hi, arrived, slot_free, ready, b, s, count):
            act.wait_ge(arrived, count)
            act.wait_ge(slot_free, b + 1)
            nc.scalar.activation(hi, raw, ACT.Copy).then_inc(ready, 1)

        @block.scalar
        def _(act):
            act.sem_inc(u_ok, SLOTS2)
            act.sem_inc(v_ok, SLOTS2)
            act.sem_inc(uh_done, SLOTS2)
            act.sem_inc(wv_done, SLOTS2)
            act.sem_inc(w_ok, UNROLL)

            def step(b, s, count, next_count, more=True):
                v = s % SLOTS2
                if more:
                    split_hi(act, m["u_raw"][:, 1 - v], m["u_hi"][:, 1 - v], u_in[1 - v], uh_done, u_hi_ok,
                             b + 1, s + 1, next_count)
                act.wait_ge(uh_done, b + 1 + SLOTS2)
                nc.scalar.activation(acts[s % 4], acts[s % 4], ACT.Gelu).then_inc(gelu_ok, 1)
                split_hi(act, m["v_raw"][:, v], m["v_hi"][:, v], v_in[v], wv_done, v_hi_ok, b, s, count)
                act.wait_ge(prod_ok, b + 1)
                nc.scalar.activation(m["w_hi"][:, v], prods[s % 4], ACT.Copy).then_inc(w_hi_ok, 1)

            split_hi(act, m["u_raw"][:, 0], m["u_hi"][:, 0], u_in[0], uh_done, u_hi_ok, 0, 0, 16)
            step(0, 0, 16, 16)
            with act.Fori(0, ROUNDS) as i:
                for r in range(UNROLL):
                    s = 1 + r
                    step(i * UNROLL + s, s, i * (UNROLL // 2 * 16) + 16 * (s // 2 + 1),
                         i * (UNROLL // 2 * 16) + 16 * ((s + 1) // 2 + 1))
            for b in range(1 + ROUNDS * UNROLL, NK):
                step(b, b, 16 * (b // 2 + 1), 16 * ((b + 1) // 2 + 1), more=(b + 1 < NK))

        @block.vector
        def _(dve):
            def split_lo(raw, hi, lo, hi_ready, slot_free, ready, b):
                dve.wait_ge(hi_ready, b + 1)
                dve.wait_ge(slot_free, b + 1)
                nc.vector.tensor_tensor(lo, raw, hi.bitcast(F32), ALU.subtract).then_inc(ready, 1)

            def step(b, s, more=True):
                v = s % SLOTS2
                if more:
                    split_lo(m["u_raw"][:, 1 - v], m["u_hi"][:, 1 - v], m["u_lo"][:, 1 - v],
                             u_hi_ok, uh_done, u_ok, b + 1)
                dve.wait_ge(gelu_ok, b + 1)
                nc.vector.tensor_tensor(prods[s % 4], acts[s % 4],
                                        m["G"][:, bass.ds(b, 1), :].rearrange("p o t -> p (o t)"),
                                        ALU.mult).then_inc(prod_ok, 1)
                split_lo(m["v_raw"][:, v], m["v_hi"][:, v], m["v_lo"][:, v], v_hi_ok, wv_done, v_ok, b)
                dve.wait_ge(w_hi_ok, b + 1)
                nc.vector.tensor_tensor(m["w_lo"][:, v], prods[s % 4], m["w_hi"][:, v].bitcast(F32),
                                        ALU.subtract).then_inc(w_ok, 1)

            split_lo(m["u_raw"][:, 0], m["u_hi"][:, 0], m["u_lo"][:, 0], u_hi_ok, uh_done, u_ok, 0)
            step(0, 0)
            with dve.Fori(0, ROUNDS) as i:
                for r in range(UNROLL):
                    step(i * UNROLL + (1 + r), 1 + r)
            for b in range(1 + ROUNDS * UNROLL, NK):
                step(b, b, more=(b + 1 < NK))


def tail(nc, io, m, bank):
    ident = m["consts"][:, C_ID:C_ID + P]
    st = m["small"][:, 136:160]
    psum = bank.psum

    with ExitStack() as ctx:
        def sem(name):
            return ctx.enter_context(nc.semaphore(name))

        proj_full = sem("ple_proj_full")
        rT_full, gate_full = sem("rT_full"), sem("ple_gate_full")
        rT_ok = sem("rT_ready")
        sig_ok, out_done = sem("ple_sigmoid"), sem("out_written")
        var_ok, std_ok = sem("var2_ready"), sem("std2_ready")
        dv = Steps(ctx, nc, "tail_dve")
        r_ok = Steps(ctx, nc, "r_ready")
        proj_ok = Steps(ctx, nc, "ple_proj_copied")
        logit_ok = Steps(ctx, nc, "ple_logits")
        y_ok = Steps(ctx, nc, "y_ready")
        block = ctx.enter_context(nc.Block())
        pairs = [(n, c) for n in range(NT) for c in range(2)]

        @block.tensor
        def _(pe):
            for j, (n, c) in enumerate(pairs):
                for k in range(PLE // P):
                    last = nc.tensor.matmul(psum[j][:, :], m["pT"][:, k, n * P:(n + 1) * P],
                                            m["w_ple_proj"][:, k, c * 512:(c + 1) * 512],
                                            start=(k == 0), stop=(k == PLE // P - 1))
                last.then_inc(proj_full, 1)
            for j, (n, c) in enumerate(pairs):
                pe.wait_ge(proj_ok.sem, j + 1)
                pe.wait_ge(r_ok.sem, j + 1)
                for i in range(4):
                    last = nc.tensor.transpose(psum[j][:, i * P:(i + 1) * P],
                                               m["r"][:, n, (4 * c + i) * P:(4 * c + i + 1) * P], ident)
                last.then_inc(rT_full, 1)
            for j, (n, c) in enumerate(pairs):
                pe.wait_ge(rT_ok, 2 * (n + 1))
                for k in range(KD):
                    last = nc.tensor.matmul(psum[4 + j][:, :], m["rT"][:, k, n * P:(n + 1) * P],
                                            m["w_ple_gate"][:, k, c * 512:(c + 1) * 512],
                                            start=(k == 0), stop=(k == KD - 1))
                last.then_inc(gate_full, 1)

        @block.scalar
        def _(act):
            for j, (n, c) in enumerate(pairs):
                act.wait_ge(rT_full, j + 1)
                nc.scalar.activation(m["rT"][:, 4 * c:4 * c + 4, n * P:(n + 1) * P],
                                     psum[j][:, :].rearrange("p (k t) -> p k t", t=P), ACT.Copy).then_inc(rT_ok, 1)
            for j, (n, c) in enumerate(pairs):
                act.wait_ge(logit_ok.sem, j + 1)
                s = m["ple2"][:, n, c * 512:(c + 1) * 512]
                nc.scalar.activation(s, s, ACT.Sigmoid).then_inc(sig_ok, 1)
            for n in range(NT):
                act.wait_ge(var_ok, n + 1)
                nc.scalar.activation(st[:, 15:16], st[:, 14:15], ACT.Sqrt).then_inc(std_ok, 1)

        @block.vector
        def _(dve):
            for j, (n, c) in enumerate(pairs):
                half = slice(c * 512, (c + 1) * 512)
                r_ok.done(nc.vector.scalar_tensor_tensor(out=m["r"][:, n, half], in0=m["h"][:, n, half], scalar=ALPHA,
                                                         in1=psum[4 + j][:, :], op0=ALU.mult, op1=ALU.add))
                dve.wait_ge(proj_full, j + 1)
                proj_ok.done(nc.vector.tensor_copy(m["ple"][:, n, half], psum[j][:, :]))
            for j, (n, c) in enumerate(pairs):
                dve.wait_ge(gate_full, j + 1)
                logit_ok.done(nc.vector.tensor_tensor(m["ple2"][:, n, c * 512:(c + 1) * 512], psum[4 + j][:, :],
                                                      m["rows"][:, 0, c * 512:(c + 1) * 512], ALU.add))
            r_ok.wait(dve)
            proj_ok.wait(dve)
            for n in range(NT):
                dve.wait_ge(sig_ok, 2 * (n + 1))
                z = m["ple"][:, n, :]
                dv.done(nc.vector.tensor_tensor(z, z, m["ple2"][:, n, :], ALU.mult))
                dv.wait(dve)
                dv.done(nc.vector.tensor_tensor(z, z, m["r"][:, n, :], ALU.add))
                dv.wait(dve)
                layer_norm(nc, dve, dv, st, z, m["y_out"][:, n, :], m["rows"][:, 1, :], m["rows"][:, 2, :],
                           var_ok, std_ok, n, y_ok)

        @block.sync
        def _(sp):
            for n in range(NT):
                sp.wait_ge(y_ok.sem, n + 1)
                sp.dma_start(io["out"][n * P:(n + 1) * P, :], m["y_out"][:, n, :]).then_inc(out_done, 16)
            sp.wait_ge(out_done, 16 * NT)


def program(nc, io):
    m = memory(nc)
    with ExitStack() as ctx:
        psum = [ctx.enter_context(nc.psum_tensor(f"bank{b}", [P, 512], F32)) for b in range(8)]
        bank = Banks(ctx, nc, psum, group_order())
        front(nc, io, m, bank)
        route(nc, io, m, bank)
        experts(nc, io, m, bank)
        tail(nc, io, m, bank)


def constants():
    c = np.zeros((P, C_COLS), np.float32)
    c[:, C_ID:C_ID + P] = np.eye(P, dtype=np.float32)
    q, k = np.arange(P)[:, None], np.arange(P)[None, :]
    c[:, C_MASK + P:C_MASK + T] = np.where(k <= q, 0.0, NEG)
    c[:, C_IOTA:C_IOTA + NK] = np.arange(NK)
    for n in range(NT):
        o = C_ROPE + n * ROPE_W
        for rot, theta in ((ROT, 500000.0), (ROPE, 10000.0)):
            inv = np.power(np.float32(theta), -np.arange(0, rot, 2, dtype=np.float32) / np.float32(rot))
            ang = (np.arange(P, dtype=np.float32) + n * P)[:, None] * inv[None, :].astype(np.float32)
            cos, sin = np.cos(ang), np.sin(ang)
            c[:, o:o + 2 * rot] = np.concatenate([cos, cos, -sin, sin], axis=1)
            o += 2 * rot
    return c


def kernel(**inputs):
    import concourse.bacc as bacc
    from concourse.bass_utils import run_bass_kernel_spmd

    i = {k: np.asarray(v) for k, v in inputs.items()}
    arrays = {
        "x": i["x"][0],
        "xT": i["x"][0].T,
        "pT": i["p"][0, 0].T,
        "w_in": i["w_in"][0],
        "w_q_up": i["w_q_up"][0],
        "w_kv_up": i["w_kv_up"][0],
        "w_branch_moba": i["w_branch_moba"][0],
        "w_branch_mla": i["w_branch_mla"][0],
        "w_out": i["w_out"][0],
        "ln1_g": i["ln1_g"][0],
        "ln1_b": i["ln1_b"][0],
        "peer_w_q": i["peer_w_q"][0],
        "subkT": i["peer_sub_keys"][0].reshape(HP, NK, DKH).transpose(0, 2, 1),
        "uT": i["peer_u"][0].reshape(NK, NK, KD, P).transpose(0, 3, 2, 1),
        "v": i["peer_v"][0].reshape(NK, NK, D),
        "w_ple_proj": i["w_ple_proj"][0],
        "w_ple_gate": i["w_ple_gate"][0],
        "b_ple_gate": i["b_ple_gate"][0],
        "ln2_g": i["ln2_g"][0],
        "ln2_b": i["ln2_b"][0],
        "cols": np.concatenate([i["b_gates"][0].reshape(-1, P).T, i["mla_q_norm"][0].reshape(-1, P).T,
                                i["mla_kv_norm"][0].reshape(-1, P).T], axis=1),
        "consts": constants(),
    }
    nc = bacc.Bacc("TRN2", target_bir_lowering=False, num_devices=1)
    feeds, io = {}, {}
    for name, a in arrays.items():
        a = np.ascontiguousarray(a)
        feeds[f"{name}_dram"] = a
        io[name] = nc.dram_tensor(f"{name}_dram", a.shape, mybir.dt.from_np(a.dtype), kind="ExternalInput").ap()
    io["out"] = nc.dram_tensor("out_dram", (T, D), F32, kind="ExternalOutput").ap()
    program(nc, io)
    r = run_bass_kernel_spmd(nc, [feeds], core_ids=[0])
    return r.results[0]["out_dram"].reshape(1, T, D)
```

```python
from contextlib import ExitStack

import numpy as np

import concourse.bass as bass
from concourse import mybir

P = 128
D = 1024
T = 256
NT = T // P
KD = D // P
H = 8
DH = 64
ROT = DH // 4
QLORA, KVLORA, ROPE = 512, 256, 32
DQK = DH + ROPE
W = H * DH
Q0, K0, V0, CQ0, CKV0, KR0 = 0, W, 2 * W, 3 * W, 3 * W + QLORA, 3 * W + QLORA + KVLORA
TOK = KR0 + ROPE
IN_COLS = TOK + 2 * D
CHUNK = 512
PH = 8
NK = 128
DKH = 128
HP = 2 * PH
TK = 16
SLOTS = PH * TK
PLE = 256
OHT = 8
HEADS_AHEAD = 3
AHEAD = 20
ALPHA = 2.0 ** 0.25
LN_EPS, RMS_EPS = 1e-5, 1e-6
NEG = -1e30
LOWEST = -3.0e38

F32 = mybir.dt.float32
F32R = mybir.dt.float32r
U32 = mybir.dt.uint32
BF16 = mybir.dt.bfloat16
ALU = mybir.AluOpType
ACT = mybir.ActivationFunctionType
AX_X = mybir.AxisListType.X

C_ID, C_MASK, C_IOTA, C_ROPE = 0, P, P + T, 2 * P + T
ROPE_W = 2 * ROT + 2 * ROPE
C_COLS = C_ROPE + NT * ROPE_W
B_GATE, B_QN, B_KVN = 0, 2 * KD, 2 * KD + QLORA // P
B_COLS = B_KVN + KVLORA // P

KB = 1024


class Banks:

    def __init__(self, ctx, nc, psum, order):
        self.psum = psum
        self.full = [ctx.enter_context(nc.semaphore(f"bank_full{b}")) for b in range(8)]
        self.drained = [ctx.enter_context(nc.semaphore(f"bank_drained{b}")) for b in range(8)]
        self.at = {name: g for g, name in enumerate(order)}

    def fill(self, pe, name):
        g = self.at[name]
        if g >= 8:
            pe.wait_ge(self.drained[g % 8], g // 8)
        return self.psum[g % 8]

    def filled(self, name, last):
        last.then_inc(self.full[self.at[name] % 8], 1)

    def read(self, eng, name):
        g = self.at[name]
        eng.wait_ge(self.full[g % 8], g // 8 + 1)
        return self.psum[g % 8]

    def drain(self, name, last):
        last.then_inc(self.drained[self.at[name] % 8], 1)

    def await_drained(self, eng, name):
        g = self.at[name]
        eng.wait_ge(self.drained[g % 8], g // 8 + 1)


class Steps:

    def __init__(self, ctx, nc, name):
        self.sem = ctx.enter_context(nc.semaphore(name))
        self.n = 0

    def done(self, ins):
        ins.then_inc(self.sem, 1)
        self.n += 1

    def wait(self, eng):
        eng.wait_ge(self.sem, self.n)


def over(eng, lo, hi, step, unroll=4):
    rounds = (hi - lo) // unroll
    if rounds:
        with eng.Fori(0, rounds) as i:
            for r in range(unroll):
                step(i * unroll + (lo + r), lo + r)
    for b in range(lo + rounds * unroll, hi):
        step(b, b)


def group_order():
    o = [("tok", c, n) for c in range(5) for n in range(NT)]
    o += [("qT", n) for n in range(NT)] + [("kT", n) for n in range(NT)]
    o += [("gate", j) for j in range(0, 8)]
    o += [("cqT", n) for n in range(NT)] + [("ckvT", n) for n in range(NT)] + [("krT",)]
    o += [("gate", j) for j in range(8, 12)]
    o += [("qup", n, c) for n in range(NT) for c in range(2)]
    o += [("knT", g) for g in range(H // 2)]
    o += [("vm", n) for n in range(NT)]
    o += [("gate", j) for j in range(12, 16)]
    o += [("qmT", n, c) for n in range(NT) for c in range(2)]
    o += [("S", h) for h in range(HEADS_AHEAD)]
    for h in range(2 * H):
        o += [("PT", h)]
        if h + HEADS_AHEAD < 2 * H:
            o += [("S", h + HEADS_AHEAD)]
        o += [("Y", h)]
    o += [("br", c) for c in range(KD)]
    o += [("mix", n, c) for n in range(NT) for c in range(2)]
    o += [("hT", n, c) for n in range(NT) for c in range(2)]
    for c in range(4):
        o += [("pq", 2 * c), ("pq", 2 * c + 1)] + [("sim", n, c) for n in range(NT)]
    o += [("slotT", w) for w in range(3)]
    return o


def memory(nc):
    m = {}
    base = -(-nc.sbuf_base // 32) * 32

    def put(name, shape, off, dt=F32):
        size = int(np.prod(shape[1:])) * (2 if dt == BF16 else 4)
        m[name] = nc.alloc_sbuf_tensor_at(name, shape, dt, offset=base + off)
        return off + -(-size // 32) * 32

    o = put("xT", [P, KD, T], 0)
    o = put("ring", [P, 3, KD, CHUNK], o)
    o = put("tok", [P, NT, TOK], o)
    o = put("sigT", [P, 2, KD, T], o)
    o = put("qT", [P, W // P, T], o)
    o = put("kT", [P, W // P, T], o)
    o = put("cqT", [P, QLORA // P, T], o)
    o = put("ckvT", [P, KVLORA // P, T], o)
    o = put("qmT", [P, H, T], o)
    o = put("kmT", [P, H, T], o)
    o = put("vm", [P, NT, W], o)
    o = put("w_q_up", [P, QLORA // P, H * DQK], o)
    o = put("w_kv_up", [P, KVLORA // P, H * 2 * DH], o)
    o = put("w_br", [P, 2, W // P, D], o)
    o = put("probs", [P, HEADS_AHEAD, NT, T], o)
    o = put("probsT", [P, HEADS_AHEAD, 3, P], o)
    assert o <= 196 * KB, o
    m["qm"] = m["tok"]
    put("yT", [P, 2, W // P, T], 0)
    put("mergedT", [P, KD, T], (8 + 48) * KB + 2 * TOK * 4 + 16 * KB)
    put("w_out", [P, KD, D], 8 * KB)
    put("x_tok", [P, NT, D], 40 * KB)
    put("ln1", [P, 2, D], 48 * KB)
    put("h", [P, NT, D], 196 * KB)
    o = put("consts", [P, C_COLS], 204 * KB)
    o = put("cols", [P, B_COLS], o)
    o = put("small", [P, 160], o)
    assert base + o <= nc.sbuf_usable_end, o

    put("G", [P, NK, T], 0)
    o = put("hT", [P, KD, T], 0)
    o = put("ring2", [P, 3, KD, CHUNK], o)
    o = put("subk", [P, HP, NK], o)
    o = put("pqT", [P, HP, T], o)
    o = put("sims", [P, NT, HP, NK], o)
    o = put("sims2", [P, 4, NK], o)
    o = put("ahead_raw", [P, 2, KD, P], o)
    o = put("ahead_hi", [P, 2, KD, P], o, F32R)
    o = put("ahead_lo", [P, 2, KD, P], o, F32R)
    assert o <= 128 * KB, o
    put("ahead", [P, AHEAD, T], 128 * KB)
    o = put("cand", [P, 2, TK * TK], 152 * KB)
    o = put("cand2", [P, 2, TK * TK], o)
    o = put("eq", [P, 2, SLOTS // 4, TK], o)
    o = put("topv", [P, NT, HP, TK], o)
    o = put("topi", [P, NT, HP, TK], o, U32)
    o = put("topf", [P, NT, HP, TK], o)
    o = put("best", [P, NT, PH, TK], o)
    o = put("bpos", [P, NT, PH, TK], o, U32)
    o = put("bab", [P, 2, SLOTS // 4], o, U32)
    o = put("babf", [P, 2, SLOTS // 4], o)
    o = put("slot", [P, 3, NT, SLOTS], o)
    o = put("ex", [P, NT, PH, TK], o)
    o = put("pstat", [P, 2, NT, PH], o)
    assert o <= 176 * KB, o
    assert AHEAD <= 20
    o = put("slotT", [P, 3, T], 148 * KB)
    o = put("keys", [P, 2, T], o, BF16)
    o = put("iota_t", [P, NK, OHT], o, BF16)
    o = put("oh1_plain", [P, 2, NK, OHT], o, BF16)
    o = put("oh2_plain", [P, NK, OHT], o, BF16)
    o = put("oh1", [P, 2, OHT, NK], o)
    o = put("oh2", [P, 2, OHT, NK], o)
    assert o <= 176 * KB, o
    o = put("u_raw", [P, 2, KD, P], 128 * KB)
    o = put("u_hi", [P, 2, KD, P], o, F32R)
    o = put("u_lo", [P, 2, KD, P], o, F32R)
    o = put("v_raw", [P, 2, D], o)
    o = put("v_hi", [P, 2, D], o, F32R)
    o = put("v_lo", [P, 2, D], o, F32R)
    o = put("h_hi", [P, KD, T], o, F32R)
    o = put("h_lo", [P, KD, T], o, F32R)
    o = put("w_hi", [P, 2, T], o, F32R)
    o = put("w_lo", [P, 2, T], o, F32R)
    assert o <= 196 * KB, o
    o = put("w_ple_gate", [P, KD, D], 0)
    o = put("w_ple_proj", [P, PLE // P, D], o)
    o = put("pT", [P, PLE // P, T], o)
    o = put("rows", [P, 3, D], o)
    o = put("r", [P, NT, D], o)
    o = put("rT", [P, KD, T], o)
    o = put("ple", [P, NT, D], o)
    o = put("ple2", [P, NT, D], o)
    o = put("y_out", [P, NT, D], o)
    assert o <= 120 * KB, o
    return m


def rope(nc, dve, steps, src, dst, tmp, table, heads, rot, last):
    half = rot // 2
    cos = table[:, 0:rot].unsqueeze(1).to_broadcast([P, heads, rot])
    sin = table[:, rot:2 * rot].unsqueeze(1).to_broadcast([P, heads, rot])
    a, b = tmp
    steps.done(nc.vector.tensor_tensor(a, src, cos, ALU.mult))
    steps.done(nc.vector.tensor_tensor(b[:, :, 0:half], src[:, :, half:rot], sin[:, :, 0:half], ALU.mult))
    steps.done(nc.vector.tensor_tensor(b[:, :, half:rot], src[:, :, 0:half], sin[:, :, half:rot], ALU.mult))
    steps.wait(dve)
    last.done(nc.vector.tensor_tensor(dst, a, b, ALU.add))
    last.wait(dve)


def layer_norm(nc, dve, steps, st, z, out, gain, shift, var_ok, std_ok, n, last):
    zz = z.rearrange("p (c f) -> p c f", f=512)
    for c in range(D // 512):
        steps.done(nc.vector.bn_stats(st[:, 6 * c:6 * c + 6], zz[:, c, :]))
    steps.wait(dve)
    steps.done(nc.vector.bn_aggr(st[:, 12:14], st[:, 0:12]))
    steps.wait(dve)
    nc.vector.tensor_scalar(st[:, 14:15], st[:, 13:14], LN_EPS, None, ALU.add).then_inc(var_ok, 1)
    dve.wait_ge(std_ok, n + 1)
    steps.done(nc.vector.reciprocal(st[:, 16:17], st[:, 15:16]))
    steps.wait(dve)
    steps.done(nc.vector.tensor_scalar(out, z, st[:, 12:13], st[:, 16:17], ALU.subtract, ALU.mult))
    steps.wait(dve)
    steps.done(nc.vector.tensor_tensor(out, out, gain, ALU.mult))
    steps.wait(dve)
    last.done(nc.vector.tensor_tensor(out, out, shift, ALU.add))
    last.wait(dve)


QUP = ((0, 5 * DQK), (5 * DQK, H * DQK))
W_STARTS = [Q0, K0, V0, CQ0, CKV0] + [TOK + CHUNK * j for j in range(2 * D // CHUNK)]
W_WIDTHS = [CHUNK] * 4 + [TOK - CKV0] + [CHUNK] * (2 * D // CHUNK)
TOK_CHUNKS = 5


def front(nc, io, m, bank):
    ident = m["consts"][:, C_ID:C_ID + P]
    tok, ring, small = m["tok"], m["ring"], m["small"]
    n_chunks = len(W_STARTS)
    scales = [DH ** -0.5] * H + [DQK ** -0.5] * H
    ss, rs = small[:, 0:4], small[:, 4:8]
    mx, nmx = small[:, 8:40], small[:, 40:72]
    den, rden = small[:, 72:104], small[:, 104:136]
    st = small[:, 136:160]

    with ExitStack() as ctx:
        def sem(name):
            return ctx.enter_context(nc.semaphore(name))

        x_in, c_in, b_in = sem("x_in"), sem("consts_in"), sem("cols_in")
        w_in_sem = [sem(f"w_in_slot{k}") for k in range(3)]
        wq_in, wkv_in, wb_in = sem("w_q_up_in"), sem("w_kv_up_in"), sem("w_branch_in")
        wo_in, xt_in, ln_in = sem("w_out_in"), sem("x_rows_in"), sem("ln1_in")
        ss_ready, root_ready, ms_ready = sem("squares_summed"), sem("root_ready"), sem("mean_square_ready")
        exped = sem("exp_done")
        var_ok, std_ok = sem("var_ready"), sem("std_ready")
        dv = Steps(ctx, nc, "front_dve")
        qk_roped = Steps(ctx, nc, "qk_roped")
        lora_ready = Steps(ctx, nc, "lora_ready")
        qm_roped = Steps(ctx, nc, "qm_roped")
        nmax = Steps(ctx, nc, "neg_max_ready")
        probs_ok = Steps(ctx, nc, "probs_ready")
        merged_ok = Steps(ctx, nc, "merged_ready")
        h_ok = Steps(ctx, nc, "h_ready")
        block = ctx.enter_context(nc.Block())

        @block.sync
        def _(sp):
            sp.dma_start(m["xT"][:], io["xT"].rearrange("(k p) t -> p k t", p=P)).then_inc(x_in, 16)
            w_in = io["w_in"].rearrange("(k p) c -> p k c", p=P)
            for c in range(n_chunks):
                if c >= 3:
                    used = c - 3
                    bank.read(sp, ("tok", used, NT - 1) if used < TOK_CHUNKS else ("gate", 4 * (used - TOK_CHUNKS) + 3))
                a, w = W_STARTS[c], W_WIDTHS[c]
                sp.dma_start(ring[:, c % 3, :, 0:w], w_in[:, :, a:a + w]).then_inc(w_in_sem[c % 3], 16)
                if c == 0:
                    sp.dma_start(m["consts"][:], io["consts"]).then_inc(c_in, 16)
                    sp.dma_start(m["cols"][:], io["cols"]).then_inc(b_in, 16)
                if c == 5:
                    sp.dma_start(m["w_q_up"][:], io["w_q_up"].rearrange("(k p) c -> p k c", p=P)).then_inc(wq_in, 16)
                    sp.dma_start(m["w_kv_up"][:], io["w_kv_up"].rearrange("(k p) c -> p k c", p=P)).then_inc(wkv_in, 16)
            for b, w in enumerate(("w_branch_moba", "w_branch_mla")):
                sp.dma_start(m["w_br"][:, b], io[w].rearrange("(k p) c -> p k c", p=P)).then_inc(wb_in, 16)
            for j in (7, 11, 15):
                bank.read(sp, ("gate", j))
            sp.dma_start(m["w_out"][:], io["w_out"].rearrange("(k p) c -> p k c", p=P)).then_inc(wo_in, 16)
            sp.dma_start(m["x_tok"][:], io["x"].rearrange("(n p) d -> p n d", p=P)).then_inc(xt_in, 16)
            sp.dma_start(m["ln1"][:, 0, :], io["ln1_g"].partition_broadcast(P)).then_inc(ln_in, 16)
            sp.dma_start(m["ln1"][:, 1, :], io["ln1_b"].partition_broadcast(P)).then_inc(ln_in, 16)

        @block.tensor
        def _(pe):
            def gate(j):
                c = TOK_CHUNKS + j // 4
                if j % 4 == 0:
                    pe.wait_ge(w_in_sem[c % 3], 16 * (c // 3 + 1))
                ps = bank.fill(pe, ("gate", j))
                for k in range(KD):
                    last = nc.tensor.matmul(ps[:, 0:T], ring[:, c % 3, k, (j % 4) * P:(j % 4 + 1) * P],
                                            m["xT"][:, k, :], start=(k == 0), stop=(k == KD - 1))
                bank.filled(("gate", j), last)

            def turn(name, blocks, width=P):
                ps = bank.fill(pe, name)
                for i, b in enumerate(blocks):
                    last = nc.tensor.transpose(ps[0:width, i * P:(i + 1) * P], b, ident)
                bank.filled(name, last)

            pe.wait_ge(x_in, 16)
            for c in range(TOK_CHUNKS):
                pe.wait_ge(w_in_sem[c % 3], 16 * (c // 3 + 1))
                for n in range(NT):
                    ps = bank.fill(pe, ("tok", c, n))
                    for k in range(KD):
                        last = nc.tensor.matmul(ps[:, 0:W_WIDTHS[c]], m["xT"][:, k, n * P:(n + 1) * P],
                                                ring[:, c % 3, k, 0:W_WIDTHS[c]], start=(k == 0), stop=(k == KD - 1))
                    bank.filled(("tok", c, n), last)
            pe.wait_ge(c_in, 16)
            for j in range(4):
                gate(j)
            for which, base in (("qT", Q0), ("kT", K0)):
                for n in range(NT):
                    pe.wait_ge(qk_roped.sem, n + 1)
                    turn((which, n), [tok[:, n, base + i * P:base + (i + 1) * P] for i in range(W // P)])
            for j in range(4, 8):
                gate(j)
            for n in range(NT):
                pe.wait_ge(lora_ready.sem, n + 1)
                turn(("cqT", n), [tok[:, n, CQ0 + i * P:CQ0 + (i + 1) * P] for i in range(QLORA // P)])
            for n in range(NT):
                turn(("ckvT", n), [tok[:, n, CKV0 + i * P:CKV0 + (i + 1) * P] for i in range(KVLORA // P)])
            turn(("krT",), [tok[:, n, KR0:KR0 + ROPE] for n in range(NT)], ROPE)
            for j in range(8, 12):
                gate(j)
            pe.wait_ge(wq_in, 16)
            for n in range(NT):
                bank.await_drained(pe, ("cqT", n))
                for c, (a, b) in enumerate(QUP):
                    ps = bank.fill(pe, ("qup", n, c))
                    for k in range(QLORA // P):
                        last = nc.tensor.matmul(ps[:, 0:b - a], m["cqT"][:, k, n * P:(n + 1) * P],
                                                m["w_q_up"][:, k, a:b], start=(k == 0), stop=(k == QLORA // P - 1))
                    bank.filled(("qup", n, c), last)
            pe.wait_ge(wkv_in, 16)
            for n in range(NT):
                bank.await_drained(pe, ("ckvT", n))
            KK = KVLORA // P
            for g in range(H // 2):
                ps = bank.fill(pe, ("knT", g))
                for e in range(2):
                    col = (2 * g + e) * 2 * DH
                    for k in range(KK):
                        last = nc.tensor.matmul(ps[0:DH, e * T:(e + 1) * T], m["w_kv_up"][:, k, col:col + DH],
                                                m["ckvT"][:, k, :], start=(k == 0), stop=(k == KK - 1))
                bank.filled(("knT", g), last)
            v_cols = m["w_kv_up"][:].rearrange("p k (h e d) -> p k h e d", h=H, e=2)
            for n in range(NT):
                ps = bank.fill(pe, ("vm", n))
                for k in range(KK):
                    last = nc.tensor.matmul(ps[:, 0:W].rearrange("p (h d) -> p h d", h=H),
                                            m["ckvT"][:, k, n * P:(n + 1) * P], v_cols[:, k, :, 1, :],
                                            start=(k == 0), stop=(k == KK - 1))
                bank.filled(("vm", n), last)
            for j in range(12, 16):
                gate(j)
            for n in range(NT):
                pe.wait_ge(qm_roped.sem, n + 1)
                for c in range(2):
                    turn(("qmT", n, c), [m["qm"][:, n, (4 * c + i) * DQK:(4 * c + i + 1) * DQK] for i in range(4)], DQK)

            def operands(h):
                if h < H:
                    r = slice(DH * (h % 2), DH * (h % 2) + DH)
                    return m["qT"][r, h // 2, :], m["kT"][r, h // 2, :]
                return m["qmT"][0:DQK, h - H, :], m["kmT"][0:DQK, h - H, :]

            def scores(h):
                if h == 0:
                    for n in range(NT):
                        bank.await_drained(pe, ("qT", n))
                        bank.await_drained(pe, ("kT", n))
                if h == H:
                    bank.await_drained(pe, ("krT",))
                    for g in range(H // 2):
                        bank.await_drained(pe, ("knT", g))
                    for n in range(NT):
                        bank.await_drained(pe, ("vm", n))
                        for c in range(2):
                            bank.await_drained(pe, ("qmT", n, c))
                q, k = operands(h)
                ps = bank.fill(pe, ("S", h))
                nc.tensor.matmul(ps[:, 0:P], q[:, 0:P], k[:, 0:P], start=True, stop=True)
                bank.filled(("S", h), nc.tensor.matmul(ps[:, P:P + T], q[:, P:T], k[:, :], start=True, stop=True))

            def values(h):
                bank.await_drained(pe, ("PT", h))
                v = (lambda n: tok[:, n, V0 + h * DH:V0 + (h + 1) * DH]) if h < H else \
                    (lambda n: m["vm"][:, n, (h - H) * DH:(h - H + 1) * DH])
                pT = m["probsT"][:, h % HEADS_AHEAD]
                ps = bank.fill(pe, ("Y", h))
                nc.tensor.matmul(ps[0:DH, 0:P], v(0), pT[:, 0, :], start=True, stop=True)
                nc.tensor.matmul(ps[0:DH, P:T], v(0), pT[:, 1, :], start=True, stop=False)
                last = nc.tensor.matmul(ps[0:DH, P:T], v(1), pT[:, 2, :], start=False, stop=True)
                bank.filled(("Y", h), last)

            for h in range(HEADS_AHEAD):
                scores(h)
            for h in range(2 * H):
                pe.wait_ge(probs_ok.sem, h + 1)
                pr = m["probs"][:, h % HEADS_AHEAD]
                turn(("PT", h), [pr[:, 0, 0:P], pr[:, 1, 0:P], pr[:, 1, P:T]])
                if h + HEADS_AHEAD < 2 * H:
                    scores(h + HEADS_AHEAD)
                values(h)
            pe.wait_ge(wb_in, 32)
            for h in range(2 * H):
                bank.await_drained(pe, ("Y", h))
            for c in range(KD):
                ps = bank.fill(pe, ("br", c))
                for b in range(2):
                    for k in range(W // P):
                        last = nc.tensor.matmul(ps[:, b * T:(b + 1) * T], m["w_br"][:, b, k, c * P:(c + 1) * P],
                                                m["yT"][:, b, k, :], start=(k == 0), stop=(k == W // P - 1))
                bank.filled(("br", c), last)
            pe.wait_ge(merged_ok.sem, KD)
            pe.wait_ge(wo_in, 16)
            for n in range(NT):
                for c in range(2):
                    ps = bank.fill(pe, ("mix", n, c))
                    for k in range(KD):
                        last = nc.tensor.matmul(ps[:, :], m["mergedT"][:, k, n * P:(n + 1) * P],
                                                m["w_out"][:, k, c * 512:(c + 1) * 512],
                                                start=(k == 0), stop=(k == KD - 1))
                    bank.filled(("mix", n, c), last)

        @block.scalar
        def _(act):
            def copy_out(name, dst, src):
                bank.drain(name, nc.scalar.activation(dst, src(bank.read(act, name)), ACT.Copy))

            for c in range(TOK_CHUNKS):
                a, w = W_STARTS[c], W_WIDTHS[c]
                for n in range(NT):
                    copy_out(("tok", c, n), tok[:, n, a:a + w], lambda ps: ps[:, 0:w])
            squares = [m["probs"][:, 0].rearrange("p a b -> p (a b)"), m["probs"][:, 1].rearrange("p a b -> p (a b)")]
            for n in range(NT):
                bank.await_drained(act, ("tok", 3, n))
                bank.await_drained(act, ("tok", 4, n))
                if n:
                    act.wait_ge(ss_ready, 2 * n)
                nc.scalar.activation(squares[0][:, 0:QLORA], tok[:, n, CQ0:CQ0 + QLORA],
                                     ACT.Square, accum_out=ss[:, n:n + 1]).then_inc(ss_ready, 1)
                nc.scalar.activation(squares[1][:, 0:KVLORA], tok[:, n, CKV0:CKV0 + KVLORA],
                                     ACT.Square, accum_out=ss[:, NT + n:NT + n + 1]).then_inc(ss_ready, 1)
            act.wait_ge(ms_ready, 1)
            nc.scalar.activation(rs, ss, ACT.Sqrt).then_inc(root_ready, 1)
            act.wait_ge(b_in, 16)

            def gate(j):
                ps = bank.read(act, ("gate", j))
                bank.drain(("gate", j), nc.scalar.activation(m["sigT"][:, j // KD, j % KD, :], ps[:, 0:T], ACT.Sigmoid,
                                                             bias=m["cols"][:, B_GATE + j:B_GATE + j + 1]))

            for j in range(8):
                gate(j)
            copy_out(("krT",), m["kmT"][DH:DQK, :, :], lambda ps: ps[0:ROPE, 0:T].unsqueeze(1).to_broadcast([ROPE, H, T]))
            for j in range(8, 12):
                gate(j)
            for n in range(NT):
                bank.read(act, ("qT", n))
                bank.read(act, ("kT", n))
            for n in range(NT):
                for c, (a, b) in enumerate(QUP):
                    copy_out(("qup", n, c), m["qm"][:, n, a:b], lambda ps: ps[:, 0:b - a])
            for g in range(H // 2):
                copy_out(("knT", g), m["kmT"][0:DH, 2 * g:2 * g + 2, :],
                         lambda ps: ps[0:DH, :].rearrange("p (e t) -> p e t", e=2))
            for n in range(NT):
                copy_out(("vm", n), m["vm"][:, n, :], lambda ps: ps[:, 0:W])
            for j in range(12, 16):
                gate(j)
            for n in range(NT):
                for c in range(2):
                    copy_out(("qmT", n, c), m["qmT"][0:DQK, 4 * c:4 * c + 4, n * P:(n + 1) * P],
                             lambda ps: ps[0:DQK, :].rearrange("p (h t) -> p h t", h=4))

            def expo(h):
                act.wait_ge(nmax.sem, h + 1)
                for n in range(NT):
                    w = (n + 1) * P
                    pr = m["probs"][:, h % HEADS_AHEAD, n, 0:w]
                    last = nc.scalar.activation(pr, pr, ACT.Exp, bias=nmx[:, 2 * h + n:2 * h + n + 1],
                                                accum_out=den[:, 2 * h + n:2 * h + n + 1])
                last.then_inc(exped, 1)

            expo(0)
            expo(1)
            for h in range(2 * H):
                if h + 2 < 2 * H:
                    expo(h + 2)
                if h >= HEADS_AHEAD:
                    bank.read(act, ("Y", h - HEADS_AHEAD))
                copy_out(("PT", h), m["probsT"][:, h % HEADS_AHEAD].rearrange("p a b -> p (a b)"), lambda ps: ps[:, 0:3 * P])
            for n in range(NT):
                act.wait_ge(var_ok, n + 1)
                nc.scalar.activation(st[:, 15:16], st[:, 14:15], ACT.Sqrt).then_inc(std_ok, 1)

        @block.vector
        def _(dve):
            dve.wait_ge(c_in, 16)
            idle = m["probsT"][:].rearrange("p a b c -> p (a b c)")
            tmp = (idle[:, 0:T], idle[:, T:2 * T])

            def table(n, rot):
                o = C_ROPE + n * ROPE_W + (0 if rot == ROT else 2 * ROT)
                return m["consts"][:, o:o + 2 * rot]

            def temps(heads, rot):
                return [x[:, 0:heads * rot].rearrange("p (h d) -> p h d", d=rot) for x in tmp]

            for n in range(NT):
                bank.await_drained(dve, ("tok", 0, n))
                bank.await_drained(dve, ("tok", 1, n))
                qk = tok[:, n, 0:2 * W].rearrange("p (h d) -> p h d", d=DH)[:, :, 0:ROT]
                rope(nc, dve, dv, qk, qk, temps(2 * H, ROT), table(n, ROT), 2 * H, ROT, qk_roped)
            dve.wait_ge(ss_ready, 2 * NT)
            dv.done(nc.vector.tensor_scalar(ss[:, 0:NT], ss[:, 0:NT], 1.0 / QLORA, RMS_EPS, ALU.mult, ALU.add))
            dv.wait(dve)
            nc.vector.tensor_scalar(ss[:, NT:2 * NT], ss[:, NT:2 * NT], 1.0 / KVLORA, RMS_EPS,
                                    ALU.mult, ALU.add).then_inc(ms_ready, 1)
            dve.wait_ge(root_ready, 1)
            dv.done(nc.vector.reciprocal(rs, rs))
            dv.wait(dve)
            for n in range(NT):
                for base, w, col in ((CQ0, QLORA, n), (CKV0, KVLORA, NT + n)):
                    dv.done(nc.vector.tensor_scalar(tok[:, n, base:base + w], tok[:, n, base:base + w],
                                                    rs[:, col:col + 1], None, ALU.mult))
                kr = tok[:, n, KR0:KR0 + ROPE].unsqueeze(1)
                rope(nc, dve, dv, kr, kr, temps(1, ROPE), table(n, ROPE), 1, ROPE, lora_ready)
            for which in ("qT", "kT"):
                for n in range(NT):
                    ps = bank.read(dve, (which, n))
                    bank.drain((which, n), nc.vector.tensor_copy(m[which][:, :, n * P:(n + 1) * P],
                                                                 ps[:, :].rearrange("p (k t) -> p k t", t=P)))
            dve.wait_ge(b_in, 16)
            for which, K, col in (("cqT", QLORA // P, B_QN), ("ckvT", KVLORA // P, B_KVN)):
                for n in range(NT):
                    ps = bank.read(dve, (which, n))
                    gain = m["cols"][:, col:col + K].unsqueeze(2).to_broadcast([P, K, P])
                    bank.drain((which, n), nc.vector.tensor_tensor(
                        m[which][:, :, n * P:(n + 1) * P],
                        ps[:, 0:K * P].rearrange("p (k t) -> p k t", t=P), gain, ALU.mult))
            for n in range(NT):
                bank.await_drained(dve, ("qup", n, 0))
                bank.await_drained(dve, ("qup", n, 1))
                qr = m["qm"][:, n, 0:H * DQK].rearrange("p (h d) -> p h d", d=DQK)[:, :, DH:DQK]
                rope(nc, dve, dv, qr, qr, temps(H, ROPE), table(n, ROPE), H, ROPE, qm_roped)

            def mask_max(h):
                ps = bank.read(dve, ("S", h))
                if h >= HEADS_AHEAD:
                    bank.read(dve, ("PT", h - HEADS_AHEAD))
                for n in range(NT):
                    w = (n + 1) * P
                    mask = m["consts"][:, C_MASK + (NT - 1 - n) * P:C_MASK + T]
                    c = 2 * h + n
                    last = nc.vector.tensor_tensor_reduce(
                        out=m["probs"][:, h % HEADS_AHEAD, n, 0:w], in0=ps[:, n * P:n * P + w], in1=mask, scale=scales[h],
                        scalar=LOWEST, op0=ALU.add, op1=ALU.max, accum_out=mx[:, c:c + 1])
                bank.drain(("S", h), last)
                bank.await_drained(dve, ("S", h))
                nmax.done(nc.vector.tensor_scalar(nmx[:, 2 * h:2 * h + 2], mx[:, 2 * h:2 * h + 2], -1.0, None, ALU.mult))

            def normalise(h):
                dve.wait_ge(exped, h + 1)
                dv.done(nc.vector.reciprocal(rden[:, 2 * h:2 * h + 2], den[:, 2 * h:2 * h + 2]))
                dv.wait(dve)
                for n in range(NT):
                    pr = m["probs"][:, h % HEADS_AHEAD, n, 0:(n + 1) * P]
                    last = nc.vector.tensor_scalar(pr, pr, rden[:, 2 * h + n:2 * h + n + 1], None, ALU.mult)
                probs_ok.done(last)

            def keep_y(h):
                ps = bank.read(dve, ("Y", h))
                r = slice(DH * (h % 2), DH * (h % 2) + DH)
                bank.drain(("Y", h), nc.vector.tensor_copy(m["yT"][r, h // H, h % H // 2, :], ps[0:DH, 0:T]))

            for h in range(HEADS_AHEAD):
                mask_max(h)
            for h in range(2 * H):
                normalise(h)
                if h >= 1:
                    keep_y(h - 1)
                if h + HEADS_AHEAD < 2 * H:
                    mask_max(h + HEADS_AHEAD)
            keep_y(2 * H - 1)
            for j in range(2 * KD):
                bank.await_drained(dve, ("gate", j))
            for c in range(KD):
                ps = bank.read(dve, ("br", c))
                t = m["probs"][:, c % 2]
                bank.drain(("br", c), nc.vector.tensor_tensor(t, ps[:, :].rearrange("p (b t) -> p b t", b=2),
                                                              m["sigT"][:, :, c, :], ALU.mult))
                bank.await_drained(dve, ("br", c))
                merged_ok.done(nc.vector.tensor_tensor(m["mergedT"][:, c, :], t[:, 0, :], t[:, 1, :], ALU.add))
            dve.wait_ge(xt_in, 16)
            dve.wait_ge(ln_in, 32)
            for n in range(NT):
                z = m["x_tok"][:, n, :]
                for c in range(2):
                    ps = bank.read(dve, ("mix", n, c))
                    zc = z[:, c * 512:(c + 1) * 512]
                    bank.drain(("mix", n, c), nc.vector.scalar_tensor_tensor(
                        out=zc, in0=zc, scalar=ALPHA, in1=ps[:, :], op0=ALU.mult, op1=ALU.add))
                for c in range(2):
                    bank.await_drained(dve, ("mix", n, c))
                layer_norm(nc, dve, dv, st, z, m["h"][:, n, :], m["ln1"][:, 0, :], m["ln1"][:, 1, :],
                           var_ok, std_ok, n, h_ok)


def split_product(nc, out, w_hi, w_lo, x_hi, x_lo):
    for k in range(KD):
        nc.tensor.matmul(out, w_hi[:, k, :], x_hi[:, k, :], start=(k == 0), stop=False)
        nc.tensor.matmul(out, w_hi[:, k, :], x_lo[:, k, :], start=False, stop=False)
        last = nc.tensor.matmul(out, w_lo[:, k, :], x_hi[:, k, :], start=False, stop=(k == KD - 1))
    return last


def route(nc, io, m, bank):
    consts = m["consts"]
    ident, iota = consts[:, C_ID:C_ID + P], consts[:, C_IOTA:C_IOTA + NK]
    iota16 = consts[:, C_IOTA:C_IOTA + TK]
    GT = 4
    RINGS = 2
    BODY = RINGS * OHT
    BANKS = BODY // GT

    with ExitStack() as ctx:
        def sem(name):
            return ctx.enter_context(nc.semaphore(name))

        wq_in = [sem(f"peer_wq_slot{k}") for k in range(3)]
        subk_in, split_ok = sem("sub_keys_in"), sem("h_split")
        exp_ok = sem("gate_exp_ready")
        a_in = [sem(f"ahead_slot{k}") for k in range(2)]
        a_hi_ok, a_ok = sem("ahead_hi_ready"), sem("ahead_split")
        a_done, a_gelu = sem("ahead_uh_done"), sem("ahead_gelu")
        lo_ok = sem("h_lo_ready")
        oh1_ok = sem("onehot1_ready")
        oh_ready = sem("onehot_ready")
        g_full = sem("g_bank_full")
        g_free = sem("g_bank_free")
        dv = Steps(ctx, nc, "route_dve")
        plain1_ok, plain2_ok = sem("onehot1_plain"), sem("onehot2_plain")
        exp_in = Steps(ctx, nc, "gate_exp_in")
        slot_ok = Steps(ctx, nc, "slots_ready")
        block = ctx.enter_context(nc.Block())

        @block.sync
        def _(sp):
            w_q = io["peer_w_q"].rearrange("(k p) c -> p k c", p=P)
            for c in range(4):
                if c >= 3:
                    bank.read(sp, ("pq", 2 * (c - 3) + 1))
                sp.dma_start(m["ring2"][:, c % 3], w_q[:, :, c * CHUNK:(c + 1) * CHUNK]).then_inc(wq_in[c % 3], 16)
                if c == 0:
                    sp.dma_start(m["subk"][:], io["subkT"].rearrange("h d n -> d h n")).then_inc(subk_in, 16)

            def load(b, s):
                sp.wait_ge(a_ok, b + 1)
                sp.dma_start(m["ahead_raw"][:, s % 2], io["uT"][bass.ds(b, 1)].rearrange("o p k e -> (o p) k e")
                             ).then_inc(a_in[s % 2], 16)

            over(sp, 0, AHEAD, load)

        @block.gpsimd
        def _(pool):
            def split_lo(b, s):
                pool.wait_ge(a_hi_ok, b + 1)
                pool.wait_ge(a_done, b + 1)
                nc.gpsimd.tensor_tensor(m["ahead_lo"][:, s % 2], m["ahead_raw"][:, s % 2],
                                        m["ahead_hi"][:, s % 2].bitcast(F32), ALU.subtract).then_inc(a_ok, 1)

            over(pool, 0, AHEAD, split_lo)

        @block.tensor
        def _(pe):
            for n in range(NT):
                for c in range(2):
                    ps = bank.fill(pe, ("hT", n, c))
                    for i in range(4):
                        k = 4 * c + i
                        last = nc.tensor.transpose(ps[:, i * P:(i + 1) * P], m["h"][:, n, k * P:(k + 1) * P], ident)
                    bank.filled(("hT", n, c), last)
            for n in range(NT):
                for c in range(2):
                    bank.await_drained(pe, ("hT", n, c))
            for c in range(4):
                pe.wait_ge(wq_in[c % 3], 16 * (c // 3 + 1))
                for g in (2 * c, 2 * c + 1):
                    ps = bank.fill(pe, ("pq", g))
                    for e in range(2):
                        col = (2 * (g % 2) + e) * DKH
                        for k in range(KD):
                            last = nc.tensor.matmul(ps[:, e * T:(e + 1) * T], m["ring2"][:, c % 3, k, col:col + DKH],
                                                    m["hT"][:, k, :], start=(k == 0), stop=(k == KD - 1))
                    bank.filled(("pq", g), last)
                if c == 0:
                    pe.wait_ge(subk_in, 16)
                for g in (2 * c, 2 * c + 1):
                    bank.await_drained(pe, ("pq", g))
                for n in range(NT):
                    ps = bank.fill(pe, ("sim", n, c))
                    for i in range(4):
                        hp = 4 * c + i
                        last = nc.tensor.matmul(ps[:, i * NK:(i + 1) * NK], m["pqT"][:, hp, n * P:(n + 1) * P],
                                                m["subk"][:, hp, :], start=True, stop=True)
                    bank.filled(("sim", n, c), last)
            for c in (2, 3):
                for name in (("pq", 2 * c), ("pq", 2 * c + 1), ("sim", 0, c), ("sim", 1, c)):
                    bank.await_drained(pe, name)
            pe.wait_ge(split_ok, 1)
            pe.wait_ge(lo_ok, 1)

            def activations(b, s):
                pe.wait_ge(a_ok, b + 3)
                pe.wait_ge(a_gelu, b + 1)
                split_product(nc, bank.psum[s % 2][:, 0:T], m["ahead_hi"][:, s % 2], m["ahead_lo"][:, s % 2],
                              m["h_hi"], m["h_lo"]).then_inc(a_done, 1)

            over(pe, 0, AHEAD, activations)
            pe.wait_ge(a_gelu, AHEAD + 2)
            pe.wait_ge(slot_ok.sem, 1)
            for w in range(3):
                ps = bank.fill(pe, ("slotT", w))
                for n in range(NT):
                    last = nc.tensor.transpose(ps[:, n * P:(n + 1) * P], m["slot"][:, w, n, :], ident)
                bank.filled(("slotT", w), last)
            for w in range(3):
                bank.await_drained(pe, ("slotT", w))
            with pe.Fori(0, T // BODY) as i:
                for g in range(BANKS):
                    pe.wait_ge(g_free, i * BANKS + g + 1)
                    slot, t0 = g * GT // OHT, g * GT % OHT
                    if t0 == 0:
                        pe.wait_ge(oh1_ok, i * RINGS + RINGS + slot + 1)
                        pe.wait_ge(oh_ready, i * RINGS + slot + 2)
                    for j in range(GT):
                        last = nc.tensor.matmul(bank.psum[g][:, j * NK:(j + 1) * NK], m["oh2"][:, slot, t0 + j, :],
                                                m["oh1"][:, slot, t0 + j, :], start=True, stop=True)
                    last.then_inc(g_full, 1)

        @block.scalar
        def _(act):
            for n in range(NT):
                for c in range(2):
                    ps = bank.read(act, ("hT", n, c))
                    bank.drain(("hT", n, c), nc.scalar.activation(
                        m["hT"][:, 4 * c:4 * c + 4, n * P:(n + 1) * P],
                        ps[:, :].rearrange("p (k t) -> p k t", t=P), ACT.Copy))
            for n in range(NT):
                for c in range(2):
                    bank.await_drained(act, ("hT", n, c))
            nc.scalar.activation(m["h_hi"][:], m["hT"][:], ACT.Copy).then_inc(split_ok, 1)
            for c in range(4):
                for g in (2 * c, 2 * c + 1):
                    ps = bank.read(act, ("pq", g))
                    bank.drain(("pq", g), nc.scalar.activation(
                        m["pqT"][:, 2 * g:2 * g + 2, :], ps[:, :].rearrange("p (e t) -> p e t", e=2), ACT.Copy))
                for n in range(NT):
                    ps = bank.read(act, ("sim", n, c))
                    bank.drain(("sim", n, c), nc.scalar.activation(
                        m["sims"][:, n, 4 * c:4 * c + 4, :], ps[:, :].rearrange("p (i k) -> p i k", k=NK), ACT.Copy))
            act.sem_inc(a_ok, 2)
            act.sem_inc(a_done, 2)
            act.sem_inc(a_gelu, 2)

            def split_hi(b, s):
                act.wait_ge(a_in[s % 2], 16 * (b // 2 + 1) if isinstance(b, int) else b * 8 + (16 - 8 * (s % 2)))
                act.wait_ge(a_done, b + 1)
                nc.scalar.activation(m["ahead_hi"][:, s % 2], m["ahead_raw"][:, s % 2], ACT.Copy).then_inc(a_hi_ok, 1)

            def gelu(b, s):
                act.wait_ge(a_done, b + 3)
                nc.scalar.activation(m["ahead"][:, bass.ds(b, 1), :].rearrange("p o t -> p (o t)"),
                                     bank.psum[s % 2][:, 0:T], ACT.Gelu).then_inc(a_gelu, 1)

            split_hi(0, 0)
            over(act, 0, AHEAD - 1, lambda b, s: (split_hi(b + 1, s + 1), gelu(b, s)))
            gelu(AHEAD - 1, AHEAD - 1)
            act.wait_ge(exp_in.sem, 1)
            nc.scalar.activation(m["ex"][:], m["ex"][:], ACT.Exp).then_inc(exp_ok, 1)
            for w in range(3):
                bank.await_drained(act, ("slotT", w))
            act.sem_inc(g_free, BANKS)
            act.sem_inc(g_full, BANKS)
            act.sem_inc(oh1_ok, RINGS)
            act.sem_inc(oh_ready, 1)

            def widen(j, s):
                act.wait_ge(plain1_ok, j + 1)
                act.wait_ge(g_full, j * (OHT // GT) + OHT // GT)
                nc.scalar.activation(m["oh1"][:, s % RINGS], m["oh1_plain"][:, s % RINGS].rearrange("p k t -> p t k"),
                                     ACT.Copy).then_inc(oh1_ok, 1)

            def store(j, s):
                for g in range(OHT // GT):
                    act.wait_ge(g_full, j * (OHT // GT) + BANKS + g + 1)
                    nc.scalar.activation(m["G"][:, :, bass.ds(j * OHT + GT * g, GT)],
                                         bank.psum[(s % RINGS) * (OHT // GT) + g][:, :].rearrange("p (t i) -> p i t", t=GT),
                                         ACT.Copy).then_inc(g_free, 1)

            last = T // OHT - 1
            widen(0, 0)
            over(act, 0, last, lambda j, s: (widen(j + 1, s + 1), store(j, s)), unroll=RINGS)
            store(last, last)

        @block.vector
        def _(dve):
            def top16(rows):
                for src, _, vals, _ in rows:
                    dv.done(nc.vector.max(vals[:, 0:8], src))
                dv.wait(dve)
                for src, scratch, vals, idx in rows:
                    dv.done(nc.vector.max_index(idx[:, 0:8], vals[:, 0:8], src))
                    dv.done(nc.vector.match_replace(scratch, vals[:, 0:8], src, LOWEST))
                dv.wait(dve)
                for _, scratch, vals, _ in rows:
                    dv.done(nc.vector.max(vals[:, 8:16], scratch))
                dv.wait(dve)
                for _, scratch, vals, idx in rows:
                    dv.done(nc.vector.max_index(idx[:, 8:16], vals[:, 8:16], scratch))
                dv.wait(dve)

            dve.wait_ge(split_ok, 1)
            nc.vector.tensor_tensor(m["h_lo"][:], m["hT"][:], m["h_hi"][:].bitcast(F32), ALU.subtract).then_inc(lo_ok, 1)
            for c in range(4):
                for n in range(NT):
                    bank.await_drained(dve, ("sim", n, c))
                    tv, ti, tf = (m[x][:, n, 4 * c:4 * c + 4, :] for x in ("topv", "topi", "topf"))
                    best, bpos = (m[x][:, n, 2 * c:2 * c + 2, :] for x in ("best", "bpos"))
                    top16([(m["sims"][:, n, 4 * c + i, :], m["sims2"][:, i, :], tv[:, i, :], ti[:, i, :])
                           for i in range(4)])
                    dv.done(nc.vector.tensor_copy(tf, ti))
                    tv4 = tv.rearrange("p (h e) k -> p h e k", e=2)
                    dv.done(nc.vector.tensor_tensor(
                        m["cand"][:].rearrange("p h (a b) -> p h a b", a=TK),
                        tv4[:, :, 0, :].unsqueeze(3).to_broadcast([P, 2, TK, TK]),
                        tv4[:, :, 1, :].unsqueeze(2).to_broadcast([P, 2, TK, TK]), ALU.add))
                    dv.wait(dve)
                    top16([(m["cand"][:, i, :], m["cand2"][:, i, :], best[:, i, :], bpos[:, i, :]) for i in range(2)])
                    pos = bpos.rearrange("p h k -> p (h k)")
                    dv.done(nc.vector.tensor_scalar(m["bab"][:, 0, :], pos, 4, None, ALU.logical_shift_right))
                    dv.done(nc.vector.tensor_scalar(m["bab"][:, 1, :], pos, TK - 1, None, ALU.bitwise_and))
                    dv.wait(dve)
                    dv.done(nc.vector.tensor_copy(m["babf"][:], m["bab"][:]))
                    dv.wait(dve)
                    q = SLOTS // 4
                    tf4 = tf.rearrange("p (h e) k -> p h e k", e=2)
                    for e in range(2):
                        dv.done(nc.vector.tensor_tensor(
                            m["eq"][:, e], m["babf"][:, e, :].unsqueeze(2).to_broadcast([P, q, TK]),
                            iota16.unsqueeze(1).to_broadcast([P, q, TK]), ALU.is_equal))
                    dv.wait(dve)
                    for e in range(2):
                        eq4 = m["eq"][:, e].rearrange("p (h k) a -> p h k a", h=2)
                        dv.done(nc.vector.tensor_tensor(
                            eq4, eq4, tf4[:, :, e, :].unsqueeze(2).to_broadcast([P, 2, TK, TK]), ALU.mult))
                    dv.wait(dve)
                    for e in range(2):
                        dv.done(nc.vector.tensor_reduce(m["slot"][:, e, n, c * q:(c + 1) * q], m["eq"][:, e],
                                                        AX_X, ALU.add))
            heads = [P, NT * PH, TK]
            best, ex = (m[x][:].rearrange("p n h k -> p (n h) k") for x in ("best", "ex"))
            total, inverse = (m["pstat"][:, j].rearrange("p n h -> p (n h)") for j in range(2))
            exp_in.done(nc.vector.tensor_tensor(ex, best, best[:, :, 0:1].to_broadcast(heads), ALU.subtract))
            dve.wait_ge(exp_ok, 1)
            dv.done(nc.vector.tensor_reduce(total, ex, AX_X, ALU.add))
            dv.wait(dve)
            dv.done(nc.vector.reciprocal(inverse, total))
            dv.wait(dve)
            slot_ok.done(nc.vector.tensor_tensor(m["slot"][:, 2].rearrange("p n (h k) -> p (n h) k", h=PH), ex,
                                                 inverse.unsqueeze(2).to_broadcast(heads), ALU.mult))
            for w in range(3):
                ps = bank.read(dve, ("slotT", w))
                bank.drain(("slotT", w), nc.vector.tensor_copy(m["slotT"][:, w, :], ps[:, 0:T]))
            for w in range(3):
                bank.await_drained(dve, ("slotT", w))
            dv.done(nc.vector.tensor_copy(m["keys"][:], m["slotT"][:, 0:2, :]))
            dv.done(nc.vector.tensor_copy(m["iota_t"][:], iota.unsqueeze(2).to_broadcast([P, NK, OHT])))
            dv.wait(dve)
            rows = [P, NK, OHT]
            with dve.Fori(0, T // BODY) as i:
                for s in range(RINGS):
                    t = bass.ds(i * BODY + s * OHT, OHT)
                    dve.wait_ge(oh1_ok, i * RINGS + s + 1)
                    nc.vector.tensor_tensor(m["oh1_plain"][:, s], m["iota_t"][:],
                                            m["keys"][:, 0, t].unsqueeze(1).to_broadcast(rows),
                                            ALU.is_equal).then_inc(plain1_ok, 1)
                    dve.wait_ge(oh_ready, i * RINGS + s + 1)
                    nc.vector.tensor_tensor(m["oh2_plain"][:], m["iota_t"][:],
                                            m["keys"][:, 1, t].unsqueeze(1).to_broadcast(rows),
                                            ALU.is_equal).then_inc(plain2_ok, 1)
                    dve.wait_ge(plain2_ok, i * RINGS + s + 1)
                    dve.wait_ge(g_full, i * BANKS + (s + 1) * (OHT // GT))
                    nc.vector.tensor_tensor(m["oh2"][:, s], m["oh2_plain"][:].rearrange("p k t -> p t k"),
                                            m["slotT"][:, 2, t].unsqueeze(2).to_broadcast([P, OHT, NK]),
                                            ALU.mult).then_inc(oh_ready, 1)


def experts(nc, io, m, bank):
    acts = [bank.psum[b][:, 0:T] for b in range(4)]
    prods = [bank.psum[b][:, T:2 * T] for b in range(4)]
    out = [[bank.psum[4 + 2 * n + c] for c in range(2)] for n in range(NT)]
    BANKS = 4
    RING = 2
    RAW_OVER = RING * KD * P // T
    HI_OVER = 2 * RAW_OVER

    with ExitStack() as ctx:
        def sem(name):
            return ctx.enter_context(nc.semaphore(name))

        u_in = [sem(f"u_slot{k}") for k in range(RING)]
        v_in = [sem(f"v_slot{k}") for k in range(RING)]
        u_hi_ok, v_hi_ok = sem("u_hi_ready"), sem("v_hi_ready")
        u_ok, v_ok = sem("u_split"), sem("v_split")
        gelu_ok, prod_ok, w_hi_ok = sem("gelu_ready"), sem("gated_ready"), sem("w_hi_ready")
        w_ok = sem("w_split")
        uh_done, wv_done = sem("uh_done"), sem("wv_done")
        tail_in = sem("tail_weights_in")
        block = ctx.enter_context(nc.Block())

        def loads(b, s):
            return 16 * (b // 2 + 1) if isinstance(b, int) else b * 8 + (16 - 8 * (s % 2))

        @block.sync
        def _(sp):
            def load_v(b, s):
                sp.wait_ge(v_ok, b + 1)
                sp.dma_start(m["v_raw"][:, s % RING], io["v"][bass.ds(b, 1)].rearrange("o p d -> (o p) d")
                             ).then_inc(v_in[s % RING], 16)

            def load_u(b, s):
                sp.wait_ge(u_ok, b - AHEAD + 1)
                sp.dma_start(m["u_raw"][:, s % RING], io["uT"][bass.ds(b, 1)].rearrange("o p k e -> (o p) k e")
                             ).then_inc(u_in[s % RING], 16)

            def load(b, s):
                load_v(b, s)
                load_u(b + 1, s + 1)

            over(sp, 0, AHEAD - 1, load_v)
            sp.wait_ge(prod_ok, RAW_OVER)
            first, with_slices = AHEAD - 1, 75
            over(sp, first, with_slices, load)
            w_g = io["w_ple_gate"].rearrange("(k p) c -> p k c", p=P)
            with sp.Fori(0, KD) as i:
                for r in range(BANKS):
                    load(i * BANKS + (with_slices + r), with_slices + r)
                sp.dma_start(m["w_ple_gate"][:, bass.ds(i, 1), :], w_g[:, bass.ds(i, 1), :]).then_inc(tail_in, 16)
            sp.dma_start(m["w_ple_proj"][:], io["w_ple_proj"].rearrange("(k p) c -> p k c", p=P)).then_inc(tail_in, 16)
            sp.dma_start(m["pT"][:], io["pT"].rearrange("(k p) t -> p k t", p=P)).then_inc(tail_in, 16)
            over(sp, with_slices + KD * BANKS, NK - 1, load)
            for j, w in enumerate(("b_ple_gate", "ln2_g", "ln2_b")):
                sp.dma_start(m["rows"][:, j, :], io[w].partition_broadcast(P)).then_inc(tail_in, 16)
            load_v(NK - 1, NK - 1)
            sp.wait_ge(tail_in, 16 * (KD + 5))

        @block.tensor
        def _(pe):
            def activations(b, s):
                pe.wait_ge(u_ok, b - AHEAD + 1 + RING)
                pe.wait_ge(w_ok, b + 1)
                split_product(nc, acts[s % BANKS], m["u_hi"][:, s % RING], m["u_lo"][:, s % RING],
                              m["h_hi"], m["h_lo"]).then_inc(uh_done, 1)

            def values(b, s):
                pe.wait_ge(v_ok, b + 1 + RING)
                pe.wait_ge(w_ok, b + 1 + BANKS)
                first = isinstance(b, int) and b == 0
                v = s % RING
                for n in range(NT):
                    t = slice(n * P, (n + 1) * P)
                    for w, x, start in (("w_hi", "v_hi", first), ("w_hi", "v_lo", False), ("w_lo", "v_hi", False)):
                        for c in range(2):
                            last = nc.tensor.matmul(out[n][c][:, :], m[w][:, v, t], m[x][:, v, c * 512:(c + 1) * 512],
                                                    start=start, stop=False, skip_group_check=True)
                last.then_inc(wv_done, 1)

            for b in range(3):
                values(b, b)
            over(pe, 3, AHEAD - 1, values)
            over(pe, AHEAD - 1, NK - 1, lambda b, s: (activations(b + 1, s + 1), values(b, s)))
            values(NK - 1, NK - 1)

        @block.scalar
        def _(act):
            for free, depth in ((u_ok, RING), (v_ok, RING), (uh_done, RING), (wv_done, RING), (w_ok, BANKS)):
                act.sem_inc(free, depth)

            def u_hi(b, s):
                act.wait_ge(u_in[s % RING], loads(b - AHEAD, s))
                act.wait_ge(uh_done, b - AHEAD + 1)
                nc.scalar.activation(m["u_hi"][:, s % RING], m["u_raw"][:, s % RING], ACT.Copy).then_inc(u_hi_ok, 1)

            def gelu(b, s):
                act.wait_ge(uh_done, b - AHEAD + 1 + RING)
                nc.scalar.activation(acts[s % BANKS], acts[s % BANKS], ACT.Gelu).then_inc(gelu_ok, 1)

            def v_and_w_hi(b, s):
                act.wait_ge(v_in[s % RING], loads(b, s))
                act.wait_ge(wv_done, b + 1)
                nc.scalar.activation(m["v_hi"][:, s % RING], m["v_raw"][:, s % RING], ACT.Copy).then_inc(v_hi_ok, 1)
                act.wait_ge(prod_ok, b + 1)
                nc.scalar.activation(m["w_hi"][:, s % RING], prods[s % BANKS], ACT.Copy).then_inc(w_hi_ok, 1)

            over(act, 0, AHEAD - 1, v_and_w_hi)
            act.wait_ge(prod_ok, HI_OVER)
            u_hi(AHEAD, AHEAD)
            v_and_w_hi(AHEAD - 1, AHEAD - 1)
            over(act, AHEAD, NK - 1, lambda b, s: (u_hi(b + 1, s + 1), gelu(b, s), v_and_w_hi(b, s)))
            gelu(NK - 1, NK - 1)
            v_and_w_hi(NK - 1, NK - 1)

        @block.vector
        def _(dve):
            def u_lo(b, s):
                dve.wait_ge(u_hi_ok, b - AHEAD + 1)
                dve.wait_ge(uh_done, b - AHEAD + 1)
                nc.vector.tensor_tensor(m["u_lo"][:, s % RING], m["u_raw"][:, s % RING],
                                        m["u_hi"][:, s % RING].bitcast(F32), ALU.subtract).then_inc(u_ok, 1)

            def gated(b, s, a):
                nc.vector.tensor_tensor(prods[s % BANKS], a, m["G"][:, bass.ds(b, 1), :].rearrange("p o t -> p (o t)"),
                                        ALU.mult).then_inc(prod_ok, 1)

            def v_and_w_lo(b, s):
                v = s % RING
                dve.wait_ge(v_hi_ok, b + 1)
                nc.vector.tensor_tensor(m["v_lo"][:, v], m["v_raw"][:, v], m["v_hi"][:, v].bitcast(F32),
                                        ALU.subtract).then_inc(v_ok, 1)
                dve.wait_ge(w_hi_ok, b + 1)
                nc.vector.tensor_tensor(m["w_lo"][:, v], prods[s % BANKS], m["w_hi"][:, v].bitcast(F32),
                                        ALU.subtract).then_inc(w_ok, 1)

            def step_ahead(b, s):
                gated(b, s, m["ahead"][:, bass.ds(b, 1), :].rearrange("p o t -> p (o t)"))
                v_and_w_lo(b, s)

            def step(b, s):
                dve.wait_ge(gelu_ok, b - AHEAD + 1)
                gated(b, s, acts[s % BANKS])
                v_and_w_lo(b, s)

            over(dve, 0, AHEAD - 1, step_ahead)
            gated(AHEAD - 1, AHEAD - 1, m["ahead"][:, AHEAD - 1, :])
            dve.wait_ge(prod_ok, AHEAD)
            u_lo(AHEAD, AHEAD)
            v_and_w_lo(AHEAD - 1, AHEAD - 1)
            over(dve, AHEAD, NK - 1, lambda b, s: (u_lo(b + 1, s + 1), step(b, s)))
            step(NK - 1, NK - 1)


def tail(nc, io, m, bank):
    ident = m["consts"][:, C_ID:C_ID + P]
    st = m["small"][:, 136:160]
    psum = bank.psum

    with ExitStack() as ctx:
        def sem(name):
            return ctx.enter_context(nc.semaphore(name))

        proj_full = sem("ple_proj_full")
        rT_full, gate_full = sem("rT_full"), sem("ple_gate_full")
        rT_ok = sem("rT_ready")
        sig_ok, out_done = sem("ple_sigmoid"), sem("out_written")
        var_ok, std_ok = sem("var2_ready"), sem("std2_ready")
        dv = Steps(ctx, nc, "tail_dve")
        r_ok = Steps(ctx, nc, "r_ready")
        proj_ok = Steps(ctx, nc, "ple_proj_copied")
        logit_ok = Steps(ctx, nc, "ple_logits")
        y_ok = Steps(ctx, nc, "y_ready")
        block = ctx.enter_context(nc.Block())
        pairs = [(n, c) for n in range(NT) for c in range(2)]

        @block.tensor
        def _(pe):
            for j, (n, c) in enumerate(pairs):
                for k in range(PLE // P):
                    last = nc.tensor.matmul(psum[j][:, :], m["pT"][:, k, n * P:(n + 1) * P],
                                            m["w_ple_proj"][:, k, c * 512:(c + 1) * 512],
                                            start=(k == 0), stop=(k == PLE // P - 1))
                last.then_inc(proj_full, 1)
            for j, (n, c) in enumerate(pairs):
                pe.wait_ge(proj_ok.sem, j + 1)
                pe.wait_ge(r_ok.sem, j + 1)
                for i in range(4):
                    last = nc.tensor.transpose(psum[j][:, i * P:(i + 1) * P],
                                               m["r"][:, n, (4 * c + i) * P:(4 * c + i + 1) * P], ident)
                last.then_inc(rT_full, 1)
            for j, (n, c) in enumerate(pairs):
                pe.wait_ge(rT_ok, 2 * (n + 1))
                for k in range(KD):
                    last = nc.tensor.matmul(psum[4 + j][:, :], m["rT"][:, k, n * P:(n + 1) * P],
                                            m["w_ple_gate"][:, k, c * 512:(c + 1) * 512],
                                            start=(k == 0), stop=(k == KD - 1))
                last.then_inc(gate_full, 1)

        @block.scalar
        def _(act):
            for j, (n, c) in enumerate(pairs):
                act.wait_ge(rT_full, j + 1)
                nc.scalar.activation(m["rT"][:, 4 * c:4 * c + 4, n * P:(n + 1) * P],
                                     psum[j][:, :].rearrange("p (k t) -> p k t", t=P), ACT.Copy).then_inc(rT_ok, 1)
            for j, (n, c) in enumerate(pairs):
                act.wait_ge(logit_ok.sem, j + 1)
                s = m["ple2"][:, n, c * 512:(c + 1) * 512]
                nc.scalar.activation(s, s, ACT.Sigmoid).then_inc(sig_ok, 1)
            for n in range(NT):
                act.wait_ge(var_ok, n + 1)
                nc.scalar.activation(st[:, 15:16], st[:, 14:15], ACT.Sqrt).then_inc(std_ok, 1)

        @block.vector
        def _(dve):
            for j, (n, c) in enumerate(pairs):
                half = slice(c * 512, (c + 1) * 512)
                r_ok.done(nc.vector.scalar_tensor_tensor(out=m["r"][:, n, half], in0=m["h"][:, n, half], scalar=ALPHA,
                                                         in1=psum[4 + j][:, :], op0=ALU.mult, op1=ALU.add))
                dve.wait_ge(proj_full, j + 1)
                proj_ok.done(nc.vector.tensor_copy(m["ple"][:, n, half], psum[j][:, :]))
            for j, (n, c) in enumerate(pairs):
                dve.wait_ge(gate_full, j + 1)
                logit_ok.done(nc.vector.tensor_tensor(m["ple2"][:, n, c * 512:(c + 1) * 512], psum[4 + j][:, :],
                                                      m["rows"][:, 0, c * 512:(c + 1) * 512], ALU.add))
            r_ok.wait(dve)
            proj_ok.wait(dve)
            for n in range(NT):
                dve.wait_ge(sig_ok, 2 * (n + 1))
                z = m["ple"][:, n, :]
                dv.done(nc.vector.tensor_tensor(z, z, m["ple2"][:, n, :], ALU.mult))
                dv.wait(dve)
                dv.done(nc.vector.tensor_tensor(z, z, m["r"][:, n, :], ALU.add))
                dv.wait(dve)
                layer_norm(nc, dve, dv, st, z, m["y_out"][:, n, :], m["rows"][:, 1, :], m["rows"][:, 2, :],
                           var_ok, std_ok, n, y_ok)

        @block.sync
        def _(sp):
            for n in range(NT):
                sp.wait_ge(y_ok.sem, n + 1)
                sp.dma_start(io["out"][n * P:(n + 1) * P, :], m["y_out"][:, n, :]).then_inc(out_done, 16)
            sp.wait_ge(out_done, 16 * NT)


def program(nc, io):
    m = memory(nc)
    with ExitStack() as ctx:
        psum = [ctx.enter_context(nc.psum_tensor(f"bank{b}", [P, 512], F32)) for b in range(8)]
        bank = Banks(ctx, nc, psum, group_order())
        front(nc, io, m, bank)
        route(nc, io, m, bank)
        experts(nc, io, m, bank)
        tail(nc, io, m, bank)


def constants():
    c = np.zeros((P, C_COLS), np.float32)
    c[:, C_ID:C_ID + P] = np.eye(P, dtype=np.float32)
    q, k = np.arange(P)[:, None], np.arange(P)[None, :]
    c[:, C_MASK + P:C_MASK + T] = np.where(k <= q, 0.0, NEG)
    c[:, C_IOTA:C_IOTA + NK] = np.arange(NK)
    for n in range(NT):
        o = C_ROPE + n * ROPE_W
        for rot, theta in ((ROT, 500000.0), (ROPE, 10000.0)):
            inv = np.power(np.float32(theta), -np.arange(0, rot, 2, dtype=np.float32) / np.float32(rot))
            ang = (np.arange(P, dtype=np.float32) + n * P)[:, None] * inv[None, :].astype(np.float32)
            cos, sin = np.cos(ang), np.sin(ang)
            c[:, o:o + 2 * rot] = np.concatenate([cos, cos, -sin, sin], axis=1)
            o += 2 * rot
    return c


def kernel(**inputs):
    import concourse.bacc as bacc
    from concourse.bass_utils import run_bass_kernel_spmd

    i = {k: np.asarray(v) for k, v in inputs.items()}
    arrays = {
        "x": i["x"][0],
        "xT": i["x"][0].T,
        "pT": i["p"][0, 0].T,
        "w_in": i["w_in"][0],
        "w_q_up": i["w_q_up"][0],
        "w_kv_up": i["w_kv_up"][0],
        "w_branch_moba": i["w_branch_moba"][0],
        "w_branch_mla": i["w_branch_mla"][0],
        "w_out": i["w_out"][0],
        "ln1_g": i["ln1_g"][0],
        "ln1_b": i["ln1_b"][0],
        "peer_w_q": i["peer_w_q"][0],
        "subkT": i["peer_sub_keys"][0].reshape(HP, NK, DKH).transpose(0, 2, 1),
        "uT": i["peer_u"][0].reshape(NK, NK, KD, P).transpose(0, 3, 2, 1),
        "v": i["peer_v"][0].reshape(NK, NK, D),
        "w_ple_proj": i["w_ple_proj"][0],
        "w_ple_gate": i["w_ple_gate"][0],
        "b_ple_gate": i["b_ple_gate"][0],
        "ln2_g": i["ln2_g"][0],
        "ln2_b": i["ln2_b"][0],
        "cols": np.concatenate([i["b_gates"][0].reshape(-1, P).T, i["mla_q_norm"][0].reshape(-1, P).T,
                                i["mla_kv_norm"][0].reshape(-1, P).T], axis=1),
        "consts": constants(),
    }
    nc = bacc.Bacc("TRN2", target_bir_lowering=False, num_devices=1)
    feeds, io = {}, {}
    for name, a in arrays.items():
        a = np.ascontiguousarray(a)
        feeds[f"{name}_dram"] = a
        io[name] = nc.dram_tensor(f"{name}_dram", a.shape, mybir.dt.from_np(a.dtype), kind="ExternalInput").ap()
    io["out"] = nc.dram_tensor("out_dram", (T, D), F32, kind="ExternalOutput").ap()
    program(nc, io)
    r = run_bass_kernel_spmd(nc, [feeds], core_ids=[0])
    return r.results[0]["out_dram"].reshape(1, T, D)
```

```python
from contextlib import ExitStack

import numpy as np

import concourse.bass as bass
from concourse import mybir

P = 128
D = 1024
T = 256
NT = T // P
KD = D // P
H = 8
DH = 64
ROT = DH // 4
QLORA, KVLORA, ROPE = 512, 256, 32
DQK = DH + ROPE
W = H * DH
Q0, K0, V0, CQ0, CKV0, KR0 = 0, W, 2 * W, 3 * W, 3 * W + QLORA, 3 * W + QLORA + KVLORA
TOK = KR0 + ROPE
IN_COLS = TOK + 2 * D
CHUNK = 256
PH = 8
NK = 128
DKH = 128
HP = 2 * PH
TK = 16
SLOTS = PH * TK
PLE = 256
OHT = 8
HEADS_AHEAD = 3
SIMS_AFTER = {3: 0, 8: 1, 12: 2}
BLOCKS = 4
FIRST = 4
SCORES_AHEAD = HEADS_AHEAD + 1
SLOTS_P = HEADS_AHEAD + 1
AHEAD = 24
AHEAD_LOW = 20
ALPHA = 2.0 ** 0.25
LN_EPS, RMS_EPS = 1e-5, 1e-6
NEG = -1e30
LOWEST = -3.0e38

F32 = mybir.dt.float32
F32R = mybir.dt.float32r
U32 = mybir.dt.uint32
BF16 = mybir.dt.bfloat16
ALU = mybir.AluOpType
ACT = mybir.ActivationFunctionType
AX_X = mybir.AxisListType.X

C_ID, C_MASK, C_IOTA, C_ROPE = 0, P, P + T, 2 * P + T
ROPE_W = 2 * ROT + 2 * ROPE
C_COLS = C_ROPE + NT * ROPE_W
B_GATE, B_QN, B_KVN = 0, 2 * KD, 2 * KD + QLORA // P
B_COLS = B_KVN + KVLORA // P

KB = 1024


class Banks:

    def __init__(self, ctx, nc, psum, order):
        self.psum = psum
        self.full = [ctx.enter_context(nc.semaphore(f"bank_full{b}")) for b in range(8)]
        self.drained = [ctx.enter_context(nc.semaphore(f"bank_drained{b}")) for b in range(8)]
        self.order = order
        self.at = {name: g for g, name in enumerate(order)}

    def fill(self, pe, name):
        g = self.at[name]
        if g >= 8:
            pe.wait_ge(self.drained[g % 8], g // 8)
        return self.psum[g % 8]

    def filled(self, name, last):
        last.then_inc(self.full[self.at[name] % 8], 1)

    def read(self, eng, name):
        g = self.at[name]
        eng.wait_ge(self.full[g % 8], g // 8 + 1)
        return self.psum[g % 8]

    def drain(self, name, last):
        last.then_inc(self.drained[self.at[name] % 8], 1)

    def await_drained(self, eng, name):
        g = self.at[name]
        eng.wait_ge(self.drained[g % 8], g // 8 + 1)


class Steps:

    def __init__(self, ctx, nc, name):
        self.sem = ctx.enter_context(nc.semaphore(name))
        self.n = 0

    def done(self, ins):
        ins.then_inc(self.sem, 1)
        self.n += 1

    def wait(self, eng):
        eng.wait_ge(self.sem, self.n)


def over(eng, lo, hi, step, unroll=4):
    rounds = (hi - lo) // unroll
    if rounds:
        with eng.Fori(0, rounds) as i:
            for r in range(unroll):
                step(i * unroll + (lo + r), lo + r)
    for b in range(lo + rounds * unroll, hi):
        step(b, b)


def group_order():
    o = [("tok", c, n) for c in range(TOK_CHUNKS) for n in range(NT)]
    o += [("gate", j) for j in range(0, 4)]
    o += [("qT", n) for n in range(NT)] + [("kT", n) for n in range(NT)]
    o += [("gate", j) for j in range(4, 8)]
    o += [("cqT", n) for n in range(NT)] + [("ckvT", n) for n in range(NT)] + [("krT",)]
    o += [("gate", j) for j in range(8, 12)]
    o += [("qup", n, c) for n in range(NT) for c in range(2)]
    o += [("knT", g) for g in range(H // 2)]
    o += [("vm", n) for n in range(NT)]
    o += [("gate", j) for j in range(12, 16)]
    o += [("qmT", n, c) for n in range(NT) for c in range(2)]
    o += [("S", h) for h in range(SCORES_AHEAD)]
    for h in range(2 * H):
        o += [("PT", h)]
        if h + SCORES_AHEAD < 2 * H:
            o += [("S", h + SCORES_AHEAD)]
        o += [("Y", h)]
    o += [("br", c) for c in range(KD)]
    o += [("mix", n, c) for n in range(NT) for c in range(2)]
    o += [("hT", n, c) for n in range(NT) for c in range(2)]
    for hp in range(HP):
        o += [("pq", hp)]
        if hp in SIMS_AFTER:
            o += [("sim", n, SIMS_AFTER[hp]) for n in range(NT)]
    o += [("sim", n, 3) for n in range(NT)]
    o += [("slotT", w) for w in range(3)]
    return o


def memory(nc):
    m = {}
    base = -(-nc.sbuf_base // 32) * 32

    def put(name, shape, off, dt=F32):
        size = int(np.prod(shape[1:])) * (2 if dt == BF16 else 4)
        m[name] = nc.alloc_sbuf_tensor_at(name, shape, dt, offset=base + off)
        return off + -(-size // 32) * 32

    o = put("x_hi", [P, KD, T], 0, F32R)
    o = put("x_lo", [P, KD, T], o, F32R)
    o = put("w_raw", [P, 2, KD, CHUNK + ROPE], o)
    o = put("wi_hi", [P, 2, KD, CHUNK + ROPE], o, F32R)
    o = put("wi_lo", [P, 2, KD, CHUNK + ROPE], o, F32R)
    o = put("tok", [P, NT, TOK], o)
    o = put("sigT", [P, 2, KD, T], o)
    qk = o
    o = put("qT", [P, W // P, T], o)
    o = put("kT", [P, W // P, T], o)
    o = put("cqT", [P, QLORA // P, T], o)
    o = put("ckvT", [P, KVLORA // P, T], o)
    o = put("qmT", [P, H, T], o)
    o = put("kmT", [P, H, T], o)
    o = put("vm", [P, NT, W], o)
    o = put("w_q_up", [P, QLORA // P, H * DQK], o)
    o = put("w_kv_up", [P, KVLORA // P, H * 2 * DH], o)
    o = put("w_br", [P, 2, W // P, D], o)
    o = put("scratch", [P, QLORA + KVLORA + 2 * T], o)
    assert o <= 196 * KB, o
    w_up = (QLORA // P * H * DQK + KVLORA // P * H * 2 * DH) * 4
    attn = o - 4 * (QLORA + KVLORA + 2 * T) - 2 * W // P * D * 4 - w_up
    attn = put("probs", [P, SLOTS_P, NT, T], attn)
    put("probsT", [P, HEADS_AHEAD, 3, P], attn)
    put("xT", [P, KD, T], 180 * KB)
    m["qm"] = m["tok"]
    put("yT_hi", [P, 2, W // P, T], 0, F32R)
    put("yT_lo0", [P, W // P, T], 64 * KB, F32R)
    put("yT_lo1", [P, W // P, T], qk + 8 * KB, F32R)
    at = put("wb_hi", [P, 2, 2 * W // P, P], qk + 14 * KB, F32R)
    put("wb_lo", [P, 2, 2 * W // P, P], at, F32R)
    put("mergedT", [P, KD, T], 8 * KB)
    put("w_out", [P, KD, D], 16 * KB)
    put("x_tok", [P, NT, D], 48 * KB)
    put("ln1", [P, 2, D], 56 * KB)
    put("h", [P, NT, D], 196 * KB)
    o = put("consts", [P, C_COLS], 204 * KB)
    o = put("cols", [P, B_COLS], o)
    o = put("small", [P, 160], o)
    assert base + o <= nc.sbuf_usable_end, o

    put("G", [P, NK, T], 0)
    o = put("subk", [P, HP, NK], 8 * KB)
    o = put("pqT", [P, HP, T], o)
    o = put("sims", [P, NT, HP, NK], o)
    o = put("sims2", [P, 4, NK], o)
    assert o <= 64 * KB, o
    o = put("b_hi", [P, 4, KD, P], 64 * KB, F32R)
    o = put("b_lo", [P, 4, KD, P], o, F32R)
    o = put("b_raw", [P, BLOCKS, KD, P], 112 * KB)
    assert o <= 128 * KB, o
    put("ahead", [P, AHEAD_LOW, T], 128 * KB)
    put("ahead_high", [P, AHEAD - AHEAD_LOW, T], 172 * KB)
    o = put("cand", [P, 2, TK * TK], 148 * KB)
    o = put("cand2", [P, 2, TK * TK], o)
    assert o <= 152 * KB
    o = put("eq", [P, 2, SLOTS // 4, TK], 156 * KB, BF16)
    o = put("topv", [P, NT, HP, TK], o)
    o = put("topi", [P, NT, HP, TK], o, U32)
    o = put("topf", [P, NT, HP, TK], o, BF16)
    o = put("best", [P, NT, PH, TK], o)
    o = put("bpos", [P, NT, PH, TK], o, U32)
    o = put("slot", [P, 3, NT, SLOTS], o)
    o = put("ex", [P, NT, PH, TK], o)
    assert o <= 172 * KB, o
    o = put("bab", [P, 2, SLOTS // 4], 192 * KB, U32)
    o = put("babf", [P, 2, SLOTS // 4], o, BF16)
    o = put("iota16", [P, TK], o, BF16)
    o = put("pstat", [P, 2, NT, PH], o)
    o = put("oh1_plain", [P, 2, NK, OHT], 148 * KB, BF16)
    assert o == 152 * KB, o
    o = put("gateT", [P, T], o)
    o = put("keys", [P, 2, T], o, BF16)
    o = put("iota_t", [P, NK, OHT], o, BF16)
    o = put("oh1", [P, 2, OHT, NK], o)
    o = put("oh2", [P, 2, OHT, NK], o)
    assert o <= 172 * KB, o
    put("oh2_plain", [P, 2, NK, OHT], 192 * KB, BF16)
    o = put("u_raw", [P, 2, KD, P], 128 * KB)
    o = put("u_hi", [P, 2, KD, P], o, F32R)
    o = put("u_lo0", [P, KD, P], o, F32R)
    o = put("v_raw", [P, 2, D], o)
    o = put("v_hi", [P, 2, D], o, F32R)
    o = put("v_lo", [P, 2, D], o, F32R)
    o = put("u_lo1", [P, KD, P], o, F32R)
    assert o == 176 * KB, o
    o = put("h_hi", [P, KD, T], o, F32R)
    o = put("h_lo", [P, KD, T], o, F32R)
    o = put("w_hi", [P, 2, T], o, F32R)
    o = put("w_lo", [P, 2, T], o, F32R)
    assert o <= 196 * KB, o
    put("v_deep", [P, 2, D], 0)
    o = put("w_g_raw", [P, KD, D], 0)
    o = put("w_g_hi", [P, KD, D], o, F32R)
    o = put("w_g_lo", [P, KD, D], o, F32R)
    o = put("w_ple_proj", [P, PLE // P, D], o)
    o = put("pT", [P, PLE // P, T], o)
    o = put("rows", [P, 3, D], o)
    assert o <= 120 * KB, o
    o = put("r", [P, NT, D], 128 * KB)
    o = put("rT_hi", [P, KD, T], o, F32R)
    o = put("rT_lo", [P, KD, T], o, F32R)
    o = put("sig", [P, NT, D], o)
    o = put("z", [P, NT, D], o)
    o = put("y_out", [P, NT, D], o)
    assert o <= 192 * KB, o
    return m


def made_ahead(m, b):
    if isinstance(b, int) and b >= AHEAD_LOW:
        return m["ahead_high"][:, b - AHEAD_LOW, :]
    return m["ahead"][:, bass.ds(b, 1), :].rearrange("p o t -> p (o t)")


def rope(nc, dve, steps, src, dst, tmp, table, heads, rot, last):
    half = rot // 2
    cos = table[:, 0:rot].unsqueeze(1).to_broadcast([P, heads, rot])
    sin = table[:, rot:2 * rot].unsqueeze(1).to_broadcast([P, heads, rot])
    a, b = tmp
    steps.done(nc.vector.tensor_tensor(a, src, cos, ALU.mult))
    steps.done(nc.vector.tensor_tensor(b[:, :, 0:half], src[:, :, half:rot], sin[:, :, 0:half], ALU.mult))
    steps.done(nc.vector.tensor_tensor(b[:, :, half:rot], src[:, :, 0:half], sin[:, :, half:rot], ALU.mult))
    steps.wait(dve)
    last.done(nc.vector.tensor_tensor(dst, a, b, ALU.add))
    last.wait(dve)


def half_stats(nc, steps, st, z, c):
    steps.done(nc.vector.bn_stats(st[:, 6 * c:6 * c + 6], z[:, c * 512:(c + 1) * 512]))


def layer_norm(nc, dve, steps, st, z, out, gain, shift, var_ok, std_ok, n, last):
    steps.wait(dve)
    steps.done(nc.vector.bn_aggr(st[:, 12:14], st[:, 0:12]))
    steps.wait(dve)
    nc.vector.tensor_scalar(st[:, 14:15], st[:, 13:14], LN_EPS, None, ALU.add).then_inc(var_ok, 1)
    steps.done(nc.vector.scalar_tensor_tensor(out=z, in0=z, scalar=st[:, 12:13], in1=gain,
                                              op0=ALU.subtract, op1=ALU.mult))
    dve.wait_ge(std_ok, n + 1)
    steps.done(nc.vector.reciprocal(st[:, 16:17], st[:, 15:16]))
    steps.wait(dve)
    for c in range(2):
        half = slice(c * 512, (c + 1) * 512)
        last.done(nc.vector.scalar_tensor_tensor(out=out[:, half], in0=z[:, half], scalar=st[:, 16:17],
                                                 in1=shift[:, half], op0=ALU.mult, op1=ALU.add))
    last.wait(dve)


PAIRS = [(n, c) for n in range(NT) for c in range(2)]
HALVES = (slice(0, KD // 2), slice(KD // 2, KD))
QUP = ((0, 5 * DQK), (5 * DQK, H * DQK))
W_STARTS = list(range(0, KR0, CHUNK)) + list(range(TOK, IN_COLS, CHUNK))
W_WIDTHS = [CHUNK] * (KR0 // CHUNK - 1) + [CHUNK + ROPE] + [CHUNK] * (2 * D // CHUNK)
TOK_CHUNKS = KR0 // CHUNK
GPC = CHUNK // P
CQ_CHUNK = CQ0 // CHUNK


def front(nc, io, m, bank, block_in):
    ident = m["consts"][:, C_ID:C_ID + P]
    tok, small = m["tok"], m["small"]
    n_chunks = len(W_STARTS)
    scales = [DH ** -0.5] * H + [DQK ** -0.5] * H
    ss, rs = small[:, 0:4], small[:, 4:8]
    mx, nmx = small[:, 8:40], small[:, 40:72]
    den, rden = small[:, 72:104], small[:, 104:136]
    st = small[:, 136:160]

    with ExitStack() as ctx:
        def sem(name):
            return ctx.enter_context(nc.semaphore(name))

        c_in, b_in = sem("consts_in"), sem("cols_in")
        x_in = [sem(f"x_half{i}_in") for i in range(2)]
        w_in_sem = [sem(f"w_in_slot{k}") for k in range(2)]
        w_first_in = [sem(f"w_in_chunk0_half{i}_in") for i in range(2)]
        x_hi_ok, x_lo_ok = sem("x_hi_ready"), sem("x_lo_ready")
        w_first_hi_ok, w_first_ok = sem("w_in_first_hi"), sem("w_in_first_split")
        w_hi_ok, w_ok = sem("w_in_hi_ready"), sem("w_in_split")
        wq_in, wkv_in, wb_in = sem("w_q_up_in"), sem("w_kv_up_in"), sem("w_branch_in")
        wo_in, xt_in, ln_in = sem("w_out_in"), sem("x_rows_in"), sem("ln1_in")
        ss_ready, root_ready, ms_ready = sem("squares_summed"), sem("root_ready"), sem("mean_square_ready")
        y_hi_ok = sem("y_hi_ready")
        wb_hi_ok, wb_ok = sem("w_branch_hi"), sem("w_branch_split")
        b_first_ok = sem("block_first_split")
        b_first_hi_ok, h_hi_ok = sem("block_first_hi"), sem("h_hi_ready")
        exped = sem("exp_done")
        var_ok, std_ok = sem("var_ready"), sem("std_ready")
        dv = Steps(ctx, nc, "front_dve")
        qk_roped = Steps(ctx, nc, "qk_roped")
        lora_ready = Steps(ctx, nc, "lora_ready")
        qm_roped = Steps(ctx, nc, "qm_roped")
        nmax = Steps(ctx, nc, "neg_max_ready")
        probs_ok = Steps(ctx, nc, "probs_ready")
        merged_ok = Steps(ctx, nc, "merged_ready")
        h_ok = Steps(ctx, nc, "h_ready")
        block = ctx.enter_context(nc.Block())

        @block.sync
        def _(sp):
            xT = io["xT"].rearrange("(k p) t -> p k t", p=P)
            w_in = io["w_in"].rearrange("(k p) c -> p k c", p=P)
            for i, half in enumerate(HALVES):
                sp.dma_start(m["xT"][:, half], xT[:, half]).then_inc(x_in[i], 16)
                sp.dma_start(m["w_raw"][:, 0, half, 0:CHUNK], w_in[:, half, 0:CHUNK]).then_inc(w_first_in[i], 16)
            for c in range(n_chunks):
                if c == 2:
                    sp.wait_ge(w_first_ok, 2)
                if c > 2:
                    sp.wait_ge(w_ok, c - 2)
                a, w = W_STARTS[c], W_WIDTHS[c]
                if c:
                    sp.dma_start(m["w_raw"][:, c % 2, :, 0:w], w_in[:, :, a:a + w]).then_inc(w_in_sem[c % 2], 16)
                if c == 1:
                    sp.dma_start(m["consts"][:], io["consts"]).then_inc(c_in, 16)
                    sp.dma_start(m["cols"][:], io["cols"]).then_inc(b_in, 16)
                if 4 <= c < 4 + QLORA // P:
                    k = c - 4
                    sp.dma_start(m["w_q_up"][:, k, :], io["w_q_up"][k * P:(k + 1) * P, :]).then_inc(wq_in, 16)
                if 11 <= c < 11 + KVLORA // P:
                    k = c - 11
                    sp.dma_start(m["w_kv_up"][:, k, :], io["w_kv_up"][k * P:(k + 1) * P, :]).then_inc(wkv_in, 16)
            for b, w in enumerate(("w_branch_moba", "w_branch_mla")):
                sp.dma_start(m["w_br"][:, b], io[w].rearrange("(k p) c -> p k c", p=P)).then_inc(wb_in, 16)
            for j in (13, 15):
                bank.read(sp, ("gate", j))
            sp.dma_start(m["w_out"][:], io["w_out"].rearrange("(k p) c -> p k c", p=P)).then_inc(wo_in, 16)
            sp.dma_start(m["x_tok"][:], io["x"].rearrange("(n p) d -> p n d", p=P)).then_inc(xt_in, 16)
            sp.dma_start(m["ln1"][:, 0, :], io["ln1_g"].partition_broadcast(P)).then_inc(ln_in, 16)
            sp.dma_start(m["ln1"][:, 1, :], io["ln1_b"].partition_broadcast(P)).then_inc(ln_in, 16)
            bank.read(sp, ("br", KD - 1))
            for b in range(FIRST + BLOCKS):
                if b >= BLOCKS:
                    sp.wait_ge(b_first_ok, b - BLOCKS + 1)
                sp.dma_start(m["b_raw"][:, b % BLOCKS], io["peer_wqT"][b]).then_inc(block_in[b % BLOCKS], 16)

        @block.tensor
        def _(pe):
            def split_matmul(out, w, x, k, last):
                nc.tensor.matmul(out, w[0], x[0], start=(k == 0), stop=False)
                nc.tensor.matmul(out, w[0], x[1], start=False, stop=False)
                return nc.tensor.matmul(out, w[1], x[0], start=False, stop=last)

            def gate(j):
                c = TOK_CHUNKS + j // GPC
                if j % GPC == 0:
                    pe.wait_ge(w_ok, c)
                ps = bank.fill(pe, ("gate", j))
                cols = slice(j % GPC * P, (j % GPC + 1) * P)
                for k in range(KD):
                    last = split_matmul(ps[:, 0:T], [m[w][:, c % 2, k, cols] for w in ("wi_hi", "wi_lo")],
                                        [m[x][:, k, :] for x in ("x_hi", "x_lo")], k, k == KD - 1)
                bank.filled(("gate", j), last)

            def turn(name, blocks, width=P):
                ps = bank.fill(pe, name)
                for i, b in enumerate(blocks):
                    last = nc.tensor.transpose(ps[0:width, i * P:(i + 1) * P], b, ident)
                bank.filled(name, last)

            for c in range(TOK_CHUNKS):
                if c:
                    pe.wait_ge(w_ok, c)
                for n in range(NT):
                    ps = bank.fill(pe, ("tok", c, n))
                    for k in range(KD):
                        if c == n == 0 and k % (KD // 2) == 0:
                            pe.wait_ge(w_first_ok, k // (KD // 2) + 1)
                        last = split_matmul(ps[:, 0:W_WIDTHS[c]],
                                            [m[x][:, k, n * P:(n + 1) * P] for x in ("x_hi", "x_lo")],
                                            [m[w][:, c % 2, k, 0:W_WIDTHS[c]] for w in ("wi_hi", "wi_lo")],
                                            k, k == KD - 1)
                    bank.filled(("tok", c, n), last)
            pe.wait_ge(c_in, 16)
            for j in range(4):
                gate(j)
            for which, base in (("qT", Q0), ("kT", K0)):
                for n in range(NT):
                    pe.wait_ge(qk_roped.sem, n + 1)
                    turn((which, n), [tok[:, n, base + i * P:base + (i + 1) * P] for i in range(W // P)])
            for j in range(4, 8):
                gate(j)
            for n in range(NT):
                pe.wait_ge(lora_ready.sem, n + 1)
                turn(("cqT", n), [tok[:, n, CQ0 + i * P:CQ0 + (i + 1) * P] for i in range(QLORA // P)])
            for n in range(NT):
                turn(("ckvT", n), [tok[:, n, CKV0 + i * P:CKV0 + (i + 1) * P] for i in range(KVLORA // P)])
            turn(("krT",), [tok[:, n, KR0:KR0 + ROPE] for n in range(NT)], ROPE)
            for j in range(8, 12):
                gate(j)
            pe.wait_ge(wq_in, 16 * (QLORA // P))
            for n in range(NT):
                bank.await_drained(pe, ("cqT", n))
                for c, (a, b) in enumerate(QUP):
                    ps = bank.fill(pe, ("qup", n, c))
                    for k in range(QLORA // P):
                        last = nc.tensor.matmul(ps[:, 0:b - a], m["cqT"][:, k, n * P:(n + 1) * P],
                                                m["w_q_up"][:, k, a:b], start=(k == 0), stop=(k == QLORA // P - 1))
                    bank.filled(("qup", n, c), last)
            pe.wait_ge(wkv_in, 16 * (KVLORA // P))
            for n in range(NT):
                bank.await_drained(pe, ("ckvT", n))
            KK = KVLORA // P
            for g in range(H // 2):
                ps = bank.fill(pe, ("knT", g))
                for e in range(2):
                    col = (2 * g + e) * 2 * DH
                    for k in range(KK):
                        last = nc.tensor.matmul(ps[0:DH, e * T:(e + 1) * T], m["w_kv_up"][:, k, col:col + DH],
                                                m["ckvT"][:, k, :], start=(k == 0), stop=(k == KK - 1))
                bank.filled(("knT", g), last)
            v_cols = m["w_kv_up"][:].rearrange("p k (h e d) -> p k h e d", h=H, e=2)
            for n in range(NT):
                ps = bank.fill(pe, ("vm", n))
                for k in range(KK):
                    last = nc.tensor.matmul(ps[:, 0:W].rearrange("p (h d) -> p h d", h=H),
                                            m["ckvT"][:, k, n * P:(n + 1) * P], v_cols[:, k, :, 1, :],
                                            start=(k == 0), stop=(k == KK - 1))
                bank.filled(("vm", n), last)
            for j in range(12, 16):
                gate(j)
            for n in range(NT):
                pe.wait_ge(qm_roped.sem, n + 1)
                for c in range(2):
                    turn(("qmT", n, c), [m["qm"][:, n, (4 * c + i) * DQK:(4 * c + i + 1) * DQK] for i in range(4)], DQK)

            def operands(h):
                if h < H:
                    r = slice(DH * (h % 2), DH * (h % 2) + DH)
                    return m["qT"][r, h // 2, :], m["kT"][r, h // 2, :]
                return m["qmT"][0:DQK, h - H, :], m["kmT"][0:DQK, h - H, :]

            def scores(h):
                if h == 0:
                    for n in range(NT):
                        bank.await_drained(pe, ("qT", n))
                        bank.await_drained(pe, ("kT", n))
                if h == H:
                    bank.await_drained(pe, ("krT",))
                    for g in range(H // 2):
                        bank.await_drained(pe, ("knT", g))
                    for n in range(NT):
                        bank.await_drained(pe, ("vm", n))
                        for c in range(2):
                            bank.await_drained(pe, ("qmT", n, c))
                q, k = operands(h)
                ps = bank.fill(pe, ("S", h))
                nc.tensor.matmul(ps[:, 0:P], q[:, 0:P], k[:, 0:P], start=True, stop=True)
                bank.filled(("S", h), nc.tensor.matmul(ps[:, P:P + T], q[:, P:T], k[:, :], start=True, stop=True))

            def values(h):
                bank.await_drained(pe, ("PT", h))
                v = (lambda n: tok[:, n, V0 + h * DH:V0 + (h + 1) * DH]) if h < H else \
                    (lambda n: m["vm"][:, n, (h - H) * DH:(h - H + 1) * DH])
                pT = m["probsT"][:, h % HEADS_AHEAD]
                ps = bank.fill(pe, ("Y", h))
                nc.tensor.matmul(ps[0:DH, 0:P], v(0), pT[:, 0, :], start=True, stop=True)
                nc.tensor.matmul(ps[0:DH, P:T], v(0), pT[:, 1, :], start=True, stop=False)
                last = nc.tensor.matmul(ps[0:DH, P:T], v(1), pT[:, 2, :], start=False, stop=True)
                bank.filled(("Y", h), last)

            for h in range(SCORES_AHEAD):
                scores(h)
            for h in range(2 * H):
                pe.wait_ge(probs_ok.sem, h + 1)
                pr = m["probs"][:, h % SLOTS_P]
                turn(("PT", h), [pr[:, 0, 0:P], pr[:, 1, 0:P], pr[:, 1, P:T]])
                if h + SCORES_AHEAD < 2 * H:
                    scores(h + SCORES_AHEAD)
                values(h)
            for h in range(2 * H):
                bank.await_drained(pe, ("Y", h))
            for c in range(KD):
                pe.wait_ge(wb_ok, c + 1)
                ps = bank.fill(pe, ("br", c))
                for b in range(2):
                    K = W // P
                    for k in range(K):
                        last = split_matmul(ps[:, b * T:(b + 1) * T], [m[w][:, c % 2, b * K + k, :] for w in ("wb_hi", "wb_lo")],
                                            [m["yT_hi"][:, b, k, :], m[f"yT_lo{b}"][:, k, :]], k, k == K - 1)
                bank.filled(("br", c), last)
            pe.wait_ge(merged_ok.sem, KD)
            pe.wait_ge(wo_in, 16)
            for n in range(NT):
                for c in range(2):
                    ps = bank.fill(pe, ("mix", n, c))
                    for k in range(KD):
                        last = nc.tensor.matmul(ps[:, :], m["mergedT"][:, k, n * P:(n + 1) * P],
                                                m["w_out"][:, k, c * 512:(c + 1) * 512],
                                                start=(k == 0), stop=(k == KD - 1))
                    bank.filled(("mix", n, c), last)
            for n in range(NT):
                for c in range(2):
                    pe.wait_ge(h_ok.sem, 2 * n + c + 1)
                    turn(("hT", n, c), [m["h"][:, n, (4 * c + i) * P:(4 * c + i + 1) * P] for i in range(4)])

        @block.scalar
        def _(act):
            def copy_out(name, dst, src):
                bank.drain(name, nc.scalar.activation(dst, src(bank.read(act, name)), ACT.Copy))

            def w_hi(c):
                act.wait_ge(w_in_sem[c % 2], 16 * ((c + 1) // 2))
                if c >= 2:
                    used = c - 2
                    bank.read(act, ("tok", used, NT - 1) if used < TOK_CHUNKS
                              else ("gate", GPC * (used - TOK_CHUNKS) + GPC - 1))
                w = W_WIDTHS[c]
                nc.scalar.activation(m["wi_hi"][:, c % 2, :, 0:w], m["w_raw"][:, c % 2, :, 0:w],
                                     ACT.Copy).then_inc(w_hi_ok, 1)

            for i, half in enumerate(HALVES):
                act.wait_ge(x_in[i], 16)
                nc.scalar.activation(m["x_hi"][:, half], m["xT"][:, half], ACT.Copy).then_inc(x_hi_ok, 1)
                act.wait_ge(w_first_in[i], 16)
                nc.scalar.activation(m["wi_hi"][:, 0, half, 0:CHUNK], m["w_raw"][:, 0, half, 0:CHUNK], ACT.Copy).then_inc(w_first_hi_ok, 1)
            w_hi(1)
            for c in range(TOK_CHUNKS):
                a, w = W_STARTS[c], W_WIDTHS[c]
                for n in range(NT):
                    copy_out(("tok", c, n), tok[:, n, a:a + w], lambda ps: ps[:, 0:w])
                w_hi(c + 2)
            squares = m["scratch"]
            for n in range(NT):
                for c in range(CQ_CHUNK, CQ_CHUNK + 3):
                    bank.await_drained(act, ("tok", c, n))
                if n:
                    act.wait_ge(ss_ready, 2 * n)
                nc.scalar.activation(squares[:, 0:QLORA], tok[:, n, CQ0:CQ0 + QLORA],
                                     ACT.Square, accum_out=ss[:, n:n + 1]).then_inc(ss_ready, 1)
                nc.scalar.activation(squares[:, QLORA:QLORA + KVLORA], tok[:, n, CKV0:CKV0 + KVLORA],
                                     ACT.Square, accum_out=ss[:, NT + n:NT + n + 1]).then_inc(ss_ready, 1)
            act.wait_ge(ms_ready, 1)
            nc.scalar.activation(rs, ss, ACT.Sqrt).then_inc(root_ready, 1)
            act.wait_ge(b_in, 16)

            def gate(j):
                ps = bank.read(act, ("gate", j))
                bank.drain(("gate", j), nc.scalar.activation(m["sigT"][:, j // KD, j % KD, :], ps[:, 0:T], ACT.Sigmoid,
                                                             bias=m["cols"][:, B_GATE + j:B_GATE + j + 1]))
                c = TOK_CHUNKS + j // GPC + 2
                if j % GPC == GPC - 1 and c < n_chunks:
                    w_hi(c)

            for j in range(8):
                gate(j)
            copy_out(("krT",), m["kmT"][DH:DQK, :, :], lambda ps: ps[0:ROPE, 0:T].unsqueeze(1).to_broadcast([ROPE, H, T]))
            for j in range(8, 12):
                gate(j)
            for n in range(NT):
                bank.read(act, ("qT", n))
                bank.read(act, ("kT", n))
            for n in range(NT):
                for c, (a, b) in enumerate(QUP):
                    copy_out(("qup", n, c), m["qm"][:, n, a:b], lambda ps: ps[:, 0:b - a])
            for g in range(H // 2):
                copy_out(("knT", g), m["kmT"][0:DH, 2 * g:2 * g + 2, :],
                         lambda ps: ps[0:DH, :].rearrange("p (e t) -> p e t", e=2))
            for n in range(NT):
                copy_out(("vm", n), m["vm"][:, n, :], lambda ps: ps[:, 0:W])
            for j in range(12, 16):
                gate(j)
            for n in range(NT):
                for c in range(2):
                    copy_out(("qmT", n, c), m["qmT"][0:DQK, 4 * c:4 * c + 4, n * P:(n + 1) * P],
                             lambda ps: ps[0:DQK, :].rearrange("p (h t) -> p h t", h=4))

            def expo(h):
                act.wait_ge(nmax.sem, h + 1)
                for n in range(NT):
                    w = (n + 1) * P
                    pr = m["probs"][:, h % SLOTS_P, n, 0:w]
                    last = nc.scalar.activation(pr, pr, ACT.Exp, bias=nmx[:, 2 * h + n:2 * h + n + 1],
                                                accum_out=den[:, 2 * h + n:2 * h + n + 1])
                last.then_inc(exped, 1)

            def y_hi(h):
                ps = bank.read(act, ("Y", h))
                r = slice(DH * (h % 2), DH * (h % 2) + DH)
                nc.scalar.activation(m["yT_hi"][r, h // H, h % H // 2, :], ps[0:DH, 0:T], ACT.Copy).then_inc(y_hi_ok, 1)

            def wb_hi(c):
                if c == 0:
                    act.wait_ge(wb_in, 32)
                    bank.read(act, ("S", 2 * H - 1))
                if c >= 2:
                    bank.read(act, ("br", c - 2))
                nc.scalar.activation(m["wb_hi"][:, c % 2].rearrange("p (b k) e -> p b k e", b=2),
                                     m["w_br"][:, :, :, c * P:(c + 1) * P], ACT.Copy).then_inc(wb_hi_ok, 1)

            expo(0)
            expo(1)
            for h in range(2 * H):
                if h + 2 < 2 * H:
                    expo(h + 2)
                else:
                    wb_hi(h + 2 - 2 * H)
                if h >= 2:
                    y_hi(h - 2)
                if h >= HEADS_AHEAD:
                    bank.read(act, ("Y", h - HEADS_AHEAD))
                copy_out(("PT", h), m["probsT"][:, h % HEADS_AHEAD].rearrange("p a b -> p (a b)"), lambda ps: ps[:, 0:3 * P])
            y_hi(2 * H - 2)
            y_hi(2 * H - 1)
            for c in range(2, KD):
                wb_hi(c)
            nc.scalar.activation(st[:, 17:18], ident[:, 0:1], ACT.Sqrt)
            bank.read(act, ("br", KD - 1))
            for b in range(FIRST):
                act.wait_ge(block_in[b], 16)
                nc.scalar.activation(m["b_hi"][:, b], m["b_raw"][:, b], ACT.Copy).then_inc(b_first_hi_ok, 1)
            for n in range(NT):
                act.wait_ge(var_ok, n + 1)
                nc.scalar.activation(st[:, 15:16], st[:, 14:15], ACT.Sqrt).then_inc(std_ok, 1)
            for j, (n, c) in enumerate(PAIRS):
                ps = bank.read(act, ("hT", n, c))
                nc.scalar.activation(m["h_hi"][:, 4 * c:4 * c + 4, n * P:(n + 1) * P],
                                     ps[:, :].rearrange("p (k t) -> p k t", t=P), ACT.Copy).then_inc(h_hi_ok, 1)

        @block.vector
        def _(dve):
            tmp = [m["scratch"][:, QLORA + KVLORA + i * T:QLORA + KVLORA + (i + 1) * T] for i in range(2)]

            def table(n, rot):
                o = C_ROPE + n * ROPE_W + (0 if rot == ROT else 2 * ROT)
                return m["consts"][:, o:o + 2 * rot]

            def temps(heads, rot):
                return [x[:, 0:heads * rot].rearrange("p (h d) -> p h d", d=rot) for x in tmp]

            def w_lo(c):
                dve.wait_ge(w_hi_ok, c)
                w = W_WIDTHS[c]
                nc.vector.tensor_tensor(m["wi_lo"][:, c % 2, :, 0:w], m["w_raw"][:, c % 2, :, 0:w],
                                        m["wi_hi"][:, c % 2, :, 0:w].bitcast(F32), ALU.subtract).then_inc(w_ok, 1)

            for i, half in enumerate(HALVES):
                dve.wait_ge(x_hi_ok, i + 1)
                nc.vector.tensor_tensor(m["x_lo"][:, half], m["xT"][:, half], m["x_hi"][:, half].bitcast(F32),
                                        ALU.subtract).then_inc(x_lo_ok, 1)
                dve.wait_ge(w_first_hi_ok, i + 1)
                nc.vector.tensor_tensor(m["wi_lo"][:, 0, half, 0:CHUNK], m["w_raw"][:, 0, half, 0:CHUNK],
                                        m["wi_hi"][:, 0, half, 0:CHUNK].bitcast(F32), ALU.subtract).then_inc(w_first_ok, 1)
            chunks = iter(range(1, n_chunks))
            for _ in range(V0 // CHUNK + 2):
                w_lo(next(chunks))
            dve.wait_ge(c_in, 16)
            for n in range(NT):
                for c in range(V0 // CHUNK):
                    bank.await_drained(dve, ("tok", c, n))
                qk = tok[:, n, 0:2 * W].rearrange("p (h d) -> p h d", d=DH)[:, :, 0:ROT]
                rope(nc, dve, dv, qk, qk, temps(2 * H, ROT), table(n, ROT), 2 * H, ROT, qk_roped)
                w_lo(next(chunks))
            for _ in range(2):
                w_lo(next(chunks))
            dve.wait_ge(ss_ready, 2 * NT)
            dv.done(nc.vector.tensor_scalar(ss[:, 0:NT], ss[:, 0:NT], 1.0 / QLORA, RMS_EPS, ALU.mult, ALU.add))
            dv.wait(dve)
            nc.vector.tensor_scalar(ss[:, NT:2 * NT], ss[:, NT:2 * NT], 1.0 / KVLORA, RMS_EPS,
                                    ALU.mult, ALU.add).then_inc(ms_ready, 1)
            dve.wait_ge(root_ready, 1)
            dv.done(nc.vector.reciprocal(rs, rs))
            dv.wait(dve)
            for n in range(NT):
                for base, w, col in ((CQ0, QLORA, n), (CKV0, KVLORA, NT + n)):
                    dv.done(nc.vector.tensor_scalar(tok[:, n, base:base + w], tok[:, n, base:base + w],
                                                    rs[:, col:col + 1], None, ALU.mult))
                bank.await_drained(dve, ("tok", TOK_CHUNKS - 1, n))
                kr = tok[:, n, KR0:KR0 + ROPE].unsqueeze(1)
                rope(nc, dve, dv, kr, kr, temps(1, ROPE), table(n, ROPE), 1, ROPE, lora_ready)
            w_lo(next(chunks))
            for which in ("qT", "kT"):
                for n in range(NT):
                    ps = bank.read(dve, (which, n))
                    bank.drain((which, n), nc.vector.tensor_copy(m[which][:, :, n * P:(n + 1) * P],
                                                                 ps[:, :].rearrange("p (k t) -> p k t", t=P)))
            for _ in range(2):
                w_lo(next(chunks))
            dve.wait_ge(b_in, 16)
            for which, K, col in (("cqT", QLORA // P, B_QN), ("ckvT", KVLORA // P, B_KVN)):
                for n in range(NT):
                    ps = bank.read(dve, (which, n))
                    gain = m["cols"][:, col:col + K].unsqueeze(2).to_broadcast([P, K, P])
                    bank.drain((which, n), nc.vector.tensor_tensor(
                        m[which][:, :, n * P:(n + 1) * P],
                        ps[:, 0:K * P].rearrange("p (k t) -> p k t", t=P), gain, ALU.mult))
            for c in chunks:
                w_lo(c)
            for n in range(NT):
                bank.await_drained(dve, ("qup", n, 0))
                bank.await_drained(dve, ("qup", n, 1))
                qr = m["qm"][:, n, 0:H * DQK].rearrange("p (h d) -> p h d", d=DQK)[:, :, DH:DQK]
                rope(nc, dve, dv, qr, qr, temps(H, ROPE), table(n, ROPE), H, ROPE, qm_roped)

            def mask_max(h):
                ps = bank.read(dve, ("S", h))
                if h >= SLOTS_P:
                    bank.read(dve, ("PT", h - SLOTS_P))
                for n in range(NT):
                    w = (n + 1) * P
                    mask = m["consts"][:, C_MASK + (NT - 1 - n) * P:C_MASK + T]
                    c = 2 * h + n
                    last = nc.vector.tensor_tensor_reduce(
                        out=m["probs"][:, h % SLOTS_P, n, 0:w], in0=ps[:, n * P:n * P + w], in1=mask, scale=scales[h],
                        scalar=LOWEST, op0=ALU.add, op1=ALU.max, accum_out=mx[:, c:c + 1])
                bank.drain(("S", h), last)
                bank.await_drained(dve, ("S", h))
                nmax.done(nc.vector.tensor_scalar(nmx[:, 2 * h:2 * h + 2], mx[:, 2 * h:2 * h + 2], -1.0, None, ALU.mult))

            def normalise(h):
                dve.wait_ge(exped, h + 1)
                dv.done(nc.vector.reciprocal(rden[:, 2 * h:2 * h + 2], den[:, 2 * h:2 * h + 2]))
                dv.wait(dve)
                for n in range(NT):
                    pr = m["probs"][:, h % SLOTS_P, n, 0:(n + 1) * P]
                    last = nc.vector.tensor_scalar(pr, pr, rden[:, 2 * h + n:2 * h + n + 1], None, ALU.mult)
                probs_ok.done(last)

            def keep_y(h):
                ps = bank.read(dve, ("Y", h))
                r = slice(DH * (h % 2), DH * (h % 2) + DH)
                dve.wait_ge(y_hi_ok, h + 1)
                bank.drain(("Y", h), nc.vector.tensor_tensor(
                    m[f"yT_lo{h // H}"][r, h % H // 2, :], ps[0:DH, 0:T],
                    m["yT_hi"][r, h // H, h % H // 2, :].bitcast(F32), ALU.subtract))

            def wb_lo(c):
                dve.wait_ge(wb_hi_ok, c + 1)
                nc.vector.tensor_tensor(m["wb_lo"][:, c % 2].rearrange("p (b k) e -> p b k e", b=2),
                                        m["w_br"][:, :, :, c * P:(c + 1) * P],
                                        m["wb_hi"][:, c % 2].bitcast(F32).rearrange("p (b k) e -> p b k e", b=2),
                                        ALU.subtract).then_inc(wb_ok, 1)

            for h in range(HEADS_AHEAD):
                mask_max(h)
            for h in range(2 * H):
                normalise(h)
                if h + HEADS_AHEAD < 2 * H:
                    mask_max(h + HEADS_AHEAD)
                if h >= 2:
                    keep_y(h - 2)
            wb_lo(0)
            keep_y(2 * H - 2)
            keep_y(2 * H - 1)
            wb_lo(1)
            for j in range(2 * KD):
                bank.await_drained(dve, ("gate", j))
            for c in range(KD):
                ps = bank.read(dve, ("br", c))
                t = m["probs"][:, c % 2]
                bank.drain(("br", c), nc.vector.tensor_tensor(t, ps[:, :].rearrange("p (b t) -> p b t", b=2),
                                                              m["sigT"][:, :, c, :], ALU.mult))
                if c + 2 < KD:
                    wb_lo(c + 2)
                bank.await_drained(dve, ("br", c))
                merged_ok.done(nc.vector.tensor_tensor(m["mergedT"][:, c, :], t[:, 0, :], t[:, 1, :], ALU.add))
            merged_ok.wait(dve)
            for b in range(FIRST):
                dve.wait_ge(b_first_hi_ok, b + 1)
                nc.vector.tensor_tensor(m["b_lo"][:, b], m["b_raw"][:, b], m["b_hi"][:, b].bitcast(F32),
                                        ALU.subtract).then_inc(b_first_ok, 1)
            dve.wait_ge(xt_in, 16)
            dve.wait_ge(ln_in, 32)
            for n in range(NT):
                z = m["x_tok"][:, n, :]
                for c in range(2):
                    ps = bank.read(dve, ("mix", n, c))
                    zc = z[:, c * 512:(c + 1) * 512]
                    bank.drain(("mix", n, c), nc.vector.scalar_tensor_tensor(
                        out=zc, in0=zc, scalar=ALPHA, in1=ps[:, :], op0=ALU.mult, op1=ALU.add))
                    bank.await_drained(dve, ("mix", n, c))
                    half_stats(nc, dv, st, z, c)
                layer_norm(nc, dve, dv, st, z, m["h"][:, n, :], m["ln1"][:, 0, :], m["ln1"][:, 1, :],
                           var_ok, std_ok, n, h_ok)
            for j, (n, c) in enumerate(PAIRS):
                dve.wait_ge(h_hi_ok, j + 1)
                ps = bank.read(dve, ("hT", n, c))
                t = slice(n * P, (n + 1) * P)
                bank.drain(("hT", n, c), nc.vector.tensor_tensor(
                    m["h_lo"][:, 4 * c:4 * c + 4, t], ps[:, :].rearrange("p (k t) -> p k t", t=P),
                    m["h_hi"][:, 4 * c:4 * c + 4, t].bitcast(F32), ALU.subtract))


def split_product(nc, out, w_hi, w_lo, x_hi, x_lo):
    for k in range(KD):
        nc.tensor.matmul(out, w_hi[:, k, :], x_hi[:, k, :], start=(k == 0), stop=False)
        nc.tensor.matmul(out, w_hi[:, k, :], x_lo[:, k, :], start=False, stop=False)
        last = nc.tensor.matmul(out, w_lo[:, k, :], x_hi[:, k, :], start=False, stop=(k == KD - 1))
    return last


def route(nc, io, m, bank, b_in, v_in):
    consts = m["consts"]
    ident, iota = consts[:, C_ID:C_ID + P], consts[:, C_IOTA:C_IOTA + NK]
    iota16 = m["iota16"][:]
    GT = 4
    RINGS = 2
    RAW, RING = BLOCKS, 4
    BODY = RINGS * OHT
    BANKS = BODY // GT

    with ExitStack() as ctx:
        def sem(name):
            return ctx.enter_context(nc.semaphore(name))

        subk_in = sem("sub_keys_in")
        exp_ok = sem("gate_exp_ready")
        b_hi_ok = sem("block_hi_ready")
        b_ok = sem("block_split")
        b_done = sem("block_done")
        a_gelu = sem("ahead_gelu")
        oh1_ok = sem("onehot1_ready")
        oh_ready = sem("onehot_ready")
        g_full = sem("g_bank_full")
        g_free = sem("g_bank_free")
        dv = Steps(ctx, nc, "route_dve")
        plain1_ok, plain2_ok = sem("onehot1_plain"), sem("onehot2_plain")
        exp_in = Steps(ctx, nc, "gate_exp_in")
        slot_ok = Steps(ctx, nc, "gates_ready")
        keys_ok = Steps(ctx, nc, "key_numbers_ready")
        block = ctx.enter_context(nc.Block())

        @block.sync
        def _(sp):
            def load(src, base):
                def step(b, s):
                    sp.wait_ge(b_ok, b + base + 1)
                    sp.dma_start(m["b_raw"][:, s % RAW], src[bass.ds(b, 1)].rearrange("o p k e -> (o p) k e")
                                 ).then_inc(b_in[s % RAW], 16)
                return step

            sp.dma_start(m["subk"][:], io["subkT"].rearrange("h d n -> d h n")).then_inc(subk_in, 16)
            over(sp, FIRST + RAW, HP, load(io["peer_wqT"], 0))
            over(sp, 0, AHEAD, load(io["uT"], HP))
            sp.wait_ge(oh1_ok, T // OHT + RINGS)
            sp.dma_start(m["v_raw"][:, 0], io["v"][0]).then_inc(v_in[0], 16)

        @block.gpsimd
        def _(pool):
            def split_lo(b, s):
                pool.wait_ge(b_hi_ok, b + 1)
                pool.wait_ge(b_done, b + 1)
                nc.gpsimd.tensor_tensor(m["b_lo"][:, s % RING], m["b_raw"][:, s % RAW],
                                        m["b_hi"][:, s % RING].bitcast(F32), ALU.subtract).then_inc(b_ok, 1)

            over(pool, FIRST, HP + AHEAD, split_lo)

        @block.tensor
        def _(pe):
            def product(b, s, out):
                if not (isinstance(b, int) and b < FIRST):
                    pe.wait_ge(b_ok, b + 1 + RAW)
                return split_product(nc, out, m["b_hi"][:, s % RING], m["b_lo"][:, s % RING], m["h_hi"], m["h_lo"])

            def similarities(c):
                if c == 0:
                    pe.wait_ge(subk_in, 16)
                for i in range(4):
                    bank.await_drained(pe, ("pq", 4 * c + i))
                for n in range(NT):
                    ps = bank.fill(pe, ("sim", n, c))
                    for i in range(4):
                        hp = 4 * c + i
                        last = nc.tensor.matmul(ps[:, i * NK:(i + 1) * NK], m["pqT"][:, hp, n * P:(n + 1) * P],
                                                m["subk"][:, hp, :], start=True, stop=True)
                    bank.filled(("sim", n, c), last)

            for hp in range(HP):
                bank.filled(("pq", hp), product(hp, hp, bank.fill(pe, ("pq", hp))[:, 0:T]))
                if hp in SIMS_AFTER:
                    similarities(SIMS_AFTER[hp])
            similarities(3)
            spare = [len(bank.order) + n for n in range(2)]
            for n in range(2):
                name = bank.order[spare[n] - 8]
                bank.await_drained(pe, name)

            def activations(b, s):
                pe.wait_ge(a_gelu, b + 1)
                product(b + HP, s, bank.psum[spare[s % 2] % 8][:, 0:T]).then_inc(b_done, 1)

            over(pe, 0, AHEAD, activations)
            pe.wait_ge(a_gelu, AHEAD + 2)
            for w in range(3):
                if w < 2:
                    pe.wait_ge(keys_ok.sem, 2)
                else:
                    pe.wait_ge(slot_ok.sem, 1)
                ps = bank.fill(pe, ("slotT", w))
                for n in range(NT):
                    last = nc.tensor.transpose(ps[:, n * P:(n + 1) * P], m["slot"][:, w, n, :], ident)
                bank.filled(("slotT", w), last)
            for w in range(3):
                bank.await_drained(pe, ("slotT", w))
            with pe.Fori(0, T // BODY) as i:
                for g in range(BANKS):
                    pe.wait_ge(g_free, i * BANKS + g + 1)
                    slot, t0 = g * GT // OHT, g * GT % OHT
                    if t0 == 0:
                        pe.wait_ge(oh1_ok, i * RINGS + RINGS + slot + 1)
                        pe.wait_ge(oh_ready, i * RINGS + RINGS + slot + 1)
                    for j in range(GT):
                        last = nc.tensor.matmul(bank.psum[g][:, j * NK:(j + 1) * NK], m["oh2"][:, slot, t0 + j, :],
                                                m["oh1"][:, slot, t0 + j, :], start=True, stop=True)
                    last.then_inc(g_full, 1)

        @block.scalar
        def _(act):
            act.sem_inc(b_hi_ok, FIRST)
            act.sem_inc(b_ok, RAW + FIRST)
            act.sem_inc(b_done, RING)
            act.sem_inc(a_gelu, 2)

            def split_hi(b, s):
                act.wait_ge(b_in[s % RAW], b * 4 + (16 - 4 * (s % RAW)))
                act.wait_ge(b_done, b + 1)
                nc.scalar.activation(m["b_hi"][:, s % RING], m["b_raw"][:, s % RAW], ACT.Copy).then_inc(b_hi_ok, 1)

            def keep_sims(c):
                for n in range(NT):
                    ps = bank.read(act, ("sim", n, c))
                    bank.drain(("sim", n, c), nc.scalar.activation(
                        m["sims"][:, n, 4 * c:4 * c + 4, :], ps[:, :].rearrange("p (i k) -> p i k", k=NK), ACT.Copy))

            LEAD = FIRST - 1
            for hp in range(HP):
                if hp:
                    split_hi(hp + LEAD, hp + LEAD)
                ps = bank.read(act, ("pq", hp))
                act.sem_inc(b_done, 1)
                bank.drain(("pq", hp), nc.scalar.activation(m["pqT"][:, hp, :], ps[:, 0:T], ACT.Copy))
                if hp in SIMS_AFTER:
                    keep_sims(SIMS_AFTER[hp])
            keep_sims(3)

            def gelu(b, s):
                act.wait_ge(b_done, b + HP + 1 + RING)
                nc.scalar.activation(made_ahead(m, b),
                                     bank.psum[(len(bank.order) + s % 2) % 8][:, 0:T],
                                     ACT.Gelu).then_inc(a_gelu, 1)

            over(act, 0, AHEAD - LEAD, lambda b, s: (split_hi(b + HP + LEAD, s + LEAD), gelu(b, s)))
            for b in range(AHEAD - LEAD, AHEAD):
                gelu(b, b)
            nc.scalar.activation(m["small"][:, 156:157], ident[:, 0:1], ACT.Exp)
            act.wait_ge(exp_in.sem, 1)
            nc.scalar.activation(m["ex"][:], m["ex"][:], ACT.Exp).then_inc(exp_ok, 1)
            for w in range(3):
                bank.await_drained(act, ("slotT", w))
            act.sem_inc(g_free, BANKS)
            act.sem_inc(g_full, BANKS)
            act.sem_inc(oh1_ok, RINGS)
            act.sem_inc(oh_ready, RINGS)

            def widen(j, s):
                act.wait_ge(plain1_ok, j + 1)
                act.wait_ge(g_full, j * (OHT // GT) + OHT // GT)
                nc.scalar.activation(m["oh1"][:, s % RINGS], m["oh1_plain"][:, s % RINGS].rearrange("p k t -> p t k"),
                                     ACT.Copy).then_inc(oh1_ok, 1)

            def store(j, s):
                for g in range(OHT // GT):
                    act.wait_ge(g_full, j * (OHT // GT) + BANKS + g + 1)
                    nc.scalar.activation(m["G"][:, :, bass.ds(j * OHT + GT * g, GT)],
                                         bank.psum[(s % RINGS) * (OHT // GT) + g][:, :].rearrange("p (t i) -> p i t", t=GT),
                                         ACT.Copy).then_inc(g_free, 1)

            last = T // OHT - 1
            widen(0, 0)
            over(act, 0, last, lambda j, s: (widen(j + 1, s + 1), store(j, s)), unroll=RINGS)
            store(last, last)

        @block.vector
        def _(dve):
            def top16(rows):
                for src, _, vals, _ in rows:
                    dv.done(nc.vector.max(vals[:, 0:8], src))
                dv.wait(dve)
                for src, scratch, vals, idx in rows:
                    dv.done(nc.vector.max_index(idx[:, 0:8], vals[:, 0:8], src))
                    dv.done(nc.vector.match_replace(scratch, vals[:, 0:8], src, LOWEST))
                dv.wait(dve)
                for _, scratch, vals, _ in rows:
                    dv.done(nc.vector.max(vals[:, 8:16], scratch))
                dv.wait(dve)
                for _, scratch, vals, idx in rows:
                    dv.done(nc.vector.max_index(idx[:, 8:16], vals[:, 8:16], scratch))
                dv.wait(dve)

            dv.done(nc.vector.tensor_copy(iota16, iota[:, 0:TK]))
            dv.done(nc.vector.tensor_copy(m["iota_t"][:], iota.unsqueeze(2).to_broadcast([P, NK, OHT])))
            heads = [P, NT * PH, TK]
            all_best, ex = (m[x][:].rearrange("p n h k -> p (n h) k") for x in ("best", "ex"))
            total, inverse = (m["pstat"][:, j].rearrange("p n h -> p (n h)") for j in range(2))
            for c in range(4):
                for n in range(NT):
                    bank.await_drained(dve, ("sim", n, c))
                    tv, ti, tf = (m[x][:, n, 4 * c:4 * c + 4, :] for x in ("topv", "topi", "topf"))
                    best, bpos = (m[x][:, n, 2 * c:2 * c + 2, :] for x in ("best", "bpos"))
                    top16([(m["sims"][:, n, 4 * c + i, :], m["sims2"][:, i, :], tv[:, i, :], ti[:, i, :])
                           for i in range(4)])
                    dv.done(nc.vector.tensor_copy(tf, ti))
                    tv4 = tv.rearrange("p (h e) k -> p h e k", e=2)
                    dv.done(nc.vector.tensor_tensor(
                        m["cand"][:].rearrange("p h (a b) -> p h a b", a=TK),
                        tv4[:, :, 0, :].unsqueeze(3).to_broadcast([P, 2, TK, TK]),
                        tv4[:, :, 1, :].unsqueeze(2).to_broadcast([P, 2, TK, TK]), ALU.add))
                    dv.wait(dve)
                    top16([(m["cand"][:, i, :], m["cand2"][:, i, :], best[:, i, :], bpos[:, i, :]) for i in range(2)])
                    final = c == 3 and n == NT - 1
                    if final:
                        exp_in.done(nc.vector.tensor_tensor(ex, all_best, all_best[:, :, 0:1].to_broadcast(heads),
                                                            ALU.subtract))
                    pos = bpos.rearrange("p h k -> p (h k)")
                    dv.done(nc.vector.tensor_scalar(m["bab"][:, 0, :], pos, 4, None, ALU.logical_shift_right))
                    dv.done(nc.vector.tensor_scalar(m["bab"][:, 1, :], pos, TK - 1, None, ALU.bitwise_and))
                    dv.wait(dve)
                    dv.done(nc.vector.tensor_copy(m["babf"][:], m["bab"][:]))
                    dv.wait(dve)
                    q = SLOTS // 4
                    tf4 = tf.rearrange("p (h e) k -> p h e k", e=2)
                    for e in range(2):
                        dv.done(nc.vector.tensor_tensor(
                            m["eq"][:, e], m["babf"][:, e, :].unsqueeze(2).to_broadcast([P, q, TK]),
                            iota16.unsqueeze(1).to_broadcast([P, q, TK]), ALU.is_equal))
                    dv.wait(dve)
                    for e in range(2):
                        eq4 = m["eq"][:, e].rearrange("p (h k) a -> p h k a", h=2)
                        dv.done(nc.vector.tensor_tensor(
                            eq4, eq4, tf4[:, :, e, :].unsqueeze(2).to_broadcast([P, 2, TK, TK]), ALU.mult))
                    dv.wait(dve)
                    for e in range(2):
                        (keys_ok if final else dv).done(nc.vector.tensor_reduce(m["slot"][:, e, n, c * q:(c + 1) * q], m["eq"][:, e],
                                                        AX_X, ALU.add))
            dve.wait_ge(exp_ok, 1)
            dv.done(nc.vector.tensor_reduce(total, ex, AX_X, ALU.add))
            dv.wait(dve)
            dv.done(nc.vector.reciprocal(inverse, total))
            dv.wait(dve)
            slot_ok.done(nc.vector.tensor_tensor(m["slot"][:, 2].rearrange("p n (h k) -> p (n h) k", h=PH), ex,
                                                 inverse.unsqueeze(2).to_broadcast(heads), ALU.mult))
            for w, dst in enumerate((m["keys"][:, 0, :], m["keys"][:, 1, :], m["gateT"][:])):
                ps = bank.read(dve, ("slotT", w))
                bank.drain(("slotT", w), nc.vector.tensor_copy(dst, ps[:, 0:T]))
            for w in range(3):
                bank.await_drained(dve, ("slotT", w))
            rows = [P, NK, OHT]
            with dve.Fori(0, T // BODY) as i:
                for s in range(RINGS):
                    t = bass.ds(i * BODY + s * OHT, OHT)
                    dve.wait_ge(oh_ready, i * RINGS + s + 1)
                    nc.vector.tensor_tensor(m["oh2_plain"][:, s], m["iota_t"][:],
                                            m["keys"][:, 1, t].unsqueeze(1).to_broadcast(rows),
                                            ALU.is_equal).then_inc(plain2_ok, 1)
                    dve.wait_ge(oh1_ok, i * RINGS + s + 1)
                    nc.vector.tensor_tensor(m["oh1_plain"][:, s], m["iota_t"][:],
                                            m["keys"][:, 0, t].unsqueeze(1).to_broadcast(rows),
                                            ALU.is_equal).then_inc(plain1_ok, 1)
                    dve.wait_ge(plain2_ok, i * RINGS + s + 1)
                    dve.wait_ge(g_full, i * BANKS + (s + 1) * (OHT // GT))
                    nc.vector.tensor_tensor(m["oh2"][:, s], m["oh2_plain"][:, s].rearrange("p k t -> p t k"),
                                            m["gateT"][:, t].unsqueeze(2).to_broadcast([P, OHT, NK]),
                                            ALU.mult).then_inc(oh_ready, 1)


def experts(nc, io, m, bank, v_in):
    acts = [bank.psum[b][:, 0:T] for b in range(4)]
    prods = [bank.psum[b][:, T:2 * T] for b in range(4)]
    out = [[bank.psum[4 + 2 * n + c] for c in range(2)] for n in range(NT)]
    BANKS = 4
    RING = 2
    HI_OVER = 2 * RING * KD * P // T
    DEEP = 2 * 4 * D // T // 4

    with ExitStack() as ctx:
        def sem(name):
            return ctx.enter_context(nc.semaphore(name))

        u_in = [sem(f"u_slot{k}") for k in range(RING)]
        v_deep_in = [sem(f"v_deep_slot{k}") for k in range(4)]
        v_late_in = [sem(f"v_late_slot{k}") for k in range(2)]
        u_hi_ok, v_hi_ok = sem("u_hi_ready"), sem("v_hi_ready")
        u_ok, v_ok = sem("u_split"), sem("v_split")
        gelu_ok, prod_ok, w_hi_ok = sem("gelu_ready"), sem("gated_ready"), sem("w_hi_ready")
        w_ok = sem("w_split")
        uh_done, wv_done = sem("uh_done"), sem("wv_done")
        tail_in = sem("tail_operands_in")
        gate_in = sem("w_ple_gate_in")
        gate_hi_ok = sem("w_ple_gate_hi")
        SLICES = 75
        SPLITS = SLICES + BANKS
        block = ctx.enter_context(nc.Block())

        def loads(b, s):
            return b * 8 + (16 - 8 * (s % 2))

        def v_early(b, s):
            return m["v_raw"][:, s % 2], v_in[s % 2], loads(b, s)

        def v_deep(b, s):
            slot = m["v_raw"][:, s % 4] if s % 4 < 2 else m["v_deep"][:, s % 4 - 2]
            return slot, v_deep_in[s % 4], (b - DEEP) * 4 + (16 - 4 * (s % 4))

        def v_late(b, s):
            return m["v_raw"][:, s % 2], v_late_in[s % 2], loads(b - (AHEAD - 1), s - (AHEAD - 1))

        @block.sync
        def _(sp):
            def load_v(b, s, where):
                slot, arrived, _ = where(b, s)
                sp.dma_start(slot, io["v"][bass.ds(b, 1)].rearrange("o p d -> (o p) d")).then_inc(arrived, 16)

            def load_v2(b, s, where):
                sp.wait_ge(v_ok, b + 1)
                load_v(b, s, where)

            def load_v4(b, s):
                sp.wait_ge(v_ok, b - 4 + 1 + RING)
                load_v(b, s, v_deep)

            def load_u(b, s):
                sp.wait_ge(u_ok, b - AHEAD + 1)
                sp.dma_start(m["u_raw"][:, s % RING], io["uT"][bass.ds(b, 1)].rearrange("o p k e -> (o p) k e")
                             ).then_inc(u_in[s % RING], 16)

            def load(b, s):
                load_v2(b, s, v_late)
                load_u(b + 2, s + 2)

            for b in range(1, DEEP):
                load_v2(b, b, v_early)
            for b in range(DEEP, DEEP + 2):
                load_v2(b, b, v_deep)
            sp.wait_ge(prod_ok, DEEP)
            for b in range(DEEP + 2, DEEP + 4):
                load_v(b, b, v_deep)
            load_u(AHEAD, AHEAD)
            over(sp, DEEP + 4, AHEAD - 1, load_v4)
            over(sp, AHEAD - 1, SLICES, load)
            w_g = io["w_ple_gate"].rearrange("(k p) c -> p k c", p=P)
            sp.sem_inc(gate_in, 16)
            with sp.Fori(0, KD) as i:
                for r in range(BANKS):
                    load(i * BANKS + (SLICES + r), SLICES + r)
                sp.wait_ge(gate_in, i * 16 + 16)
                sp.dma_start(m["w_g_raw"][:, bass.ds(i, 1), :], w_g[:, bass.ds(i, 1), :]).then_inc(gate_in, 16)
            after = SLICES + KD * BANKS
            over(sp, after, after + BANKS, load)
            sp.dma_start(m["w_ple_proj"][:], io["w_ple_proj"].rearrange("(k p) c -> p k c", p=P)).then_inc(tail_in, 16)
            sp.dma_start(m["pT"][:], io["pT"].rearrange("(k p) t -> p k t", p=P)).then_inc(tail_in, 16)
            over(sp, after + BANKS, NK - 2, load)
            for j, w in enumerate(("b_ple_gate", "ln2_g", "ln2_b")):
                sp.dma_start(m["rows"][:, j, :], io[w].partition_broadcast(P)).then_inc(tail_in, 16)
            for b in range(NK - 2, NK):
                load_v2(b, b, v_late)
            sp.wait_ge(tail_in, 16 * 5)

        @block.tensor
        def _(pe):
            def activations(b, s):
                pe.wait_ge(u_ok, b - AHEAD + 1 + RING)
                pe.wait_ge(w_ok, b + 1)
                split_product(nc, acts[s % BANKS], m["u_hi"][:, s % RING], m[f"u_lo{s % RING}"],
                              m["h_hi"], m["h_lo"]).then_inc(uh_done, 1)

            def values(b, s):
                first = isinstance(b, int) and b == 0
                v = s % RING
                pe.wait_ge(v_hi_ok, b + 1)
                pe.wait_ge(w_hi_ok, b + 1)
                for w, x, start, tiles in (("w_hi", "v_hi", first, (0, 1)), ("w_hi", "v_lo", False, (1, 0)),
                                           ("w_lo", "v_hi", False, (0, 1))):
                    if x == "v_lo":
                        pe.wait_ge(v_ok, b + 1 + RING)
                    if w == "w_lo":
                        pe.wait_ge(w_ok, b + 1 + BANKS)
                    for n in tiles:
                        for c in range(2):
                            last = nc.tensor.matmul(out[n][c][:, :], m[w][:, v, n * P:(n + 1) * P],
                                                    m[x][:, v, c * 512:(c + 1) * 512],
                                                    start=start, stop=False, skip_group_check=True)
                last.then_inc(wv_done, 1)

            for b in range(3):
                values(b, b)
            over(pe, 3, AHEAD - 1, values)
            over(pe, AHEAD - 1, NK - 1, lambda b, s: (activations(b + 1, s + 1), values(b, s)))
            values(NK - 1, NK - 1)

        @block.scalar
        def _(act):
            for free, depth in ((u_ok, RING), (v_ok, RING), (uh_done, RING), (wv_done, RING), (w_ok, BANKS)):
                act.sem_inc(free, depth)

            def u_hi(b, s):
                act.wait_ge(u_in[s % RING], loads(b - AHEAD, s))
                act.wait_ge(uh_done, b - AHEAD + 1)
                nc.scalar.activation(m["u_hi"][:, s % RING], m["u_raw"][:, s % RING], ACT.Copy).then_inc(u_hi_ok, 1)

            def gelu(b, s):
                act.wait_ge(uh_done, b - AHEAD + 1 + RING)
                nc.scalar.activation(acts[s % BANKS], acts[s % BANKS], ACT.Gelu).then_inc(gelu_ok, 1)

            def v_and_w_hi(b, s, where=v_late):
                raw, arrived, count = where(b, s)
                act.wait_ge(arrived, count)
                act.wait_ge(wv_done, b + 1)
                nc.scalar.activation(m["v_hi"][:, s % RING], raw, ACT.Copy).then_inc(v_hi_ok, 1)
                act.wait_ge(prod_ok, b + 1)
                nc.scalar.activation(m["w_hi"][:, s % RING], prods[s % BANKS], ACT.Copy).then_inc(w_hi_ok, 1)

            over(act, 0, DEEP, lambda b, s: v_and_w_hi(b, s, v_early))
            over(act, DEEP, AHEAD_LOW, lambda b, s: v_and_w_hi(b, s, v_deep))
            act.wait_ge(prod_ok, HI_OVER)
            u_hi(AHEAD, AHEAD)
            for b in range(AHEAD_LOW, AHEAD - 1):
                v_and_w_hi(b, b, v_deep)
            v_and_w_hi(AHEAD - 1, AHEAD - 1)
            def step(b, s):
                u_hi(b + 1, s + 1)
                gelu(b, s)
                v_and_w_hi(b, s)

            over(act, AHEAD, SPLITS, step)
            with act.Fori(0, KD) as i:
                for r in range(BANKS):
                    step(i * BANKS + (SPLITS + r), SPLITS + r)
                act.wait_ge(gate_in, i * 16 + 32)
                nc.scalar.activation(m["w_g_hi"][:, bass.ds(i, 1), :], m["w_g_raw"][:, bass.ds(i, 1), :],
                                     ACT.Copy).then_inc(gate_hi_ok, 1)
            over(act, SPLITS + KD * BANKS, NK - 1, step)
            gelu(NK - 1, NK - 1)
            v_and_w_hi(NK - 1, NK - 1)

        @block.vector
        def _(dve):
            def u_lo(b, s):
                dve.wait_ge(u_hi_ok, b - AHEAD + 1)
                dve.wait_ge(uh_done, b - AHEAD + 1)
                nc.vector.tensor_tensor(m[f"u_lo{s % RING}"][:], m["u_raw"][:, s % RING],
                                        m["u_hi"][:, s % RING].bitcast(F32), ALU.subtract).then_inc(u_ok, 1)

            def gated(b, s, a):
                nc.vector.tensor_tensor(prods[s % BANKS], a, m["G"][:, bass.ds(b, 1), :].rearrange("p o t -> p (o t)"),
                                        ALU.mult).then_inc(prod_ok, 1)

            def v_and_w_lo(b, s, where=v_late):
                v = s % RING
                dve.wait_ge(v_hi_ok, b + 1)
                nc.vector.tensor_tensor(m["v_lo"][:, v], where(b, s)[0], m["v_hi"][:, v].bitcast(F32),
                                        ALU.subtract).then_inc(v_ok, 1)
                dve.wait_ge(w_hi_ok, b + 1)
                nc.vector.tensor_tensor(m["w_lo"][:, v], prods[s % BANKS], m["w_hi"][:, v].bitcast(F32),
                                        ALU.subtract).then_inc(w_ok, 1)

            def step_ahead(b, s, where):
                gated(b, s, made_ahead(m, b))
                v_and_w_lo(b, s, where)

            def step(b, s):
                dve.wait_ge(gelu_ok, b - AHEAD + 1)
                gated(b, s, acts[s % BANKS])
                v_and_w_lo(b, s)

            def with_u(b, s):
                u_lo(b + 1, s + 1)
                step(b, s)

            over(dve, 0, DEEP, lambda b, s: step_ahead(b, s, v_early))
            over(dve, DEEP, AHEAD_LOW, lambda b, s: step_ahead(b, s, v_deep))
            dve.wait_ge(prod_ok, AHEAD_LOW)
            u_lo(AHEAD, AHEAD)
            for b in range(AHEAD_LOW, AHEAD - 1):
                step_ahead(b, b, v_deep)
            gated(AHEAD - 1, AHEAD - 1, made_ahead(m, AHEAD - 1))
            dve.wait_ge(prod_ok, AHEAD)
            v_and_w_lo(AHEAD - 1, AHEAD - 1)
            over(dve, AHEAD, SPLITS, with_u)
            with dve.Fori(0, KD) as i:
                for r in range(BANKS):
                    with_u(i * BANKS + (SPLITS + r), SPLITS + r)
                dve.wait_ge(gate_hi_ok, i + 1)
                k = bass.ds(i, 1)
                nc.vector.tensor_tensor(m["w_g_lo"][:, k, :], m["w_g_raw"][:, k, :],
                                        m["w_g_hi"][:, k, :].bitcast(F32), ALU.subtract)
            over(dve, SPLITS + KD * BANKS, NK - 1, with_u)
            step(NK - 1, NK - 1)


def tail(nc, io, m, bank):
    ident = m["consts"][:, C_ID:C_ID + P]
    st = m["small"][:, 136:160]
    psum = bank.psum

    with ExitStack() as ctx:
        def sem(name):
            return ctx.enter_context(nc.semaphore(name))

        proj_full = sem("ple_proj_full")
        rT_full, gate_full = sem("rT_full"), sem("ple_gate_full")
        rT_hi_ok, rT_lo_ok = sem("rT_hi_ready"), sem("rT_lo_ready")
        sig_ok, out_done = sem("ple_sigmoid"), sem("out_written")
        var_ok, std_ok = sem("var2_ready"), sem("std2_ready")
        dv = Steps(ctx, nc, "tail_dve")
        r_ok = Steps(ctx, nc, "r_ready")
        logit_ok = Steps(ctx, nc, "ple_logits")
        y_ok = Steps(ctx, nc, "y_ready")
        block = ctx.enter_context(nc.Block())
        pairs = [(n, c) for n in range(NT) for c in range(2)]
        halves = [slice(c * 512, (c + 1) * 512) for c in range(2)]

        @block.tensor
        def _(pe):
            for j, (n, c) in enumerate(pairs):
                pe.wait_ge(r_ok.sem, j + 1)
                for i in range(4):
                    last = nc.tensor.transpose(psum[j][:, i * P:(i + 1) * P],
                                               m["r"][:, n, (4 * c + i) * P:(4 * c + i + 1) * P], ident)
                last.then_inc(rT_full, 1)
            for j, (n, c) in enumerate(pairs):
                for k in range(PLE // P):
                    last = nc.tensor.matmul(psum[4 + j][:, :], m["pT"][:, k, n * P:(n + 1) * P],
                                            m["w_ple_proj"][:, k, halves[c]], start=(k == 0), stop=(k == PLE // P - 1))
                last.then_inc(proj_full, 1)
            for j, (n, c) in enumerate(pairs):
                pe.wait_ge(rT_lo_ok, 2 * (n + 1))
                t = slice(n * P, (n + 1) * P)
                for k in range(KD):
                    nc.tensor.matmul(psum[j][:, :], m["rT_hi"][:, k, t], m["w_g_hi"][:, k, halves[c]],
                                     start=(k == 0), stop=False)
                    nc.tensor.matmul(psum[j][:, :], m["rT_hi"][:, k, t], m["w_g_lo"][:, k, halves[c]],
                                     start=False, stop=False)
                    last = nc.tensor.matmul(psum[j][:, :], m["rT_lo"][:, k, t], m["w_g_hi"][:, k, halves[c]],
                                            start=False, stop=(k == KD - 1))
                last.then_inc(gate_full, 1)

        @block.scalar
        def _(act):
            for j, (n, c) in enumerate(pairs):
                act.wait_ge(rT_full, j + 1)
                nc.scalar.activation(m["rT_hi"][:, 4 * c:4 * c + 4, n * P:(n + 1) * P],
                                     psum[j][:, :].rearrange("p (k t) -> p k t", t=P), ACT.Copy).then_inc(rT_hi_ok, 1)
            for n in range(NT):
                for c in range(2):
                    act.wait_ge(logit_ok.sem, 2 * n + c + 1)
                    x = m["sig"][:, n, halves[c]]
                    nc.scalar.activation(x, x, ACT.Sigmoid).then_inc(sig_ok, 1)
                if n == NT - 1:
                    nc.scalar.activation(st[:, 18:19], ident[:, 0:1], ACT.Sqrt)
                act.wait_ge(var_ok, n + 1)
                nc.scalar.activation(st[:, 15:16], st[:, 14:15], ACT.Sqrt).then_inc(std_ok, 1)

        @block.vector
        def _(dve):
            for j, (n, c) in enumerate(pairs):
                r_ok.done(nc.vector.scalar_tensor_tensor(out=m["r"][:, n, halves[c]], in0=m["h"][:, n, halves[c]],
                                                         scalar=ALPHA, in1=psum[4 + j][:, :],
                                                         op0=ALU.mult, op1=ALU.add))
            for j, (n, c) in enumerate(pairs):
                dve.wait_ge(rT_hi_ok, j + 1)
                hi = m["rT_hi"][:, 4 * c:4 * c + 4, n * P:(n + 1) * P]
                nc.vector.tensor_tensor(m["rT_lo"][:, 4 * c:4 * c + 4, n * P:(n + 1) * P],
                                        psum[j][:, :].rearrange("p (k t) -> p k t", t=P), hi.bitcast(F32),
                                        ALU.subtract).then_inc(rT_lo_ok, 1)
            r_ok.wait(dve)
            for n in range(NT):
                for c in range(2):
                    j = 2 * n + c
                    z = m["z"][:, n, halves[c]]
                    dve.wait_ge(gate_full, j + 1)
                    logit_ok.done(nc.vector.tensor_tensor(m["sig"][:, n, halves[c]], psum[j][:, :],
                                                          m["rows"][:, 0, halves[c]], ALU.add))
                    dve.wait_ge(proj_full, j + 1)
                    dve.wait_ge(sig_ok, j + 1)
                    dv.done(nc.vector.tensor_tensor(z, m["sig"][:, n, halves[c]], psum[4 + j][:, :], ALU.mult))
                    dv.wait(dve)
                    dv.done(nc.vector.tensor_tensor(z, z, m["r"][:, n, halves[c]], ALU.add))
                    dv.wait(dve)
                    half_stats(nc, dv, st, m["z"][:, n, :], c)
                layer_norm(nc, dve, dv, st, m["z"][:, n, :], m["y_out"][:, n, :], m["rows"][:, 1, :],
                           m["rows"][:, 2, :], var_ok, std_ok, n, y_ok)

        @block.sync
        def _(sp):
            for j, (n, c) in enumerate(pairs):
                sp.wait_ge(y_ok.sem, j + 1)
                sp.dma_start(io["out"][n * P:(n + 1) * P, halves[c]], m["y_out"][:, n, halves[c]]).then_inc(out_done, 16)
            sp.wait_ge(out_done, 16 * len(pairs))


def program(nc, io):
    m = memory(nc)
    with ExitStack() as ctx:
        psum = [ctx.enter_context(nc.psum_tensor(f"bank{b}", [P, 512], F32)) for b in range(8)]
        bank = Banks(ctx, nc, psum, group_order())
        b_in = [ctx.enter_context(nc.semaphore(f"block_slot{k}")) for k in range(BLOCKS)]
        v_in = [ctx.enter_context(nc.semaphore(f"v_slot{k}")) for k in range(2)]
        front(nc, io, m, bank, b_in)
        route(nc, io, m, bank, b_in, v_in)
        experts(nc, io, m, bank, v_in)
        tail(nc, io, m, bank)


def constants():
    c = np.zeros((P, C_COLS), np.float32)
    c[:, C_ID:C_ID + P] = np.eye(P, dtype=np.float32)
    q, k = np.arange(P)[:, None], np.arange(P)[None, :]
    c[:, C_MASK + P:C_MASK + T] = np.where(k <= q, 0.0, NEG)
    c[:, C_IOTA:C_IOTA + NK] = np.arange(NK)
    for n in range(NT):
        o = C_ROPE + n * ROPE_W
        for rot, theta in ((ROT, 500000.0), (ROPE, 10000.0)):
            inv = np.power(np.float32(theta), -np.arange(0, rot, 2, dtype=np.float32) / np.float32(rot))
            ang = (np.arange(P, dtype=np.float32) + n * P)[:, None] * inv[None, :].astype(np.float32)
            cos, sin = np.cos(ang), np.sin(ang)
            c[:, o:o + 2 * rot] = np.concatenate([cos, cos, -sin, sin], axis=1)
            o += 2 * rot
    return c


def kernel(**inputs):
    import concourse.bacc as bacc
    from concourse.bass_utils import run_bass_kernel_spmd

    i = {k: np.asarray(v) for k, v in inputs.items()}
    arrays = {
        "x": i["x"][0],
        "xT": i["x"][0].T,
        "pT": i["p"][0, 0].T,
        "w_in": i["w_in"][0],
        "w_q_up": i["w_q_up"][0],
        "w_kv_up": i["w_kv_up"][0],
        "w_branch_moba": i["w_branch_moba"][0],
        "w_branch_mla": i["w_branch_mla"][0],
        "w_out": i["w_out"][0],
        "ln1_g": i["ln1_g"][0],
        "ln1_b": i["ln1_b"][0],
        "peer_wqT": i["peer_w_q"][0].reshape(KD, P, HP, DKH).transpose(2, 1, 0, 3),
        "subkT": i["peer_sub_keys"][0].reshape(HP, NK, DKH).transpose(0, 2, 1),
        "uT": i["peer_u"][0].reshape(NK, NK, KD, P).transpose(0, 3, 2, 1),
        "v": i["peer_v"][0].reshape(NK, NK, D),
        "w_ple_proj": i["w_ple_proj"][0],
        "w_ple_gate": i["w_ple_gate"][0],
        "b_ple_gate": i["b_ple_gate"][0],
        "ln2_g": i["ln2_g"][0],
        "ln2_b": i["ln2_b"][0],
        "cols": np.concatenate([i["b_gates"][0].reshape(-1, P).T, i["mla_q_norm"][0].reshape(-1, P).T,
                                i["mla_kv_norm"][0].reshape(-1, P).T], axis=1),
        "consts": constants(),
    }
    nc = bacc.Bacc("TRN2", target_bir_lowering=False, num_devices=1)
    feeds, io = {}, {}
    for name, a in arrays.items():
        a = np.ascontiguousarray(a)
        feeds[f"{name}_dram"] = a
        io[name] = nc.dram_tensor(f"{name}_dram", a.shape, mybir.dt.from_np(a.dtype), kind="ExternalInput").ap()
    io["out"] = nc.dram_tensor("out_dram", (T, D), F32, kind="ExternalOutput").ap()
    program(nc, io)
    r = run_bass_kernel_spmd(nc, [feeds], core_ids=[0])
    return r.results[0]["out_dram"].reshape(1, T, D)
```
